# Optimizing a Trainium2 kernel written in Bass

```python
import math
import jax, jax.numpy as jnp
from jax import lax
import numpy as np

D_MODEL = 1024
BATCH = 1
SEQ = 256
DEPTH = 1

MLA_HEADS = 8
MLA_Q_RANK = 384
MLA_KV_RANK = 256
MLA_NOPE = 64
MLA_ROPE = 32
MLA_V = 64
MLA_SCALE = 1.0 / math.sqrt(MLA_NOPE + MLA_ROPE)
ROPE_THETA = 10000.0
FOX_HEADS = 8
FOX_DIM = 64
FOX_SCALE = 1.0 / math.sqrt(FOX_DIM)
D_FF = 2816
CONV_WIDTH = 3
BLOCK_Q = 128
EPS = 1e-6
N_ADA = 6

IN_SPLITS = (
    MLA_Q_RANK,
    MLA_KV_RANK,
    MLA_ROPE,
    FOX_HEADS * FOX_DIM,
    FOX_HEADS * FOX_DIM,
    FOX_HEADS * FOX_DIM,
    FOX_HEADS,
    D_MODEL,
    D_MODEL,
)
D_IN = sum(IN_SPLITS)
IN_OFFSETS = tuple(int(v) for v in np.cumsum(IN_SPLITS)[:-1])


def rmsnorm(x, g):
    xf = x.astype(jnp.float32)
    y = xf * lax.rsqrt(jnp.mean(xf * xf, axis=-1, keepdims=True) + EPS)
    return (y * g.astype(jnp.float32)).astype(x.dtype)

def rope(x, positions):
    r = x.shape[-1]
    inv_freq = ROPE_THETA ** (-jnp.arange(0, r, 2, dtype=jnp.float32) / r)
    ang = positions.astype(jnp.float32)[..., None] * inv_freq
    cos = jnp.cos(ang)[:, :, None, :]
    sin = jnp.sin(ang)[:, :, None, :]
    xf = x.astype(jnp.float32)
    x1, x2 = xf[..., : r // 2], xf[..., r // 2:]
    out = jnp.concatenate([x1 * cos - x2 * sin, x2 * cos + x1 * sin], axis=-1)
    return out.astype(x.dtype)

def causal_block_attention(q, k, v, scale, log_cum=None):
    b, s, h, dk = q.shape
    nb = s // BLOCK_Q
    idx = jnp.arange(nb)
    qb = q.reshape(b, nb, BLOCK_Q, h, dk).transpose(1, 0, 2, 3, 4)
    key_pos = jnp.arange(s)
    if log_cum is not None:
        f_keys = log_cum.transpose(0, 2, 1)
        fb = log_cum.reshape(b, nb, BLOCK_Q, h).transpose(1, 0, 2, 3)
        xs = (idx, qb, fb)
    else:
        xs = (idx, qb)

    def one_block(args):
        i, qi = args[0], args[1]
        logits = jnp.einsum('bqhd,bkhd->bhqk', qi, k,
                            preferred_element_type=jnp.float32) * scale
        if log_cum is not None:
            fi = args[2].transpose(0, 2, 1)
            logits = logits + (fi[..., :, None] - f_keys[:, :, None, :])
        q_pos = i * BLOCK_Q + jnp.arange(BLOCK_Q)
        mask = key_pos[None, :] <= q_pos[:, None]
        logits = jnp.where(mask[None, None], logits, -jnp.inf)
        p = jax.nn.softmax(logits, axis=-1)
        return jnp.einsum('bhqk,bkhd->bqhd', p.astype(v.dtype), v)

    out = lax.map(one_block, xs)
    return out.transpose(1, 0, 2, 3, 4).reshape(b, s, h, v.shape[-1])

def hybrid_mixer(h, positions, w_in, q_norm_g, w_uq, kv_norm_g, w_ukv, b_forget,
                 w_o_mla, w_o_fox, w_out):
    b, s, _ = h.shape
    proj = h @ w_in
    cq, ckv, k_rope, fq, fk, fv, f_logit, g_mla, g_fox = jnp.split(proj, IN_OFFSETS, axis=-1)

    q = (rmsnorm(cq, q_norm_g) @ w_uq).reshape(b, s, MLA_HEADS, MLA_NOPE + MLA_ROPE)
    q_nope, q_rope = q[..., :MLA_NOPE], q[..., MLA_NOPE:]
    kv = (rmsnorm(ckv, kv_norm_g) @ w_ukv).reshape(b, s, MLA_HEADS, MLA_NOPE + MLA_V)
    k_nope, v_mla = kv[..., :MLA_NOPE], kv[..., MLA_NOPE:]
    q_rope = rope(q_rope, positions)
    k_rope = rope(k_rope[:, :, None, :], positions)
    q_mla = jnp.concatenate([q_nope, q_rope], axis=-1)
    k_mla = jnp.concatenate(
        [k_nope, jnp.broadcast_to(k_rope, (b, s, MLA_HEADS, MLA_ROPE))], axis=-1)
    o_mla = causal_block_attention(q_mla, k_mla, v_mla, MLA_SCALE).reshape(b, s, MLA_HEADS * MLA_V)

    log_f = jax.nn.log_sigmoid(f_logit.astype(jnp.float32) + b_forget.astype(jnp.float32))
    f_cum = jnp.cumsum(log_f, axis=1)
    o_fox = causal_block_attention(
        fq.reshape(b, s, FOX_HEADS, FOX_DIM), fk.reshape(b, s, FOX_HEADS, FOX_DIM),
        fv.reshape(b, s, FOX_HEADS, FOX_DIM), FOX_SCALE, f_cum).reshape(b, s, FOX_HEADS * FOX_DIM)

    y = jax.nn.sigmoid(g_mla) * (o_mla @ w_o_mla) + jax.nn.sigmoid(g_fox) * (o_fox @ w_o_fox)
    return y @ w_out

def conv_ffn(h, w_up, conv_w, conv_b, w_down):
    s = h.shape[1]
    u = h @ w_up
    up = jnp.pad(u, ((0, 0), (CONV_WIDTH - 1, 0), (0, 0)))
    u = conv_b + sum(conv_w[j] * up[:, j:j + s] for j in range(CONV_WIDTH))
    gate, val = u[..., :D_FF], u[..., D_FF:]
    return (jax.nn.silu(gate) * val) @ w_down

def modulate(hn, shift, scale):
    return hn * (1.0 + scale[:, None, :]) + shift[:, None, :]

def first_inputs(seed: int = 0) -> dict:
    key = jax.random.key(seed)
    ks = jax.random.split(key, 24)
    nrm = lambda k, shape, fan: jax.random.normal(k, shape, jnp.float32) * (fan ** -0.5)
    L = DEPTH
    x = jax.random.normal(ks[0], (BATCH, SEQ, D_MODEL), jnp.float32)
    c = jax.random.normal(ks[1], (BATCH, D_MODEL), jnp.float32)
    offsets = jax.random.randint(ks[2], (BATCH, 1), 0, 4096, dtype=jnp.int32)
    positions = offsets + jnp.arange(SEQ, dtype=jnp.int32)[None, :]
    return {
        "x": x,
        "c": c,
        "positions": positions,
        "w_ada": 0.5 * nrm(ks[3], (L, D_MODEL, N_ADA * D_MODEL), D_MODEL),
        "b_ada": 0.01 * jax.random.normal(ks[4], (L, N_ADA * D_MODEL), jnp.float32),
        "norm_mix_g": 1.0 + 0.1 * jax.random.normal(ks[5], (L, D_MODEL), jnp.float32),
        "w_in": nrm(ks[6], (L, D_MODEL, D_IN), D_MODEL),
        "q_norm_g": 1.0 + 0.1 * jax.random.normal(ks[7], (L, MLA_Q_RANK), jnp.float32),
        "w_uq": nrm(ks[8], (L, MLA_Q_RANK, MLA_HEADS * (MLA_NOPE + MLA_ROPE)), MLA_Q_RANK),
        "kv_norm_g": 1.0 + 0.1 * jax.random.normal(ks[9], (L, MLA_KV_RANK), jnp.float32),
        "w_ukv": nrm(ks[10], (L, MLA_KV_RANK, MLA_HEADS * (MLA_NOPE + MLA_V)), MLA_KV_RANK),
        "b_forget": jax.random.uniform(ks[11], (L, FOX_HEADS), jnp.float32, 1.0, 6.0),
        "w_o_mla": nrm(ks[12], (L, MLA_HEADS * MLA_V, D_MODEL), MLA_HEADS * MLA_V),
        "w_o_fox": nrm(ks[13], (L, FOX_HEADS * FOX_DIM, D_MODEL), FOX_HEADS * FOX_DIM),
        "w_out": nrm(ks[14], (L, D_MODEL, D_MODEL), D_MODEL),
        "norm_ffn_g": 1.0 + 0.1 * jax.random.normal(ks[15], (L, D_MODEL), jnp.float32),
        "w_up": nrm(ks[16], (L, D_MODEL, 2 * D_FF), D_MODEL),
        "conv_w": nrm(ks[17], (L, CONV_WIDTH, 2 * D_FF), CONV_WIDTH),
        "conv_b": 0.01 * jax.random.normal(ks[18], (L, 2 * D_FF), jnp.float32),
        "w_down": nrm(ks[19], (L, D_FF, D_MODEL), D_FF),
        "norm_final_g": 1.0 + 0.1 * jax.random.normal(ks[20], (D_MODEL,), jnp.float32),
    }

def first_block(x, c, positions, w_ada, b_ada, norm_mix_g, w_in, q_norm_g, w_uq, kv_norm_g,
              w_ukv, b_forget, w_o_mla, w_o_fox, w_out, norm_ffn_g, w_up, conv_w, conv_b,
              w_down, norm_final_g):
    c_act = jax.nn.silu(c)
    for l in range(DEPTH):
        ada = c_act @ w_ada[l] + b_ada[l]
        sh_m, sc_m, g_m, sh_f, sc_f, g_f = jnp.split(ada, N_ADA, axis=-1)
        h = modulate(rmsnorm(x, norm_mix_g[l]), sh_m, sc_m)
        mix = hybrid_mixer(h, positions, w_in[l], q_norm_g[l], w_uq[l], kv_norm_g[l], w_ukv[l],
                           b_forget[l], w_o_mla[l], w_o_fox[l], w_out[l])
        x = x + g_m[:, None, :] * mix
        h = modulate(rmsnorm(x, norm_ffn_g[l]), sh_f, sc_f)
        x = x + g_f[:, None, :] * conv_ffn(h, w_up[l], conv_w[l], conv_b[l], w_down[l])
    return rmsnorm(x, norm_final_g)


DEPTH_2 = 2

N_MIXERS = 2
DIFF_HEADS = 8
DIFF_HEAD_DIM = D_MODEL // DIFF_HEADS // 2
MOBA_HEADS = 16
MOBA_HEAD_DIM = D_MODEL // MOBA_HEADS
MOBA_BLOCK = 256
MOBA_TOPK = 3
D_FF_2 = 4 * D_MODEL
Q_BLOCK = 128
MOBA_Q_CHUNK = 32
RMS_EPS = 1e-6
NEG_INF = -1e30
N_DIFF_LAYERS = (DEPTH_2 + N_MIXERS - 1) // N_MIXERS


def alibi_slopes(n_heads):
    return np.array([2.0 ** (-8.0 * (h + 1) / n_heads) for h in range(n_heads)], dtype=np.float32)

def lambda_init_fn(layer_idx):
    return 0.8 - 0.6 * math.exp(-0.3 * layer_idx)

def rmsnorm_2(x, g):
    xf = x.astype(jnp.float32)
    y = xf * lax.rsqrt(jnp.mean(xf * xf, axis=-1, keepdims=True) + RMS_EPS) * g.astype(jnp.float32)
    return y.astype(x.dtype)

def squared_relu_mlp(h, w1, w2):
    return jnp.square(jax.nn.relu(h @ w1)) @ w2

def diff_attention(h, w_in, w_out, lam_params, subln_w, lam_init):
    B, T, _ = h.shape
    H, d = DIFF_HEADS, DIFF_HEAD_DIM
    q, k, v = jnp.split(h @ w_in, 3, axis=-1)
    q = q.reshape(B, T, H, 2, d).transpose(3, 0, 2, 1, 4)
    kf = k.reshape(B, T, H, 2, d).transpose(3, 0, 2, 1, 4).astype(jnp.float32)
    v = v.reshape(B, T, H, 2 * d).transpose(0, 2, 1, 3)
    lf = lam_params.astype(jnp.float32)
    lam = jnp.exp(jnp.sum(lf[0] * lf[1])) - jnp.exp(jnp.sum(lf[2] * lf[3])) + lam_init
    slopes = jnp.asarray(alibi_slopes(H))
    kpos = jnp.arange(T)
    scale = d ** -0.5

    def block(i):
        t0 = i * Q_BLOCK
        qb = lax.dynamic_slice_in_dim(q, t0, Q_BLOCK, axis=3).astype(jnp.float32)
        s = jnp.einsum('mbhqd,mbhkd->mbhqk', qb, kf) * scale
        dist = (t0 + jnp.arange(Q_BLOCK))[:, None] - kpos[None, :]
        bias = -slopes[:, None, None] * dist.astype(jnp.float32)
        s = jnp.where(dist >= 0, s + bias, NEG_INF)
        p = jax.nn.softmax(s, axis=-1)
        a = p[0] - lam * p[1]
        return jnp.einsum('bhqk,bhke->bhqe', a.astype(v.dtype), v)

    o = lax.map(block, jnp.arange(T // Q_BLOCK))
    o = o.transpose(1, 0, 3, 2, 4).reshape(B, T, H, 2 * d)
    o = rmsnorm_2(o, subln_w) * (1.0 - lam_init)
    return o.reshape(B, T, H * 2 * d) @ w_out

def moba_attention(h, w_in, w_out):
    B, T, _ = h.shape
    H, dh, BLK, QC = MOBA_HEADS, MOBA_HEAD_DIM, MOBA_BLOCK, MOBA_Q_CHUNK
    q, k, v = jnp.split(h @ w_in, 3, axis=-1)
    q = q.reshape(B, T, H, dh).transpose(0, 2, 1, 3)
    k = k.reshape(B, T, H, dh).transpose(0, 2, 1, 3)
    v = v.reshape(B, T, H, dh).transpose(0, 2, 1, 3)
    NB = -(-T // BLK)
    pad = NB * BLK - T
    kp = jnp.pad(k, ((0, 0), (0, 0), (0, pad), (0, 0)))
    vp = jnp.pad(v, ((0, 0), (0, 0), (0, pad), (0, 0)))
    kb = kp.reshape(B, H, NB, BLK, dh)
    vb = vp.reshape(B, H, NB, BLK, dh)
    kmean = jnp.mean(kb.astype(jnp.float32), axis=3)
    K_SEL = min(MOBA_TOPK, NB)
    slopes = jnp.asarray(alibi_slopes(H))
    scale = dh ** -0.5
    bi = jnp.arange(B)[:, None, None, None]
    hi = jnp.arange(H)[None, :, None, None]

    def chunk(c):
        t0 = c * QC
        j = t0 // BLK
        qc = lax.dynamic_slice_in_dim(q, t0, QC, axis=2).astype(jnp.float32)
        qpos = t0 + jnp.arange(QC)
        gate = jnp.einsum('bhqd,bhnd->bhqn', qc, kmean)
        gate = jnp.where(jnp.arange(NB) < j, gate, NEG_INF)
        _, idx = lax.top_k(gate, K_SEL)
        valid = jnp.arange(K_SEL) < j
        s0 = j * BLK
        k_own = lax.dynamic_slice_in_dim(kp, s0, BLK, axis=2).astype(jnp.float32)
        v_own = lax.dynamic_slice_in_dim(vp, s0, BLK, axis=2)
        d_own = (qpos[:, None] - (s0 + jnp.arange(BLK))[None, :]).astype(jnp.float32)
        sc_own = jnp.einsum('bhqd,bhkd->bhqk', qc, k_own) * scale - slopes[:, None, None] * d_own
        sc_own = jnp.where(d_own >= 0, sc_own, NEG_INF)
        k_sel = kb[bi, hi, idx]
        v_sel = vb[bi, hi, idx]
        sel_pos = idx[..., None] * BLK + jnp.arange(BLK)
        d_sel = (qpos[None, None, :, None, None] - sel_pos).astype(jnp.float32)
        sc_sel = (jnp.einsum('bhqd,bhqkld->bhqkl', qc, k_sel.astype(jnp.float32)) * scale
                  - slopes[None, :, None, None, None] * d_sel)
        sc_sel = jnp.where(valid[:, None], sc_sel, NEG_INF)
        sc = jnp.concatenate([sc_own, sc_sel.reshape(B, H, QC, K_SEL * BLK)], axis=-1)
        p = jax.nn.softmax(sc, axis=-1)
        p_own = p[..., :BLK].astype(v.dtype)
        p_sel = p[..., BLK:].reshape(B, H, QC, K_SEL, BLK).astype(v.dtype)
        return (jnp.einsum('bhqk,bhkd->bhqd', p_own, v_own)
                + jnp.einsum('bhqkl,bhqkld->bhqd', p_sel, v_sel))

    o = lax.map(chunk, jnp.arange(T // QC))
    o = o.transpose(1, 0, 3, 2, 4).reshape(B, T, H * dh)
    return o @ w_out

def second_inputs(seed: int = 0) -> dict:
    key = jax.random.key(seed)
    ks = jax.random.split(key, 10)
    f32 = jnp.float32
    x = jax.random.normal(ks[0], (BATCH, SEQ, D_MODEL), f32)
    attn_norm = 1.0 + 0.02 * jax.random.normal(ks[1], (DEPTH_2, D_MODEL), f32)
    w_in = jax.random.normal(ks[2], (DEPTH_2, D_MODEL, 3 * D_MODEL), f32) * D_MODEL ** -0.5
    w_out = jax.random.normal(ks[3], (DEPTH_2, D_MODEL, D_MODEL), f32) * D_MODEL ** -0.5
    diff_lambda = 0.1 * jax.random.normal(ks[4], (N_DIFF_LAYERS, 4, DIFF_HEAD_DIM), f32)
    diff_subln = 1.0 + 0.02 * jax.random.normal(ks[5], (N_DIFF_LAYERS, 2 * DIFF_HEAD_DIM), f32)
    mlp_norm = 1.0 + 0.02 * jax.random.normal(ks[6], (DEPTH_2, D_MODEL), f32)
    w_ff1 = jax.random.normal(ks[7], (DEPTH_2, D_MODEL, D_FF_2), f32) * D_MODEL ** -0.5
    w_ff2 = jax.random.normal(ks[8], (DEPTH_2, D_FF_2, D_MODEL), f32) * D_FF_2 ** -0.5
    final_norm = 1.0 + 0.02 * jax.random.normal(ks[9], (D_MODEL,), f32)
    return {"x": x, "attn_norm": attn_norm, "w_in": w_in, "w_out": w_out,
            "diff_lambda": diff_lambda, "diff_subln": diff_subln, "mlp_norm": mlp_norm,
            "w_ff1": w_ff1, "w_ff2": w_ff2, "final_norm": final_norm}

def second_block(x, attn_norm, w_in, w_out, diff_lambda, diff_subln, mlp_norm, w_ff1, w_ff2, final_norm):
    h = x
    for i in range(DEPTH_2):
        hn = rmsnorm_2(h, attn_norm[i])
        if i % N_MIXERS == 0:
            li = i // N_MIXERS
            m = diff_attention(hn, w_in[i], w_out[i], diff_lambda[li], diff_subln[li], lambda_init_fn(i))
        else:
            m = moba_attention(hn, w_in[i], w_out[i])
        h = h + m
        h = h + squared_relu_mlp(rmsnorm_2(h, mlp_norm[i]), w_ff1[i], w_ff2[i])
    return rmsnorm_2(h, final_norm)


def setup_inputs(seed=0):
    out = dict(first_inputs(seed))
    for name, value in second_inputs(seed + 1).items():
        if name != "x":
            out[name + "_2"] = value
    return out


def reference(
    x, c, positions, w_ada, b_ada, norm_mix_g, w_in, q_norm_g, w_uq, kv_norm_g, w_ukv, b_forget,
    w_o_mla, w_o_fox, w_out, norm_ffn_g, w_up, conv_w, conv_b, w_down, norm_final_g,
    attn_norm_2, w_in_2, w_out_2, diff_lambda_2, diff_subln_2, mlp_norm_2, w_ff1_2, w_ff2_2,
    final_norm_2,
):
    x = first_block(
        x, c, positions, w_ada, b_ada, norm_mix_g, w_in, q_norm_g, w_uq, kv_norm_g, w_ukv,
        b_forget, w_o_mla, w_o_fox, w_out, norm_ffn_g, w_up, conv_w, conv_b, w_down,
        norm_final_g,
    )
    return second_block(
        x, attn_norm_2, w_in_2, w_out_2, diff_lambda_2, diff_subln_2, mlp_norm_2, w_ff1_2,
        w_ff2_2, final_norm_2,
    )


_drawn_inputs = setup_inputs


def setup_inputs(seed=0):
    import zlib

    import numpy as np

    out = dict(_drawn_inputs(seed))
    spreads = {}
    factors = {'b_ada': 3.546,
     'norm_mix_g': 2.904,
     'q_norm_g': 8.0,
     'kv_norm_g': 3.516,
     'conv_b': 8.0,
     'diff_subln_2': 3.583,
     'mlp_norm_2': 2.708,
     'final_norm_2': 2.737}
    for name, (base, spread) in spreads.items():
        noise = np.random.default_rng([zlib.crc32(name.encode()), seed]).standard_normal(out[name].shape)
        drawn = base * np.exp(spread * noise) if base else spread * noise
        out[name] = __import__('jax').numpy.asarray(drawn.astype(out[name].dtype))
    for name, factor in factors.items():
        out[name] = (out[name] * factor).astype(out[name].dtype)
    return out
```

```python
import math
from contextlib import ExitStack

import numpy as np

import concourse.bass as bass
from concourse import mybir
from concourse.alu_op_type import AluOpType as ALU

F32 = mybir.dt.float32
F32R = mybir.dt.float32r
I32 = mybir.dt.int32
ACT = mybir.ActivationFunctionType

T = 256
D = 1024
CH = 2048
EPS = 1e-6
NEG = -1e30
BIG = 3e38
MLA_SCALE = 1.0 / math.sqrt(96.0)
SCALE64 = 0.125
LAM_INIT = 0.8 - 0.6 * math.exp(0.0)
TWO_PI = 2.0 * math.pi
MAGIC = 12582912.0
C1 = 6.28125
C2 = float(np.float32(np.round((TWO_PI - C1) * 2.0**18) / 2.0**18))
C3 = float(np.float32(TWO_PI - C1 - C2))

RAW = 4
HL = 3

COLS = {}


def _columns():
    at = 0
    for name, n in [
        ("c", 8), ("b_ada", 48), ("norm_mix_g", 8), ("norm_ffn_g", 8), ("norm_final_g", 8),
        ("q_norm_g", 3), ("kv_norm_g", 2), ("conv_w", 132), ("conv_b", 44), ("attn_norm", 16),
        ("mlp_norm", 16), ("final_norm", 8), ("subln", 1), ("b_forget", 1), ("invf", 1), ("sgn", 1),
        ("eps", 1), ("m1", 8), ("m2", 8), ("m3", 1), ("m4", 1),
    ]:
        COLS[name] = at
        at += n
    return at


NCOL = _columns()


def weight_order():
    order = [("in", i) for i in range(10)] + [("uq", 0), ("uq", 1), ("ukv", 0)]
    order += [("in", i) for i in range(10, 18)]
    order += [("o", i) for i in range(4)] + [("out", i) for i in range(4)]
    for i in range(11):
        order += [("up", 2 * i), ("up", 2 * i + 1)]
        if i >= 1:
            order.append(("down", i - 1))
    order.append(("down", 10))
    for layer in range(2):
        for j in range(4):
            order += [(f"qkv{layer}", j), (f"qkv{layer}", 4 + j), (f"qkv{layer}", 8 + j)]
        order += [(f"out{layer}", i) for i in range(4)]
        for i in range(16):
            order.append((f"ff1{layer}", i))
            if i >= 2:
                order.append((f"ff2{layer}", i - 2))
        order += [(f"ff2{layer}", 14), (f"ff2{layer}", 15)]
    return order


USED = {"uq": 1536}


def stream_order():
    ada = [("ada", cb, kk) for cb in range(6) for kk in range(4)]
    items = ada[:8]
    late = ada[8:]
    for n, w in enumerate(weight_order()):
        items.append(("w", n) + w)
        if n < 18 and late:
            items.append(late.pop(0))
        if n >= 18:
            items += late
            late = []
    return items


class Program:

    def __init__(self, nc, ctx):
        self.nc, self.ctx = nc, ctx
        self.queues = {e: [] for e in ("sync", "scalar", "vector", "gpsimd", "tensor")}
        self.sems, self.counts, self.seen = {}, {}, {}

    def op(self, engine, waits, issue, signal=None, by=1):
        q = self.queues[engine]
        for name, value in waits:
            if self.seen.get((engine, name), 0) < value:
                self.seen[(engine, name)] = value
                q.append((None, self.sems[name], value))
        if signal is None:
            q.append((issue, None, 0))
            return None
        if signal not in self.sems:
            self.sems[signal] = self.ctx.enter_context(self.nc.semaphore(signal))
        self.counts[signal] = self.counts.get(signal, 0) + by
        q.append((issue, self.sems[signal], by))
        return signal, self.counts[signal]

    def run(self, engine, eng):
        for issue, sem, n in self.queues[engine]:
            if issue is None:
                eng.wait_ge(sem, n)
            else:
                ins = issue(eng)
                if sem is not None:
                    ins.then_inc(sem, n)


def build(nc, wall, wada, smalls, pos, xt, masks, lam4, alibi8, alibi16, out):
    ctx = ExitStack()
    with ctx:
        _build(nc, ctx, wall, wada, smalls, pos, xt, masks, lam4, alibi8, alibi16, out)


def _build(nc, ctx, wall, wada, smalls, pos, xt, masks, lam4, alibi8, alibi16, out):
    def sb(name, shape, dt=F32):
        return ctx.enter_context(nc.sbuf_tensor(name, shape, dt))

    P = Program(nc, ctx)
    op = P.op

    raw = [sb(f"raw{i}", [128, CH]) for i in range(RAW)]
    whi = [sb(f"whi{i}", [128, CH], F32R) for i in range(HL)]
    wlo = [sb(f"wlo{i}", [128, CH], F32R) for i in range(HL)]
    X = sb("X", [128, 8, T])
    Hh = sb("Hh", [128, 8, T], F32R)
    Hl = sb("Hl", [128, 8, T], F32R)
    Oh = sb("Oh", [128, 8, T], F32R)
    Ol = sb("Ol", [128, 8, T], F32R)
    QM = sb("QM", [128, 8, T])
    KM = sb("KM", [128, 8, T])
    QF = sb("QF", [128, 8, T])
    KF = sb("KF", [128, 8, T])
    V = sb("V", [128, 2, 1024])
    GA = sb("GA", [128, 16, T])
    ACC = sb("ACC", [128, 1024])
    SQ = sb("SQ", [128, 4, T])
    COS = sb("COS", [128, T])
    SIN = sb("SIN", [128, T])
    PB = sb("PB", [128, 4, 384])
    PT = sb("PT", [128, 4, 384])
    TT = sb("TT", [128, 2, T])
    DG = sb("DG", [128, 2, 128])
    ID = sb("ID", [128, 128])
    TRI = sb("TRI", [128, T])
    ONES = sb("ONES", [128, 128])
    SM = sb("SM", [128, NCOL])
    ADA = sb("ADA", [128, 48])
    GS = sb("GS", [128, 16])
    CA = sb("CA", [128, 8])
    ST = sb("ST", [128, 8])
    RS = sb("RS", [128, 8])
    NM = sb("NM", [128, 8])
    LM = sb("LM", [128, 6])
    SW = sb("SW", [128, 1])
    PS = ctx.enter_context(nc.psum_tensor("PS", [128, 8, 512], F32))

    def col(name, i=0, n=1, p0=0, p1=128):
        return SM[p0:p1, COLS[name] + i:COLS[name] + i + n]

    PBf = PB[:, :, :].rearrange("p a b -> p (a b)")
    PTf = PT[:, :, :].rearrange("p a b -> p (a b)")
    f32 = lambda ap: ap.bitcast(F32)

    small = op("sync", [], lambda e: e.dma_start(SM[:, :], smalls), "d_small", 16)
    xin = op("sync", [], lambda e: e.dma_start(X[:, :, :], xt), "d_x", 16)
    items = stream_order()
    chunk_no = {it[2:]: it[1] for it in items if it[0] == "w"}
    raw_free = {}
    landed = {}

    def load(i):
        it = items[i]
        slot = i % RAW
        if it[0] == "ada":
            _, cb, kk = it
            dst, src = raw[slot][:, :], wada[cb * 4 + kk]
        else:
            n = USED.get(it[2], CH)
            dst, src = raw[slot][:, 0:n], wall[it[1]][:, 0:n]
        landed[i] = op("sync", raw_free.get(i - RAW, []), lambda e: e.dma_start(dst, src), f"d_raw{slot}", 16)

    for i in range(RAW):
        load(i)
    posi = TT[:, 0, :].bitcast(I32)
    pin = op("scalar", [], lambda e: e.dma_start(posi, pos), "d_pos", 16)
    mk = op("scalar", [], lambda e: e.dma_start(ID[:, :], masks[:, 0:128]), "d_id", 16)
    mt = op("scalar", [], lambda e: e.dma_start(TRI[:, :], masks[:, 128:384]), "d_tri", 16)
    ones = op("gpsimd", [], lambda e: e.memset(ONES[:, :], 1.0), "g_ones")

    st = {"next": 0, "ada": None}
    hi_tok, lo_tok, mm_tok = {}, {}, {}

    ada_acc = {}
    ada_free = []

    def take_ada(i, cb, kk):
        src = raw[i % RAW]
        for half in range(2):
            k = 2 * kk + half
            w = src[:, half * 1024:(half + 1) * 1024]
            if k == 0:
                tok = op("vector", [landed[i], cact] + ada_free, lambda e, w=w: e.tensor_scalar(
                    ACC[:, :], w, CA[:, 0:1], None, ALU.mult), "v_ada")
            else:
                tok = op("vector", [landed[i], st["ada"]], lambda e, w=w, k=k: e.scalar_tensor_tensor(
                    ACC[:, :], w, CA[:, k:k + 1], ACC[:, :], ALU.mult, ALU.add), "v_ada")
            st["ada"] = tok
        raw_free[i] = [st["ada"]]
        if kk == 3:
            b = gbank()
            for j in range(8):
                t = op("tensor", [st["ada"], ones] + bank_free[b], lambda e, j=j, b=b: e.matmul(
                    PS[:, b, j:j + 1], ACC[:, j * 128:(j + 1) * 128], ONES[:, 0:1],
                    start=True, stop=True), "t_ada" if j == 7 else None)
            ada_free[:] = [t]
            tok = op("vector", [t, small], lambda e, b=b, cb=cb: e.tensor_tensor(
                ADA[:, cb * 8:(cb + 1) * 8], PS[:, b, 0:8], col("b_ada", cb * 8, 8), ALU.add), "v_adab")
            bank_free[b] = [tok]
            ada_acc[cb] = tok

    def take_weight(i, n, kind):
        slot = n % HL
        w = USED.get(kind, CH)
        src = raw[i % RAW]
        free = [mm_tok[n - HL]] if n >= HL else []
        hi_tok[n] = op("scalar", [landed[i]] + free, lambda e: e.activation(
            whi[slot][:, 0:w], src[:, 0:w], ACT.Copy), "a_whi")
        lo_tok[n] = op("vector", [hi_tok[n]] + free, lambda e: e.tensor_tensor(
            wlo[slot][:, 0:w], src[:, 0:w], f32(whi[slot][:, 0:w]), ALU.subtract), "v_wlo")
        raw_free[i] = [lo_tok[n]]

    def take_next():
        i = st["next"]
        it = items[i]
        if it[0] == "ada":
            take_ada(i, it[1], it[2])
        else:
            take_weight(i, it[1], it[2])
        st["next"] = i + 1
        if i + RAW < len(items):
            load(i + RAW)

    def ensure(n):
        while st["next"] < len(items) and max(hi_tok, default=-1) < n:
            take_next()

    bank_free = {b: [] for b in range(8)}
    rot = {"banks": [0, 1, 2, 3], "at": 0}

    def gbank():
        b = rot["banks"][rot["at"] % len(rot["banks"])]
        rot["at"] += 1
        return b

    LOOK = 2

    def mm_begin(key):
        n = chunk_no[key]
        ensure(n + LOOK)
        return n

    def mm_T(n, kts, ncols, nt, dst, waits, xh, xl, xk, first=True, last=True, share=False, signal=None):
        slot = n % HL
        w0 = list(waits) + [hi_tok[n], lo_tok[n]]
        tok = None
        for k in range(kts):
            wh = whi[slot][:, k * ncols + nt * 128:k * ncols + nt * 128 + 128]
            wl = wlo[slot][:, k * ncols + nt * 128:k * ncols + nt * 128 + 128]
            a, b = xh[:, xk(k), :], xl[:, xk(k), :]
            ww = (w0 if k == 0 else []) + xwait(xk(k))

            def go(e, wh=wh, wl=wl, a=a, b=b, k=k):
                e.matmul(dst, wh, a, start=first and k == 0, stop=False, skip_group_check=share)
                e.matmul(dst, wh, b, start=False, stop=False, skip_group_check=share)
                return e.matmul(dst, wl, a, start=False, stop=last and k == kts - 1, skip_group_check=share)

            tok = op("tensor", ww, go, signal if k == kts - 1 else None)
        return tok

    def mm_N(n, kts, ncols, c0, nc_, dst, half, waits, xh, xl, xk, signal=None):
        slot = n % HL
        tok = None
        for k in range(kts):
            wh = whi[slot][:, k * ncols + c0:k * ncols + c0 + nc_]
            wl = wlo[slot][:, k * ncols + c0:k * ncols + c0 + nc_]
            a, b = (x[:, xk(k), half * 128:half * 128 + 128] for x in (xh, xl))
            ww = (list(waits) + [hi_tok[n], lo_tok[n]] if k == 0 else []) + xwait(xk(k))

            def go(e, wh=wh, wl=wl, a=a, b=b, k=k):
                e.matmul(dst, a, wh, start=k == 0, stop=False)
                e.matmul(dst, b, wh, start=False, stop=False)
                return e.matmul(dst, a, wl, start=False, stop=k == kts - 1)

            tok = op("tensor", ww, go, signal if k == kts - 1 else None)
        return tok

    xready = {}

    def xwait(k):
        return xready.get(k, [])

    pend = []

    def pump(n=1):
        for _ in range(n):
            if pend:
                pend.pop(0)()

    def chunk_T(key, x, evac, kts=8, ncols=256, pairs=1, mid=0):
        xh, xl = x
        n = mm_begin(key)
        for pr in range(pairs):
            b = gbank()
            fr = list(bank_free[b])
            mm_T(n, kts, ncols, 2 * pr, PS[:, b, 0:T], fr, xh, xl, lambda k: k)
            pump(mid)
            tok = mm_T(n, kts, ncols, 2 * pr + 1, PS[:, b, T:2 * T], [], xh, xl, lambda k: k, signal="t_mm")
            if pr == pairs - 1:
                mm_tok[n] = tok
            evac(pr, b, tok)

    def stats(src, nk, dim, wait, b=None, sq_from_psum=None):
        if b is None:
            b = gbank()
        fr = list(bank_free[b])
        t = None
        for k in range(nk):
            s = k % 4
            sq = op("scalar", list(wait(k)) + sq_free.get(s, []), lambda e, k=k, s=s: e.activation(
                SQ[:, s, :], src(k), ACT.Square), "a_sq")
            for half in range(2):
                t = op("tensor", [sq, ones] + (fr if k == 0 else []), lambda e, k=k, s=s, half=half: e.matmul(
                    PS[:, b, half:half + 1], SQ[:, s, half * 128:half * 128 + 128], ONES[:, 0:1],
                    start=k == 0 and half == 0, stop=k == nk - 1, skip_group_check=True),
                    "t_sq" if half == 1 else None)
            sq_free[s] = [t]
        return rstd(b, t, 2, dim)

    sq_free = {}
    dg_free = []

    def rstd(b, t, n, dim):
        t = op("scalar", [t, small], lambda e: e.activation(
            ST[:, 0:n], PS[:, b, 0:n], ACT.Sqrt, bias=col("eps"), scale=1.0 / dim), "a_sqrt")
        t = op("vector", [t], lambda e: e.reciprocal(ST[:, 4:4 + n], ST[:, 0:n]), "v_rec")
        for h in range(n):
            d = op("vector", [t, mk] + dg_free, lambda e, h=h: e.tensor_scalar(
                DG[:, h % 2, :], ID[:, :], ST[:, 4 + h:5 + h], None, ALU.mult), "v_dg")
            m = op("tensor", [d], lambda e, h=h: e.matmul(
                PS[:, b, (256 if n == 2 else 0) + h * 128:(256 if n == 2 else 0) + h * 128 + 128],
                ONES[:, :], DG[:, h % 2, :], start=True, stop=True), "t_dg")
            if h % 2 == 1:
                dg_free[:] = [m]
        return b, m

    tt_free = {}

    def apply(src, nk, gain, shift, rb, rtok, dst, k0=0, waits=()):
        dh, dl = dst
        done = None
        steps = []
        for k in range(nk):
            s = k % 2
            t = op("vector", [rtok] + list(waits) + tt_free.get(s, []), lambda e, k=k, s=s, g=gain(k): e.scalar_tensor_tensor(
                TT[:, s, :], src(k), g, PS[:, rb, 256:512], ALU.mult, ALU.mult), "v_nrm")
            if shift is None:
                h = op("scalar", [t] + x_free, lambda e, k=k, s=s: e.activation(
                    dh[:, k0 + k, :], TT[:, s, :], ACT.Copy), "a_xhi")
            else:
                h = op("scalar", [t] + x_free, lambda e, k=k, s=s: e.activation(
                    dh[:, k0 + k, :], TT[:, s, :], ACT.Identity, bias=shift(k)), "a_xhi")
            steps.append((k, s, h))
            if len(steps) > 1:
                done = low(dh, dl, k0, shift, steps.pop(0))
        done = low(dh, dl, k0, shift, steps.pop(0))
        bank_free[rb] = [done]
        return done

    def low(dh, dl, k0, shift, step):
        k, s, h = step
        if shift is None:
            t = op("vector", [h] + x_free, lambda e: e.tensor_tensor(
                dl[:, k0 + k, :], TT[:, s, :], f32(dh[:, k0 + k, :]), ALU.subtract), "v_xlo")
        else:
            t = op("vector", [h] + x_free, lambda e: e.scalar_tensor_tensor(
                dl[:, k0 + k, :], TT[:, s, :], shift(k), f32(dh[:, k0 + k, :]), ALU.add, ALU.subtract), "v_xlo")
        tt_free[s] = [t]
        xready[k0 + k] = [h, t]
        return t

    x_free = []

    def split(dh, dl, src, waits, free=()):
        h = op("scalar", list(waits) + list(free), lambda e: e.activation(dh, src, ACT.Copy), "a_xhi")
        return h, op("vector", [h], lambda e: e.tensor_tensor(dl, src, f32(dh), ALU.subtract), "v_xlo")

    cact = op("scalar", [small], lambda e: e.activation(CA[:, :], col("c", 0, 8), ACT.Silu), "a_c")
    while st["next"] < 4:
        take_next()
    ANG, KR, RR = PTf[:, 0:256], PTf[:, 256:512], PTf[:, 512:768]
    t = op("vector", [pin], lambda e: e.tensor_copy(ANG, posi), "v_rope")
    t = op("vector", [t, small], lambda e: e.tensor_scalar(ANG, ANG, col("invf"), None, ALU.mult), "v_rope")
    tt_free[0] = [t]
    for dst, shift in ((SIN, 0.0), (COS, 0.25)):
        if shift:
            t = op("vector", [t], lambda e: e.tensor_scalar(KR, ANG, 1.0 / TWO_PI, 0.25, ALU.mult, ALU.add), "v_rope")
            t = op("vector", [t], lambda e: e.tensor_scalar(KR, KR, MAGIC, None, ALU.add), "v_rope")
        else:
            t = op("vector", [t], lambda e: e.tensor_scalar(KR, ANG, 1.0 / TWO_PI, MAGIC, ALU.mult, ALU.add), "v_rope")
        t = op("vector", [t], lambda e: e.tensor_scalar(KR, KR, MAGIC, None, ALU.subtract), "v_rope")
        t = op("vector", [t], lambda e: e.scalar_tensor_tensor(RR, KR, -C1, ANG, ALU.mult, ALU.add), "v_rope")
        t = op("vector", [t], lambda e: e.scalar_tensor_tensor(RR, KR, -C2, RR, ALU.mult, ALU.add), "v_rope")
        t = op("vector", [t], lambda e: e.scalar_tensor_tensor(RR, KR, -C3, RR, ALU.mult, ALU.add), "v_rope")
        if shift:
            t = op("vector", [t], lambda e: e.tensor_scalar(RR, RR, math.pi / 2, None, ALU.add), "v_rope")
        t = op("vector", [t], lambda e: e.tensor_scalar(RR, RR, 3.1415925, -3.1415925, ALU.min, ALU.max), "v_rope")
        t = op("scalar", [t], lambda e, dst=dst: e.activation(dst[:, :], RR, ACT.Sin), "a_sin")
    trig = op("vector", [t], lambda e: e.tensor_scalar(SIN[:, :], SIN[:, :], col("sgn"), None, ALU.mult), "v_rope")

    b0, r0 = stats(lambda k: X[:, k, :], 8, D, lambda k: [xin])
    while st["next"] < 8:
        take_next()
    gs_mix = op("vector", [ada_acc[1], small], lambda e: e.scalar_tensor_tensor(
        GS[:, 0:8], ADA[:, 8:16], 1.0, col("norm_mix_g", 0, 8), ALU.add, ALU.mult), "v_gs")
    H = (Hh, Hl)
    apply(lambda k: X[:, k, :], 8, lambda k: GS[:, k:k + 1], lambda k: ADA[:, k:k + 1], b0, r0, H,
          waits=[gs_mix, ada_acc[0]])

    rot["banks"] = [0, 1, 2]
    C5 = lambda k: PBf[:, k * T:(k + 1) * T]
    cq_tok = {}

    def ev_c0(pr, b, tok):
        t = op("scalar", [tok], lambda e: e.activation(PBf[:, 0:512], PS[:, b, 0:512], ACT.Copy), "a_ev")
        cq_tok[0] = cq_tok[1] = t
        bank_free[b] = [t]

    def ev_c1(pr, b, tok):
        t = op("scalar", [tok], lambda e: e.activation(PBf[:, 512:768], PS[:, b, 0:256], ACT.Copy), "a_ev")
        cq_tok[2] = t
        z, az, ls = PTf[64:80, 0:256], PTf[64:80, 256:512], PTf[64:80, 512:768]
        fc, rf, on = PTf[64:80, 768:1024], PTf[64:80, 1024:1280], PTf[64:80, 1280:1536]
        cc = lambda name, i=0, n=1: col(name, i, n, 64, 80)
        t = op("vector", [t, trig], lambda e: e.tensor_scalar(z, PS[64:80, b, 256:512], cc("b_forget"), None, ALU.add), "v_f")
        bank_free[b] = [t]
        o1 = op("vector", [], lambda e: e.memset(on, 1.0), "v_f")
        t = op("vector", [t], lambda e: e.scalar_tensor_tensor(az, z, -1.0, z, ALU.mult, ALU.max), "v_f")
        t = op("scalar", [t], lambda e: e.activation(az, az, ACT.Exp, scale=-1.0), "a_f")
        t = op("scalar", [t], lambda e: e.activation(az, az, ACT.Ln, bias=1.0), "a_f")
        t = op("vector", [t], lambda e: e.scalar_tensor_tensor(ls, z, 0.0, az, ALU.min, ALU.subtract), "v_f")
        t = op("vector", [t, o1], lambda e: e.tensor_tensor_scan(fc, on, ls, 0.0, ALU.mult, ALU.add), "v_f")
        for h in range(8):
            q = op("vector", [t], lambda e, h=h: e.tensor_scalar(
                QF[64:80, h, :], fc, cc("m1", h), cc("m2", h), ALU.mult, ALU.add), "v_fq")
        t = op("vector", [t], lambda e: e.tensor_scalar(rf, fc, cc("m3"), cc("m4"), ALU.mult, ALU.add), "v_f")
        k_ = op("scalar", [t], lambda e: e.activation(
            KF[64:80, :, :], rf.unsqueeze(1).to_broadcast([16, 8, T]), ACT.Copy), "a_f")
        aug[:] = [q, k_]

    aug = []

    def ev_c2(pr, b, tok):
        t = op("scalar", [tok], lambda e: e.activation(PBf[:, 768:1280], PS[:, b, 0:512], ACT.Copy), "a_ev")
        cq_tok[3] = cq_tok[4] = t
        bank_free[b] = [t]

    km_tok = []

    def ev_kr(pr, b, tok):
        a, c = TT[64:96, 0, :], TT[64:96, 1, :]
        t1 = op("vector", [tok, trig] + tt_free.get(0, []) + tt_free.get(1, []), lambda e: e.tensor_tensor(
            a, PS[64:96, b, 0:256], COS[64:96, :], ALU.mult), "v_kr")
        t2 = op("vector", [], lambda e: e.tensor_tensor(c, PS[64:96, b, 256:512], SIN[64:96, :], ALU.mult), "v_kr")
        bank_free[b] = [t2]
        t = op("vector", [t2], lambda e: e.tensor_tensor(a, a, c, ALU.add), "v_kr")
        t = op("scalar", [t], lambda e: e.activation(
            KM[64:96, :, :], a.unsqueeze(1).to_broadcast([32, 8, T]), ACT.Copy), "a_kr")
        tt_free[0] = tt_free[1] = [t]
        km_tok.append(t)

    def heads_out(dst, h0, toks):
        def ev(b, tok):
            bank = PS[:, b, :].rearrange("p (j t) -> p j t", j=2)
            op("scalar", [tok], lambda e: e.activation(dst[0:64, h0:h0 + 4:2, :], bank[0:64], ACT.Copy), None)
            t = op("scalar", [], lambda e: e.activation(dst[0:64, h0 + 1:h0 + 4:2, :], bank[64:128], ACT.Copy), "a_ev")
            toks.append(t)
            bank_free[b] = [t]
        return ev

    kf_tok, qf_tok, vf_tok, qm_tok, vm_tok = [], [], [], [], []
    VF, VM = V[:, :, 512:1024], V[:, :, 0:512]

    def chunk_N(key, x, dst, toks, mid=0):
        n = mm_begin(key)
        b = gbank()
        mm_N(n, 8, 256, 0, 256, PS[:, b, 0:256], 0, list(bank_free[b]), x[0], x[1], lambda k: k)
        pump(mid)
        tok = mm_N(n, 8, 256, 0, 256, PS[:, b, 256:512], 1, [], x[0], x[1], lambda k: k, signal="t_mm")
        mm_tok[n] = tok
        t = op("scalar", [tok], lambda e: e.activation(
            dst, PS[:, b, :].rearrange("p (h n) -> p h n", h=2), ACT.Copy), "a_ev")
        bank_free[b] = [t]
        toks.append(t)

    chunk_T(("in", 0), H, ev_c0)
    chunk_T(("in", 1), H, ev_c1)
    bq, rq = stats(C5, 3, 384, lambda k: [cq_tok[k]])
    chunk_T(("in", 2), H, ev_c2)
    xr = dict(xready)
    xready.clear()
    apply(C5, 3, lambda k: col("q_norm_g", k), None, bq, rq, (Oh, Ol), 0)
    cn = dict(xready)
    xready.clear()
    xready.update(xr)
    bk, rk = stats(lambda k: C5(3 + k), 2, 256, lambda k: [cq_tok[3 + k]])
    chunk_T(("in", 3), H, ev_kr)
    xready.clear()
    apply(lambda k: C5(3 + k), 2, lambda k: col("kv_norm_g", k), None, bk, rk, (Oh, Ol), 3)
    cn.update(xready)
    xready.clear()
    xready.update(xr)
    for j in range(2):
        chunk_T(("in", 4 + j), H, lambda pr, b, tok, j=j: heads_out(KF, 4 * j, kf_tok)(b, tok))
    for j in range(2):
        chunk_T(("in", 6 + j), H, lambda pr, b, tok, j=j: heads_out(QF, 4 * j, qf_tok)(b, tok))
    for j in range(2):
        chunk_N(("in", 8 + j), H, VF[:, :, 256 * j:256 * j + 256], vf_tok)

    def ev_uq(j):
        def ev(pr, b, tok):
            h0 = 4 * j + 2 * pr
            bank = PS[:, b, :].rearrange("p (j t) -> p j t", j=2)
            c = op("scalar", [tok], lambda e: e.activation(QM[0:64, h0:h0 + 2, :], bank[0:64], ACT.Copy), "a_ev")
            s1 = TT[64:96, :, :]
            s2 = SQ[64:96, 0:2, :]
            bc = lambda ap: ap.unsqueeze(1).to_broadcast([32, 2, T])
            op("vector", [c, trig] + tt_free.get(0, []) + tt_free.get(1, []) + sq_free.get(0, []) + sq_free.get(1, []),
               lambda e: e.tensor_tensor(s1, bank[64:96], bc(COS[64:96, :]), ALU.mult), None)
            t = op("vector", [], lambda e: e.tensor_tensor(s2, bank[96:128], bc(SIN[96:128, :]), ALU.mult), "v_qr")
            bank_free[b] = [t]
            t = op("vector", [t], lambda e: e.tensor_tensor(QM[64:96, h0:h0 + 2, :], s1, s2, ALU.add), "v_qr")
            tt_free[0] = tt_free[1] = sq_free[0] = sq_free[1] = [t]
            qm_tok.append([c, t])
        return ev

    pb_free, pt_free, s_free, t_free = {}, {}, {}, {}
    nm_free = {}
    a_tok, b_tok = {}, {}

    def scores(slot, q, k, waits, bias, scale, normalise=True, waitb=()):
        b = 4 + slot % 2
        op("tensor", list(waits) + s_free.get(b, []), lambda e: e.matmul(
            PS[:, b, 0:128], q[:, 0:128], k[:, 0:128], start=True, stop=True), None)
        t = op("tensor", [], lambda e: e.matmul(
            PS[:, b, 128:384], q[:, 128:256], k[:, 0:256], start=True, stop=True), "t_s")
        w = [t, mt] + list(waitb) + pb_free.get(slot, [])
        op("vector", w, lambda e: e.tensor_tensor_reduce(
            PB[:, slot, 0:128], PS[:, b, 0:128], bias[:, 128:256], -scale, BIG, ALU.add, ALU.min,
            NM[:, 2 * slot:2 * slot + 1]), None)
        t = op("vector", [], lambda e: e.tensor_tensor_reduce(
            PB[:, slot, 128:384], PS[:, b, 128:384], bias, -scale, BIG, ALU.add, ALU.min,
            NM[:, 2 * slot + 1:2 * slot + 2]), "v_s")
        s_free[b] = [t]
        op("scalar", [t], lambda e: e.activation(
            PB[:, slot, 0:128], PB[:, slot, 0:128], ACT.Exp, scale=-1.0, bias=NM[:, 2 * slot:2 * slot + 1],
            accum_out=RS[:, 2 * slot:2 * slot + 1]), None)
        t = op("scalar", [], lambda e: e.activation(
            PB[:, slot, 128:384], PB[:, slot, 128:384], ACT.Exp, scale=-1.0, bias=NM[:, 2 * slot + 1:2 * slot + 2],
            accum_out=RS[:, 2 * slot + 1:2 * slot + 2]), "a_exp")
        t = op("vector", [t], lambda e: e.reciprocal(RS[:, 2 * slot:2 * slot + 2], RS[:, 2 * slot:2 * slot + 2]), "v_rs")
        if normalise:
            op("gpsimd", [t], lambda e: e.tensor_scalar(
                PB[:, slot, 0:128], PB[:, slot, 0:128], RS[:, 2 * slot:2 * slot + 1], None, ALU.mult), None)
            t = op("gpsimd", [], lambda e: e.tensor_scalar(
                PB[:, slot, 128:384], PB[:, slot, 128:384], RS[:, 2 * slot + 1:2 * slot + 2], None, ALU.mult), "g_p")
        a_tok[slot] = t

    def turn(slot):
        b = 6 + slot % 2
        for j in range(3):
            t = op("tensor", [a_tok[slot], mk] + t_free.get(b, []), lambda e, j=j: e.transpose(
                PS[:, b, j * 128:j * 128 + 128], PB[:, slot, j * 128:j * 128 + 128], ID[:, :]),
                "t_t" if j == 2 else None)
        pb_free[slot] = [t]
        t = op("vector", [t] + pt_free.get(slot, []), lambda e: e.tensor_copy(
            PT[:, slot, :], PS[:, b, 0:384]), "v_t")
        t_free[b] = [t]
        b_tok[slot] = t

    def values(slot, v, dst, waits):
        op("tensor", [b_tok[slot]] + list(waits), lambda e: e.matmul(
            dst[:, 0:256], v(0), PT[:, slot, 0:256], start=True, stop=False), None)
        t = op("tensor", [], lambda e: e.matmul(
            dst[:, 128:256], v(1), PT[:, slot, 256:384], start=False, stop=True), "t_o")
        pt_free[slot] = [t]
        return t

    OB = 3
    otok = {}

    def pair_values(slots, v, tile, oh_free=()):
        for i, s in enumerate(slots):
            t = values(s, v[i][0], PS[64 * i:64 * i + 64, OB, 0:256], list(v[i][1]) + bank_free[OB])
        h, lo = split(Oh[:, tile, :], Ol[:, tile, :], PS[:, OB, 0:256], [t], oh_free)
        bank_free[OB] = [lo]
        otok[tile] = [h, lo]

    def pair_program(pairs):
        n = len(pairs)
        seq = []
        for i in range(n + 1):
            if i < n:
                seq.append(pairs[i][0])
            if i >= 1:
                seq.append(pairs[i - 1][1])
                seq.append(pairs[i - 1][2])
        return seq

    def head_pair(i, qs, ks, vs, tile, bias, scale, waits, oh_free=(), waitb=()):
        slots = [2 * (i % 2), 2 * (i % 2) + 1]

        def sa():
            for s, q, k in zip(slots, qs, ks):
                scores(s, q, k, waits(), bias(slots.index(s)), scale, waitb=waitb)

        def sb_():
            for s in slots:
                turn(s)

        def sc():
            pair_values(slots, vs(), tile, oh_free)

        return sa, sb_, sc

    def fox_pair(i):
        h = 2 * i
        return head_pair(
            i, [QF[0:80, h + j, :] for j in range(2)], [KF[0:80, h + j, :] for j in range(2)],
            lambda: [((lambda kb, j=j: VF[:, kb, (h + j) * 64:(h + j + 1) * 64]), [vf_tok[h // 4]]) for j in range(2)],
            4 + i, lambda j: TRI[:, :], SCALE64, lambda: [kf_tok[h // 4], qf_tok[h // 4]] + aug,
            oh_free=[mm_tok[chunk_no[("ukv", 0)]]] if ("ukv", 0) in chunk_no and chunk_no[("ukv", 0)] in mm_tok else [])

    def mla_pair(i):
        h = 2 * i
        return head_pair(
            i, [QM[0:96, h + j, :] for j in range(2)], [KM[0:96, h + j, :] for j in range(2)],
            lambda: [((lambda kb, j=j: VM[:, kb, (h + j) * 64:(h + j + 1) * 64]), vm_tok) for j in range(2)],
            i, lambda j: TRI[:, :], MLA_SCALE, lambda: qm_tok[h // 2] + km_tok,
            oh_free=[mm_tok[chunk_no[("ukv", 0)]]])

    xready.clear()
    xready.update(cn)
    for j in range(2):
        chunk_T(("uq", j), (Oh, Ol), ev_uq(j), kts=3, ncols=512, pairs=2)

    def ukv():
        n = mm_begin(("ukv", 0))
        for pr in range(2):
            b = gbank()
            mm_T(n, 2, 1024, 2 * pr, PS[:, b, 0:T], list(bank_free[b]), Oh, Ol, lambda k: 3 + k)
            tok = mm_T(n, 2, 1024, 2 * pr + 1, PS[:, b, T:2 * T], [], Oh, Ol, lambda k: 3 + k, signal="t_mm")
            heads_out(KM, 4 * pr, km_tok)(b, tok)
        for half in range(2):
            b = gbank()
            tok = mm_N(n, 2, 1024, 512, 512, PS[:, b, :], half, list(bank_free[b]), Oh, Ol, lambda k: 3 + k, signal="t_mm")
            t = op("scalar", [tok], lambda e, b=b, half=half: e.activation(VM[:, half, :], PS[:, b, :], ACT.Copy), "a_ev")
            bank_free[b] = [t]
            vm_tok.append(t)
        mm_tok[n] = tok

    ukv()
    xready.clear()
    xready.update(xr)
    pend += pair_program([fox_pair(i) for i in range(4)] + [mla_pair(i) for i in range(4)])

    ga_tok = []

    def ev_gate(g):
        def ev(pr, b, tok):
            t = op("scalar", [tok], lambda e: e.activation(
                GA[:, 2 * g:2 * g + 2, :].rearrange("p j t -> p (j t)"), PS[:, b, :], ACT.Copy), "a_ev")
            bank_free[b] = [t]
            ga_tok.append(t)
        return ev

    for g in range(8):
        pump()
        chunk_T(("in", 10 + g), H, ev_gate(g), mid=1)
        pump()
    h_used = mm_tok[chunk_no[("in", 17)]]
    while pend:
        pump()
    for tile in range(8):
        xready[tile] = otok[tile]

    yready = {}

    def step_o(i):
        n = mm_begin(("o", i))
        gm, gf = (GA[:, a + 2 * i:a + 2 * i + 2, :].rearrange("p j t -> p (j t)") for a in (0, 8))
        sg = op("scalar", ga_tok, lambda e: e.activation(gm, gm, ACT.Sigmoid), "a_sg")
        sg = op("scalar", [], lambda e: e.activation(gf, gf, ACT.Sigmoid), "a_sg")
        bs, toks = [], []
        for part in range(2):
            b = gbank()
            bs.append(b)
            slot = n % HL
            for nt in range(2):
                for k in range(4):
                    kk = 4 * part + k
                    at = kk * 256 + nt * 128
                    wh, wl = whi[slot][:, at:at + 128], wlo[slot][:, at:at + 128]
                    dst = PS[:, b, nt * T:nt * T + T]

                    def go(e, wh=wh, wl=wl, kk=kk, dst=dst, k=k):
                        e.matmul(dst, wh, Oh[:, kk, :], start=k == 0, stop=False)
                        e.matmul(dst, wh, Ol[:, kk, :], start=False, stop=False)
                        return e.matmul(dst, wl, Oh[:, kk, :], start=False, stop=k == 3)

                    tok = op("tensor", bank_free[b] + [hi_tok[n], lo_tok[n]] + xwait(kk), go,
                             "t_mm" if nt == 1 and k == 3 else None)
            toks.append(tok)
        mm_tok[n] = tok
        t = op("vector", [toks[0], sg], lambda e: e.tensor_tensor(gm, PS[:, bs[0], :], gm, ALU.mult), "v_y")
        bank_free[bs[0]] = [t]
        t = op("vector", [toks[1]], lambda e: e.tensor_tensor(gf, PS[:, bs[1], :], gf, ALU.mult), "v_y")
        bank_free[bs[1]] = [t]
        t = op("vector", [t], lambda e: e.tensor_tensor(gm, gm, gf, ALU.add), "v_y")
        fl = lambda x: x[:, 2 * i:2 * i + 2, :].rearrange("p j t -> p (j t)")
        h, lo = split(fl(Hh), fl(Hl), gm, [t], [h_used])
        yready[2 * i] = yready[2 * i + 1] = [h, lo]
        return t

    rot["banks"] = [0, 1, 2, 3]
    for i in range(4):
        ga_done = step_o(i)
    o_used = mm_tok[chunk_no[("o", 3)]]
    xready.clear()
    xready.update(yready)

    x_tok = {}

    def ev_res(i, gate, gtok):
        def ev(pr, b, tok):
            for j in range(2):
                k = 2 * i + j
                t = op("vector", [tok] + gtok, lambda e, k=k, j=j: e.scalar_tensor_tensor(
                    X[:, k, :], PS[:, b, j * T:j * T + T], gate(k), X[:, k, :], ALU.mult, ALU.add), "v_x")
                x_tok[k] = t
            bank_free[b] = [t]
        return ev

    def ev_add(i):
        def ev(pr, b, tok):
            t = op("vector", [tok], lambda e: e.tensor_tensor(
                X[:, 2 * i:2 * i + 2, :].rearrange("p j t -> p (j t)"), PS[:, b, :],
                X[:, 2 * i:2 * i + 2, :].rearrange("p j t -> p (j t)"), ALU.add), "v_x")
            x_tok[2 * i] = x_tok[2 * i + 1] = t
            bank_free[b] = [t]
        return ev

    for i in range(4):
        chunk_T(("out", i), H, ev_res(i, lambda k: ADA[:, 16 + k:17 + k], [ada_acc[2]]))
    h_used = mm_tok[chunk_no[("out", 3)]]

    gs_ffn = op("vector", [ada_acc[4], small], lambda e: e.scalar_tensor_tensor(
        GS[:, 8:16], ADA[:, 32:40], 1.0, col("norm_ffn_g", 0, 8), ALU.add, ALU.mult), "v_gs")
    bb, rr = stats(lambda k: X[:, k, :], 8, D, lambda k: [x_tok[k]])
    x_free[:] = [h_used]
    xready.clear()
    apply(lambda k: X[:, k, :], 8, lambda k: GS[:, 8 + k:9 + k], lambda k: ADA[:, 24 + k:25 + k], bb, rr, H,
          waits=[gs_ffn, ada_acc[3]])
    x_free[:] = []
    hready = dict(xready)

    wk_free = {}
    hid = {}
    hid_free = {s: [o_used] for s in range(8)}
    UC = lambda s: PBf[:, s * 512:(s + 1) * 512]

    def up_one(j):
        s = j % 3
        st1 = {}

        def ev(pr, b, tok):
            for i, tile in enumerate((j, 22 + j)):
                t = op("scalar", [tok] + wk_free.get(s, []), lambda e, i=i, tile=tile: e.activation(
                    UC(s)[:, i * T:i * T + T], PS[:, b, i * T:i * T + T], ACT.Identity,
                    bias=col("conv_b", tile), scale=col("conv_w", 88 + tile)), "a_u")
            for tap, sh in ((1, 1), (0, 2)):
                for i, tile in enumerate((j, 22 + j)):
                    u = UC(s)[:, i * T + sh:i * T + T]
                    t = op("vector", [t] if i == 0 else [], lambda e, i=i, u=u, tile=tile, tap=tap, sh=sh: e.scalar_tensor_tensor(
                        u, PS[:, b, i * T:i * T + T - sh], col("conv_w", tap * 44 + tile), u, ALU.mult, ALU.add), "v_u")
            bank_free[b] = [t]
            st1["t"] = t

        def late():
            g, m = PTf[:, (j % 2) * 512:(j % 2) * 512 + 256], PTf[:, (j % 2) * 512 + 256:(j % 2) * 512 + 512]
            t = op("scalar", [st1["t"]] + wk_free.get(("m", j % 2), []), lambda e: e.activation(g, UC(s)[:, 0:T], ACT.Silu), "a_u2")
            t = op("vector", [t], lambda e: e.tensor_tensor(m, g, UC(s)[:, T:2 * T], ALU.mult), "v_u2")
            wk_free[s] = [t]
            h, lo = split(Oh[:, j % 8, :], Ol[:, j % 8, :], m, [t], hid_free.get(j % 8, []))
            wk_free[("m", j % 2)] = [lo]
            hid[j] = [h, lo]

        return ev, late

    def down(key, i, n_pairs):
        n = mm_begin(key)
        slot = n % HL
        done = {}
        for nt in range(8):
            b = 4 + nt // 2
            dst = PS[:, b, (nt % 2) * T:(nt % 2) * T + T]
            for k in range(2):
                tile = (2 * i + k) % 8
                wh, wl = (w[slot][:, k * 1024 + nt * 128:k * 1024 + nt * 128 + 128] for w in (whi, wlo))
                start = i == 0 and k == 0 and nt % 2 == 0
                stop = i == n_pairs - 1 and k == 1

                def go(e, dst=dst, wh=wh, wl=wl, tile=tile, start=start, stop=stop):
                    e.matmul(dst, wh, Oh[:, tile, :], start=start, stop=False, skip_group_check=True)
                    e.matmul(dst, wh, Ol[:, tile, :], start=False, stop=False, skip_group_check=True)
                    return e.matmul(dst, wl, Oh[:, tile, :], start=False, stop=stop, skip_group_check=True)

                last = nt == 7 and k == 1
                sig = "t_mm" if last or (i == n_pairs - 1 and nt % 2 == 1 and k == 1) else None
                fr = bank_free[b] + s_free.get(b, []) + t_free.get(b, []) if i == 0 else []
                tok = op("tensor", [hi_tok[n], lo_tok[n]] + hid[2 * i + k] + fr, go, sig)
            if nt % 2 == 1:
                done[nt // 2] = tok
        mm_tok[n] = tok
        for k in range(2):
            hid_free[(2 * i + k) % 8] = [tok]
        return done

    late = []
    for i in range(11):
        for j in (2 * i, 2 * i + 1):
            ev, lt = up_one(j)
            chunk_T(("up", j), H, ev)
            if late:
                late.pop(0)()
            late.append(lt)
        if i >= 1:
            down(("down", i - 1), i - 1, 11)
    late.pop(0)()
    done = down(("down", 10), 10, 11)
    h_used = mm_tok[chunk_no[("up", 21)]]
    for i in range(4):
        ev_res(i, lambda k: ADA[:, 40 + k:41 + k], [ada_acc[5]])(0, 4 + i, done[i])

    bb, rr = stats(lambda k: X[:, k, :], 8, D, lambda k: [x_tok[k]])
    for k in range(8):
        t = op("vector", [rr, small], lambda e, k=k, bb=bb: e.scalar_tensor_tensor(
            X[:, k, :], X[:, k, :], col("norm_final_g", k), PS[:, bb, 256:512], ALU.mult, ALU.mult), "v_x")
        x_tok[k] = t
    bank_free[bb] = [t]

    lam_in = op("sync", [t], lambda e: e.dma_start(TT[:, 0, :], lam4), "d_lam", 16)
    tt_free[0] = []

    def lam():
        for i in range(2):
            t = op("vector", [lam_in], lambda e, i=i: e.tensor_tensor_reduce(
                TT[:, 1, i * 64:i * 64 + 64], TT[:, 0, i * 128:i * 128 + 64], TT[:, 0, i * 128 + 64:i * 128 + 128],
                1.0, 0.0, ALU.mult, ALU.add, LM[:, i:i + 1]), "v_lam")
        t = op("scalar", [t], lambda e: e.activation(LM[:, 2:4], LM[:, 0:2], ACT.Exp), "a_lam")
        t = op("vector", [t], lambda e: e.scalar_tensor_tensor(
            LM[:, 4:5], LM[:, 2:3], LAM_INIT, LM[:, 3:4], ALU.add, ALU.subtract), "v_lam")
        w = op("vector", [small], lambda e: e.tensor_scalar(SW[:, :], col("subln"), 1.0 - LAM_INIT, None, ALU.mult), "v_lam")
        tt_free[0] = tt_free[1] = [t]
        return t, w

    lam_tok, sw_tok = lam()
    ga_free = [ga_done]
    qk_free, v_free = [], []
    fin = None

    for layer in range(2):
        al = alibi8 if layer == 0 else alibi16
        nh = 8 * (layer + 1)
        al_tok = op("sync", ga_free, lambda e, al=al, nh=nh: e.dma_start(GA[:, 0:nh, :], al), "d_al", 16)
        bb, rr = stats(lambda k: X[:, k, :], 8, D, lambda k: [x_tok[k]])
        x_free[:] = [h_used]
        xready.clear()
        apply(lambda k: X[:, k, :], 8, lambda k: col("attn_norm", layer * 8 + k), None, bb, rr, H)
        x_free[:] = []
        hr = dict(xready)
        rot["banks"] = [0, 1, 2]
        qt, kt_, vt = [], [], []
        otok.clear()
        o_free = [hid_free[s][0] for s in range(8)]

        if layer == 0:
            od_tok = {}

            def diff_head(h):
                slots = [2 * (h % 2), 2 * (h % 2) + 1]

                def sa():
                    for m, s in enumerate(slots):
                        r = slice(64 * m, 64 * m + 64)
                        scores(s, QM[r, h, :], KM[r, h, :], [qt[h // 2], kt_[h // 2]], GA[:, h, :], SCALE64,
                               normalise=False, waitb=[al_tok])
                    s0, s1 = slots
                    t = a_tok[s1]
                    for c0, c1, j in ((0, 128, 0), (128, 384, 1)):
                        g = op("gpsimd", [t, lam_tok], lambda e, c0=c0, c1=c1, j=j: e.tensor_scalar(
                            PB[:, s1, c0:c1], PB[:, s1, c0:c1], RS[:, 2 * s1 + j:2 * s1 + j + 1], LM[:, 4:5],
                            ALU.mult, ALU.mult), "g_p")
                    for c0, c1, j in ((0, 128, 0), (128, 384, 1)):
                        t = op("vector", [g], lambda e, c0=c0, c1=c1, j=j: e.scalar_tensor_tensor(
                            PB[:, s0, c0:c1], PB[:, s0, c0:c1], RS[:, 2 * s0 + j:2 * s0 + j + 1], PB[:, s1, c0:c1],
                            ALU.mult, ALU.subtract), "v_a")
                    a_tok[s0] = t
                    pb_free[s1] = [t]

                def sb_():
                    turn(slots[0])

                def sc():
                    t = values(slots[0], lambda kb: V[:, kb, h * 128:h * 128 + 128], PS[:, OB, 0:256],
                               [vt[h // 2]] + bank_free[OB])
                    t = op("scalar", [t], lambda e: e.activation(QF[:, h, :], PS[:, OB, 0:256], ACT.Copy), "a_ev")
                    bank_free[OB] = [t]
                    od_tok[h] = t

                return sa, sb_, sc

            def subln(g):
                def go():
                    b = gbank()
                    fr = list(bank_free[b])
                    for i in range(2):
                        h = 2 * g + i
                        sq = op("scalar", [od_tok[h]] + sq_free.get(i, []), lambda e, i=i, h=h: e.activation(
                            SQ[:, i, :], QF[:, h, :], ACT.Square), "a_sq")
                        for half in range(2):
                            t = op("tensor", [sq] + fr, lambda e, i=i, half=half: e.matmul(
                                PS[:, b, 2 * i + half:2 * i + half + 1], SQ[:, i, half * 128:half * 128 + 128],
                                ONES[:, 0:1], start=i == 0 and half == 0, stop=True, skip_group_check=True), "t_sq")
                        sq_free[i] = [t]
                    _, t = rstd(b, t, 4, 128)
                    for i in range(2):
                        h = 2 * g + i
                        u = op("vector", [t, sw_tok] + tt_free.get(i, []), lambda e, i=i, h=h: e.scalar_tensor_tensor(
                            TT[:, i, :], QF[:, h, :], SW[:, 0:1], PS[:, b, i * T:i * T + T], ALU.mult, ALU.mult), "v_nrm")
                        hh, lo = split(Oh[:, h, :], Ol[:, h, :], TT[:, i, :], [u], o_free)
                        tt_free[i] = [lo]
                        otok[h] = [hh, lo]
                    bank_free[b] = [u]
                return go

            def ev_q(dst, toks):
                def ev(pr, b, tok, j):
                    t = op("scalar", [tok], lambda e: e.activation(
                        dst[:, 2 * j:2 * j + 2, :].rearrange("p j t -> p (j t)"), PS[:, b, :], ACT.Copy), "a_ev")
                    bank_free[b] = [t]
                    toks.append(t)
                return ev

            for j in range(4):
                if j:
                    pump()
                chunk_T(("qkv0", j), H, lambda pr, b, tok, j=j: ev_q(QM, qt)(pr, b, tok, j), mid=1)
                pump()
                chunk_T(("qkv0", 4 + j), H, lambda pr, b, tok, j=j: ev_q(KM, kt_)(pr, b, tok, j), mid=1)
                pump()
                chunk_N(("qkv0", 8 + j), H, V[:, :, 256 * j:256 * j + 256], vt, mid=1)
                while pend:
                    pump()
                pend += pair_program([diff_head(2 * j), diff_head(2 * j + 1)]) + [subln(j)]
            while pend:
                pump()
        else:
            dstq, dstk = (QM, QF), (KM, KF)

            def moba_pair(i):
                h = 2 * i
                q, k = dstq[h // 8], dstk[h // 8]
                return head_pair(
                    i, [q[0:64, (h + j) % 8, :] for j in range(2)], [k[0:64, (h + j) % 8, :] for j in range(2)],
                    lambda: [((lambda kb, j=j: V[:, kb, (h + j) * 64:(h + j + 1) * 64]), [vt[h // 4]]) for j in range(2)],
                    i, lambda j: GA[:, h + j, :], SCALE64, lambda: [qt[h // 4], kt_[h // 4]],
                    oh_free=o_free, waitb=[al_tok])

            for j in range(4):
                if j:
                    pump()
                chunk_T(("qkv1", j), H, lambda pr, b, tok, j=j: heads_out(dstq[j // 2], 4 * (j % 2), qt)(b, tok), mid=1)
                pump()
                chunk_T(("qkv1", 4 + j), H, lambda pr, b, tok, j=j: heads_out(dstk[j // 2], 4 * (j % 2), kt_)(b, tok), mid=1)
                pump()
                chunk_N(("qkv1", 8 + j), H, V[:, :, 256 * j:256 * j + 256], vt, mid=1)
                while pend:
                    pump()
                pend += pair_program([moba_pair(2 * j), moba_pair(2 * j + 1)])
            while pend:
                pump()
        ga_free = [("v_s", P.counts["v_s"])]
        h_used = mm_tok[chunk_no[(f"qkv{layer}", 11)]]
        rot["banks"] = [0, 1, 2, 3]
        xready.clear()
        xready.update(otok)
        for i in range(4):
            chunk_T((f"out{layer}", i), (Oh, Ol), ev_add(i))
        o_used = mm_tok[chunk_no[(f"out{layer}", 3)]]

        bb, rr = stats(lambda k: X[:, k, :], 8, D, lambda k: [x_tok[k]])
        x_free[:] = [h_used]
        xready.clear()
        apply(lambda k: X[:, k, :], 8, lambda k: col("mlp_norm", layer * 8 + k), None, bb, rr, H)
        x_free[:] = []
        for s in range(8):
            hid_free[s] = [o_used]
        hid.clear()
        wk_free.clear()

        def mlp_one(i):
            s = i % 2
            st1 = {}
            r, m = PBf[:, s * 512:s * 512 + 512], PTf[:, s * 512:s * 512 + 512]

            def ev(pr, b, tok):
                t = op("scalar", [tok] + wk_free.get(("r", s), []), lambda e: e.activation(r, PS[:, b, :], ACT.Relu), "a_u")
                t = op("vector", [t] + wk_free.get(("m", s), []), lambda e: e.scalar_tensor_tensor(
                    m, PS[:, b, :], 0.0, r, ALU.max, ALU.mult), "v_u")
                bank_free[b] = [t]
                wk_free[("r", s)] = [t]
                st1["t"] = t

            def late():
                a = (2 * i) % 8
                fl = lambda x: x[:, a:a + 2, :].rearrange("p j t -> p (j t)")
                h, lo = split(fl(Oh), fl(Ol), m, [st1["t"]], hid_free[a])
                wk_free[("m", s)] = [lo]
                hid[2 * i] = hid[2 * i + 1] = [h, lo]

            return ev, late

        late = []
        for i in range(16):
            ev, lt = mlp_one(i)
            chunk_T((f"ff1{layer}", i), H, ev)
            if late:
                late.pop(0)()
            late.append(lt)
            if i >= 2:
                down((f"ff2{layer}", i - 2), i - 2, 16)
        late.pop(0)()
        down((f"ff2{layer}", 14), 14, 16)
        done = down((f"ff2{layer}", 15), 15, 16)
        h_used = mm_tok[chunk_no[(f"ff1{layer}", 15)]]
        for i in range(4):
            ev_add(i)(0, 4 + i, done[i])

    bb, rr = stats(lambda k: X[:, k, :], 8, D, lambda k: [x_tok[k]])
    for k in range(8):
        t = op("vector", [rr], lambda e, k=k, bb=bb: e.scalar_tensor_tensor(
            X[:, k, :], X[:, k, :], col("final_norm", k), PS[:, bb, 256:512], ALU.mult, ALU.mult), "v_x")
        if k % 2 == 1:
            fin = op("sync" if k % 4 == 1 else "scalar", [t], lambda e, k=k: e.dma_start(
                out[:, k - 1:k + 1, :], X[:, k - 1:k + 1, :]), "d_out", 16)

    with nc.Block() as block:
        @block.sync
        def _(e):
            P.run("sync", e)
            e.wait_ge(P.sems["d_out"], P.counts["d_out"])

        @block.scalar
        def _(e):
            P.run("scalar", e)

        @block.vector
        def _(e):
            P.run("vector", e)

        @block.gpsimd
        def _(e):
            P.run("gpsimd", e)

        @block.tensor
        def _(e):
            P.run("tensor", e)


def _tiles(w, cols):
    k = w.shape[0] // 128
    return w[:, cols].reshape(k, 128, len(cols)).transpose(1, 0, 2).reshape(128, k * len(cols))


def _chunks(a):
    r = np.arange
    cut = np.cumsum([0, 384, 256, 32, 512, 512, 512, 8, 1024, 1024])
    cq, ckv, kr, fq, fk, fv, ff, gm, gf = (r(cut[i], cut[i + 1]) for i in range(9))
    sw = np.concatenate([r(16, 32), r(16)])
    cols_in = np.concatenate([cq, np.tile(ff, 16), ckv, np.tile(kr, 4), np.tile(kr[sw], 4), fk, fq, fv, gm, gf])
    uq = np.concatenate([np.concatenate([r(64), 64 + r(32), 64 + sw]) + 96 * h for h in range(8)])
    ukv = np.concatenate([np.concatenate([r(64) + 128 * h for h in range(8)]),
                          np.concatenate([64 + r(64) + 128 * h for h in range(8)])])
    up = np.concatenate([np.concatenate([r(128) + 128 * j, 2816 + r(128) + 128 * j]) for j in range(22)])
    out = []
    for kind, i in weight_order():
        c = r(256 * i, 256 * i + 256)
        if kind == "in":
            t = _tiles(a["w_in"][0], cols_in[c])
        elif kind == "uq":
            t = np.pad(_tiles(a["w_uq"][0], uq[512 * i:512 * i + 512]), ((0, 0), (0, 512)))
        elif kind == "ukv":
            t = _tiles(a["w_ukv"][0], ukv)
        elif kind == "o":
            t = np.concatenate([_tiles(a["w_o_mla"][0], c), _tiles(a["w_o_fox"][0], c)], axis=1)
        elif kind == "out":
            t = _tiles(a["w_out"][0], c)
        elif kind == "up":
            t = _tiles(a["w_up"][0], up[c])
        elif kind == "down":
            t = _tiles(a["w_down"][0][c], r(1024))
        else:
            layer = int(kind[-1])
            w = a[{"qkv": "w_in_2", "out": "w_out_2", "ff1": "w_ff1_2", "ff2": "w_ff2_2"}[kind[:-1]]][layer]
            t = _tiles(w[c], r(1024)) if kind[:-1] == "ff2" else _tiles(w, c)
        out.append(t)
    return np.stack(out)


def _slopes(n):
    return np.array([2.0 ** (-8.0 * (h + 1) / n) for h in range(n)], dtype=np.float32)


def _alibi(n):
    dist = (128 + np.arange(128)[:, None] - np.arange(256)[None, :]).astype(np.float32)
    t = -_slopes(n)[None, :, None] * dist[:, None, :] / np.float32(SCALE64)
    return np.where(dist[:, None, :] >= 0, t, np.float32(NEG)).astype(np.float32)


def _smalls(a):
    def tiles(v):
        return np.asarray(v).reshape(-1, 128).T

    p = np.arange(128)
    one = lambda f: np.array([f(i) for i in range(128)], np.float32)[:, None]
    inv = np.float32(10000.0) ** (-np.arange(0, 32, 2, dtype=np.float32) / np.float32(32))
    m1 = np.stack([one(lambda q: 8.0 if q < 72 and q - 64 == h else 0.0)[:, 0] for h in range(8)], 1)
    m2 = np.stack([one(lambda q: 1.0 if q - 72 == h else 0.0)[:, 0] for h in range(8)], 1)
    parts = [
        tiles(a["c"]), tiles(a["b_ada"]), tiles(a["norm_mix_g"]), tiles(a["norm_ffn_g"]), tiles(a["norm_final_g"]),
        tiles(a["q_norm_g"]), tiles(a["kv_norm_g"]), tiles(a["conv_w"]), tiles(a["conv_b"]),
        tiles(a["attn_norm_2"]), tiles(a["mlp_norm_2"]), tiles(a["final_norm_2"]), tiles(a["diff_subln_2"]),
        np.tile(a["b_forget"][0], 16)[:, None], inv[p % 16][:, None].astype(np.float32),
        one(lambda q: -1.0 if q % 32 < 16 else 1.0), one(lambda q: EPS), m1, m2,
        one(lambda q: -8.0 if q >= 72 else 0.0), one(lambda q: 1.0 if q < 72 else 0.0),
    ]
    return np.concatenate(parts, axis=1)


def _layout(a):
    ada = a["w_ada"][0].reshape(4, 2, 128, 6, 1024).transpose(3, 0, 2, 1, 4).reshape(24, 128, 2048)
    tri = np.where(np.arange(128)[None, :] <= np.arange(128)[:, None], np.float32(0), np.float32(NEG))
    masks = np.concatenate([np.eye(128, dtype=np.float32), np.zeros((128, 128), np.float32), tri], axis=1)
    return {
        "wall": _chunks(a),
        "wada": ada,
        "smalls": _smalls(a),
        "pos": np.tile(a["positions"], (128, 1)),
        "xt": a["x"][0].T.reshape(8, 128, 256).transpose(1, 0, 2),
        "masks": masks.astype(np.float32),
        "lam4": np.tile(a["diff_lambda_2"][0].reshape(1, 256), (128, 1)),
        "alibi8": _alibi(8),
        "alibi16": _alibi(16),
    }


def kernel(**inputs):
    import concourse.bacc as _bacc
    from concourse.bass_utils import run_bass_kernel_spmd as _run

    a = {k: np.asarray(v) for k, v in inputs.items()}
    arrays = {k: np.ascontiguousarray(v) for k, v in _layout(a).items()}
    nc = _bacc.Bacc("TRN2", target_bir_lowering=False, num_devices=1)
    aps = [nc.dram_tensor(k, v.shape, mybir.dt.from_np(v.dtype), kind="ExternalInput").ap() for k, v in arrays.items()]
    o = nc.dram_tensor("out", (128, 8, 256), F32, kind="ExternalOutput").ap()
    build(nc, *aps, o)
    r = _run(nc, [arrays], core_ids=[0])
    y = r.results[0]["out"]
    return np.ascontiguousarray(y.transpose(1, 0, 2).reshape(1024, 256).T).reshape(1, 256, 1024)
```

```python
import math
from contextlib import ExitStack

import numpy as np

import concourse.bass as bass
from concourse import mybir
from concourse.alu_op_type import AluOpType as ALU

F32 = mybir.dt.float32
F32R = mybir.dt.float32r
I32 = mybir.dt.int32
ACT = mybir.ActivationFunctionType

T = 256
D = 1024
CH = 2048
EPS = 1e-6
NEG = -1e30
BIG = 3e38
MLA_SCALE = 1.0 / math.sqrt(96.0)
SCALE64 = 0.125
LAM_INIT = 0.8 - 0.6 * math.exp(0.0)
TWO_PI = 2.0 * math.pi
MAGIC = 12582912.0
C1 = 6.28125
C2 = float(np.float32(np.round((TWO_PI - C1) * 2.0**18) / 2.0**18))
C3 = float(np.float32(TWO_PI - C1 - C2))

RAW = 4
HL = 3

COLS = {}


def _columns():
    at = 0
    for name, n in [
        ("c", 8), ("b_ada", 48), ("norm_mix_g", 8), ("norm_ffn_g", 8), ("norm_final_g", 8),
        ("q_norm_g", 3), ("kv_norm_g", 2), ("conv_w", 132), ("conv_b", 44), ("attn_norm", 16),
        ("mlp_norm", 16), ("final_norm", 8), ("subln", 1), ("b_forget", 1), ("invf", 1), ("sgn", 1),
        ("eps", 1), ("m1", 8), ("m2", 8), ("m3", 1), ("m4", 1),
    ]:
        COLS[name] = at
        at += n
    return at


NCOL = _columns()


QKV_ORDER = (0, 4, 1, 5, 8, 2, 6, 9, 3, 7, 10, 11)


def weight_order():
    order = [("in", i) for i in range(9)] + [("uq", 0), ("uq", 1), ("ukv", 0)]
    order += [("in", i) for i in range(9, 17)]
    order += [("o", i) for i in range(4)] + [("out", i) for i in range(4)]
    for i in range(11):
        order += [("up", 2 * i), ("up", 2 * i + 1)]
        if i >= 1:
            order.append(("down", i - 1))
    order.append(("down", 10))
    for layer in range(2):
        order += [(f"qkv{layer}", j) for j in QKV_ORDER]
        order += [(f"out{layer}", i) for i in range(4)]
        for i in range(16):
            order.append((f"ff1{layer}", i))
            if i >= 2:
                order.append((f"ff2{layer}", i - 2))
        order += [(f"ff2{layer}", 14), (f"ff2{layer}", 15)]
    return order


USED = {"uq": 1536}


def stream_order():
    order = weight_order()
    items = [("w", n) + order[n] for n in range(2)] + [("ada0", j) for j in range(8)]
    late = [("ada", cb, kk) for cb in range(2, 6) for kk in range(4)]
    after = list(range(4, 11)) + list(range(22, 27)) + [n for n in range(len(order)) if order[n][0] == "down"][:4]
    for n in range(2, len(order)):
        items.append(("w", n) + order[n])
        if n in after:
            items.append(late.pop(0))
    return items


class Program:

    def __init__(self, nc, ctx):
        self.nc, self.ctx = nc, ctx
        self.queues = {e: [] for e in ("sync", "scalar", "vector", "gpsimd", "tensor")}
        self.sems, self.counts, self.seen = {}, {}, {}

    def op(self, engine, waits, issue, signal=None, by=1):
        q = self.queues[engine]
        for name, value in waits:
            if self.seen.get((engine, name), 0) < value:
                self.seen[(engine, name)] = value
                q.append((None, self.sems[name], value))
        if signal is None:
            q.append((issue, None, 0))
            return None
        if signal not in self.sems:
            self.sems[signal] = self.ctx.enter_context(self.nc.semaphore(signal))
        self.counts[signal] = self.counts.get(signal, 0) + by
        q.append((issue, self.sems[signal], by))
        return signal, self.counts[signal]

    def run(self, engine, eng):
        for issue, sem, n in self.queues[engine]:
            if issue is None:
                eng.wait_ge(sem, n)
            else:
                ins = issue(eng)
                if sem is not None:
                    ins.then_inc(sem, n)


def build(nc, wall, wada, smalls, pos, xt, masks, lam4, alibi8, alibi16, out):
    ctx = ExitStack()
    with ctx:
        _build(nc, ctx, wall, wada, smalls, pos, xt, masks, lam4, alibi8, alibi16, out)


def _build(nc, ctx, wall, wada, smalls, pos, xt, masks, lam4, alibi8, alibi16, out):
    def sb(name, shape, dt=F32):
        return ctx.enter_context(nc.sbuf_tensor(name, shape, dt))

    P = Program(nc, ctx)
    op = P.op

    raw = [sb(f"raw{i}", [128, CH]) for i in range(RAW)]
    whi = [sb(f"whi{i}", [128, CH], F32R) for i in range(HL)]
    wlo = [sb(f"wlo{i}", [128, CH], F32R) for i in range(HL)]
    X = sb("X", [128, 8, T])
    Hh = sb("Hh", [128, 8, T], F32R)
    Hl = sb("Hl", [128, 8, T], F32R)
    Oh = sb("Oh", [128, 8, T], F32R)
    Ol = sb("Ol", [128, 8, T], F32R)
    QM = sb("QM", [128, 8, T])
    KM = sb("KM", [128, 8, T])
    QF = sb("QF", [128, 8, T])
    KF = sb("KF", [128, 8, T])
    V = sb("V", [128, 2, 1024])
    GA = sb("GA", [128, 16, T])
    ACC = sb("ACC", [128, 1024])
    SQ = sb("SQ", [128, 4, T])
    COS = sb("COS", [128, T])
    SIN = sb("SIN", [128, T])
    PB = sb("PB", [128, 4, 384])
    PT = sb("PT", [128, 4, 384])
    TT = sb("TT", [128, 2, T])
    RB = sb("RB", [128, 2, T])
    ID = sb("ID", [128, 128])
    TRI = sb("TRI", [128, T])
    ONES = sb("ONES", [128, 128])
    SM = sb("SM", [128, NCOL])
    ADA = sb("ADA", [128, 48])
    GS = sb("GS", [128, 16])
    CA = sb("CA", [128, 8])
    GC = sb("GC", [128, 8])
    ST = sb("ST", [128, 2])
    RS = sb("RS", [128, 8])
    NM = sb("NM", [128, 8])
    LM = sb("LM", [128, 6])
    SW = sb("SW", [128, 1])
    PS = ctx.enter_context(nc.psum_tensor("PS", [128, 8, 512], F32))

    def col(name, i=0, n=1, p0=0, p1=128):
        return SM[p0:p1, COLS[name] + i:COLS[name] + i + n]

    PBf = PB[:, :, :].rearrange("p a b -> p (a b)")
    PTf = PT[:, :, :].rearrange("p a b -> p (a b)")
    f32 = lambda ap: ap.bitcast(F32)

    small = op("sync", [], lambda e: e.dma_start(SM[:, :], smalls), "d_small", 16)
    xin = op("sync", [], lambda e: e.dma_start(X[:, :, :], xt), "d_x", 16)
    items = stream_order()
    chunk_no = {it[2:]: it[1] for it in items if it[0] == "w"}
    raw_free = {}
    landed = {}

    def load(i):
        it = items[i]
        slot = i % RAW
        if it[0] == "ada0":
            dst, src = raw[slot][:, :], wada[it[1]]
        elif it[0] == "ada":
            _, cb, kk = it
            dst, src = raw[slot][:, :], wada[cb * 4 + kk]
        else:
            n = USED.get(it[2], CH)
            dst, src = raw[slot][:, 0:n], wall[it[1]][:, 0:n]
        landed[i] = op("sync", raw_free.get(i - RAW, []), lambda e: e.dma_start(dst, src), f"d_raw{slot}", 16)

    for i in range(RAW):
        load(i)
    posi = TT[:, 0, :].bitcast(I32)
    pin = op("scalar", [], lambda e: e.dma_start(posi, pos), "d_pos", 16)
    mk = op("scalar", [], lambda e: e.dma_start(ID[:, :], masks[:, 0:128]), "d_id", 16)
    mt = op("scalar", [], lambda e: e.dma_start(TRI[:, :], masks[:, 128:384]), "d_tri", 16)
    lam_in = op("scalar", [], lambda e: e.dma_start(PTf[:, 768:1024], lam4), "d_lam", 16)
    ones = op("gpsimd", [], lambda e: e.memset(ONES[:, :], 1.0), "g_ones")

    st = {"next": 0, "ada": None}
    hi_tok, lo_tok, mm_tok = {}, {}, {}

    ada_acc = {}
    ada_free = []

    def take_ada(i, cb, kk):
        src = raw[i % RAW]
        for half in range(2):
            k = 2 * kk + half
            w = src[:, half * 1024:(half + 1) * 1024]
            if k == 0:
                while ada_late:
                    ada_late.pop(0)()
                tok = op("vector", [landed[i], cact] + ada_free, lambda e, w=w: e.tensor_scalar(
                    ACC[:, :], w, CA[:, 0:1], None, ALU.mult), "v_ada")
            else:
                tok = op("vector", [landed[i], st["ada"]], lambda e, w=w, k=k: e.scalar_tensor_tensor(
                    ACC[:, :], w, CA[:, k:k + 1], ACC[:, :], ALU.mult, ALU.add), "v_ada")
            st["ada"] = tok
        raw_free[i] = [st["ada"]]
        if kk == 3:
            acc = st["ada"]
            ada_late.append(lambda: ada_sum(cb, acc))

    ada_late = []

    def ada_sum(cb, acc):
        b = gbank()
        for j in range(8):
            t = op("tensor", [acc, ones] + bank_free[b], lambda e, j=j, b=b: e.matmul(
                PS[:, b, j:j + 1], ACC[:, j * 128:(j + 1) * 128], ONES[:, 0:1],
                start=True, stop=True), "t_ada" if j == 7 else None)
        ada_free[:] = [t]
        tok = op("vector", [t, small], lambda e, b=b, cb=cb: e.tensor_tensor(
            ADA[:, cb * 8:(cb + 1) * 8], PS[:, b, 0:8], col("b_ada", cb * 8, 8), ALU.add), "v_adab")
        bank_free[b] = [tok]
        ada_acc[cb] = tok

    gs_tok = {}

    def take_ada0(i, j):
        src = raw[i % RAW]
        b = 4 + j % 4
        free = [gs_tok[j - 4]] if j >= 4 else []
        for part in range(2):
            for k in range(8):
                t = op("tensor", [landed[i], cact] + free, lambda e, part=part, k=k: e.matmul(
                    PS[:, b, part:part + 1], src[:, k * 256 + part * 128:k * 256 + part * 128 + 128],
                    CA[:, k:k + 1], start=k == 0, stop=k == 7), "t_ada" if part == 1 and k == 7 else None)
        raw_free[i] = [t]
        t = op("vector", [t, small], lambda e: e.tensor_tensor(
            ADA[:, j:j + 9:8], PS[:, b, 0:2], SM[:, COLS["b_ada"] + j:COLS["b_ada"] + j + 9:8],
            ALU.add), "v_adab")
        gs_tok[j] = op("vector", [t], lambda e: e.scalar_tensor_tensor(
            GS[:, j:j + 1], ADA[:, 8 + j:9 + j], 1.0, col("norm_mix_g", j), ALU.add, ALU.mult), "v_gs")

    def take_weight(i, n, kind):
        slot = n % HL
        w = USED.get(kind, CH)
        src = raw[i % RAW]
        free = [mm_tok[n - HL]] if n >= HL else []
        hi_tok[n], lo_tok[n] = [], []
        for half in range(2):
            c = slice(half * CH // 2, min(w, (half + 1) * CH // 2))
            hi_tok[n].append(op("scalar", [landed[i]] + free, lambda e, c=c: e.activation(
                whi[slot][:, c], src[:, c], ACT.Copy), "a_whi"))
        for half in range(2):
            c = slice(half * CH // 2, min(w, (half + 1) * CH // 2))
            lo_tok[n].append(op("vector", [hi_tok[n][half]] + free, lambda e, c=c: e.tensor_tensor(
                wlo[slot][:, c], src[:, c], f32(whi[slot][:, c]), ALU.subtract), "v_wlo"))
        raw_free[i] = [lo_tok[n][1]]

    def weight_wait(n, last_col):
        half = (last_col - 1) // (CH // 2)
        return [hi_tok[n][half], lo_tok[n][half]]

    def take_next():
        i = st["next"]
        it = items[i]
        if it[0] == "ada0":
            take_ada0(i, it[1])
        elif it[0] == "ada":
            take_ada(i, it[1], it[2])
        else:
            take_weight(i, it[1], it[2])
        st["next"] = i + 1
        if i + RAW < len(items):
            load(i + RAW)

    def ensure(n):
        while st["next"] < len(items) and max(hi_tok, default=-1) < n:
            take_next()

    bank_free = {b: [] for b in range(8)}
    rot = {"banks": [0, 1, 2, 3], "at": 0}

    def gbank():
        b = rot["banks"][rot["at"] % len(rot["banks"])]
        rot["at"] += 1
        return b

    def mm_begin(key):
        n = chunk_no[key]
        ensure(n)
        return n

    def mm_end(n, tok):
        mm_tok[n] = tok

    def refill(n):
        while ada_late:
            ada_late.pop(0)()
        ensure(n + HL)

    def mm_T(n, kts, ncols, nt, dst, waits, xh, xl, xk, first=True, last=True, share=False, signal=None):
        slot = n % HL
        w0 = list(waits)
        tok = None
        for k in range(kts):
            wh = whi[slot][:, k * ncols + nt * 128:k * ncols + nt * 128 + 128]
            wl = wlo[slot][:, k * ncols + nt * 128:k * ncols + nt * 128 + 128]
            a, b = xh[:, xk(k), :], xl[:, xk(k), :]
            ww = (w0 if k == 0 else []) + weight_wait(n, k * ncols + nt * 128 + 128) + xwait(xk(k))

            def go(e, wh=wh, wl=wl, a=a, b=b, k=k):
                e.matmul(dst, wh, a, start=first and k == 0, stop=False, skip_group_check=share)
                e.matmul(dst, wh, b, start=False, stop=False, skip_group_check=share)
                return e.matmul(dst, wl, a, start=False, stop=last and k == kts - 1, skip_group_check=share)

            tok = op("tensor", ww, go, signal if k == kts - 1 else None)
        return tok

    def mm_N(n, kts, ncols, c0, nc_, dst, half, waits, xh, xl, xk, signal=None):
        slot = n % HL
        tok = None
        for k in range(kts):
            wh = whi[slot][:, k * ncols + c0:k * ncols + c0 + nc_]
            wl = wlo[slot][:, k * ncols + c0:k * ncols + c0 + nc_]
            a, b = (x[:, xk(k), half * 128:half * 128 + 128] for x in (xh, xl))
            ww = (list(waits) if k == 0 else []) + weight_wait(n, k * ncols + c0 + nc_) + xwait(xk(k))

            def go(e, wh=wh, wl=wl, a=a, b=b, k=k):
                e.matmul(dst, a, wh, start=k == 0, stop=False)
                e.matmul(dst, b, wh, start=False, stop=False)
                return e.matmul(dst, a, wl, start=False, stop=k == kts - 1)

            tok = op("tensor", ww, go, signal if k == kts - 1 else None)
        return tok

    xready = {}

    def xwait(k):
        return xready.get(k, [])

    heads = {"all": [], "scored": 0, "scaled": 0, "turned": 0, "valued": 0}
    post = []

    def new_head(ready, *stages):
        heads["all"].append((ready, stages))

    def middle():
        n, hs = dict(heads), heads["all"]
        if n["valued"] < n["turned"] and hs[n["valued"]][0]():
            hs[n["valued"]][1][3]()
            heads["valued"] += 1
        if post:
            post.pop(0)()
        if n["turned"] < n["scaled"] and n["turned"] - heads["valued"] < 2:
            hs[n["turned"]][1][2]()
            heads["turned"] += 1
        if n["scored"] < len(hs) and n["scored"] - heads["turned"] < 2:
            hs[n["scored"]][1][0]()
            heads["scored"] += 1

    def after():
        if post:
            post.pop(0)()
        if heads["scaled"] < heads["scored"]:
            heads["all"][heads["scaled"]][1][1]()
            heads["scaled"] += 1

    def advance():
        middle()
        after()

    def flush():
        while heads["valued"] < len(heads["all"]) or post:
            advance()

    def arriving(tiles):
        def hook(k):
            advance()
            while k not in tiles:
                advance()
            xready[k] = tiles[k]
        return hook

    def chunk_T(key, x, evac, kts=8, ncols=256, pairs=1, xk=lambda k: k):
        xh, xl = x
        n = mm_begin(key)
        for pr in range(pairs):
            b = gbank()
            fr = list(bank_free[b])
            mm_T(n, kts, ncols, 2 * pr, PS[:, b, 0:T], fr, xh, xl, xk)
            if pr == 0:
                middle()
            tok = mm_T(n, kts, ncols, 2 * pr + 1, PS[:, b, T:2 * T], [], xh, xl, xk, signal="t_mm")
            if pr == pairs - 1:
                mm_end(n, tok)
            evac(pr, b, tok)
        after()
        refill(n)

    def together(keys, x, evacs, hook=None):
        xh, xl = x
        ns = [mm_begin(key) for key in keys]
        bs = [gbank() for _ in keys]
        order = [(0, 0), (0, 1), (1, 0), (1, 1)] + [(k, 2) for k in range(2) if len(keys) > 2]
        order += [(k, c) for k in range(2, 6) for c in range(len(keys))]
        order += [(k, c) for c in range(len(keys)) for k in (6, 7)]
        for k, c in order:
            if hook and c == 0:
                hook(k)
            n, b = ns[c], bs[c]
            slot = n % HL
            for nt in range(2):
                at = k * 256 + nt * 128
                wh, wl = whi[slot][:, at:at + 128], wlo[slot][:, at:at + 128]
                dst = PS[:, b, nt * T:nt * T + T]

                def go(e, wh=wh, wl=wl, dst=dst, k=k, nt=nt):
                    e.matmul(dst, wh, xh[:, k, :], start=k == 0 and nt == 0, stop=False, skip_group_check=True)
                    e.matmul(dst, wh, xl[:, k, :], start=False, stop=False, skip_group_check=True)
                    return e.matmul(dst, wl, xh[:, k, :], start=False, stop=k == 7, skip_group_check=True)

                tok = op("tensor", bank_free[b] + weight_wait(n, at + 128) + xwait(k), go,
                         "t_mm" if k == 7 and nt == 1 else None)
            if k == 7:
                mm_end(n, tok)
        for n, b, evac in zip(ns, bs, evacs):
            evac(0, b, mm_tok[n])
        after()
        for n in ns:
            refill(n)

    sq_free = {i: [] for i in range(4)}
    rb_free = {0: [], 1: []}

    def total(b, c0, parts):
        for i, (tile, waits) in enumerate(parts):
            t = op("tensor", [ones] + list(waits) + (bank_free[b] if i == 0 else []), lambda e, i=i, tile=tile: e.matmul(
                PS[:, b, c0:c0 + T], ONES[:, :], tile, start=i == 0, stop=i == len(parts) - 1), "t_sq")
        return t

    def inverse_rms(b, c0, tok, dim, dst, free=()):
        t = op("scalar", [tok, small] + list(free), lambda e: e.activation(
            dst, PS[:, b, c0:c0 + T], ACT.Sqrt, bias=col("eps"), scale=1.0 / dim), "a_sqrt")
        return t, op("vector", [t], lambda e: e.reciprocal(dst, dst), "v_rec")

    def small_norm(src, nk, dim, waits, r):
        parts = []
        for k in range(nk):
            s = op("scalar", list(waits(k)) + sq_free[k], lambda e, k=k: e.activation(
                SQ[:, k, :], src(k), ACT.Square), "a_sq")
            parts.append((SQ[:, k, :], [s]))

        def finish():
            b = gbank()
            t = total(b, 0, parts)
            for k in range(nk):
                sq_free[k] = [t]
            t, rec = inverse_rms(b, 0, t, dim, RB[:, r, :], rb_free[r])
            bank_free[b] = [t]
            return rec

        return finish

    x_tok = {}
    nrm = {}

    def square_pair(g):
        d = 2 if g == 0 else 0
        fl = lambda x, a: x[:, a:a + 2, :].rearrange("p j t -> p (j t)")
        s = op("scalar", [x_tok[2 * g], x_tok[2 * g + 1]] + sq_free[d] + sq_free[d + 1], lambda e: e.activation(
            fl(SQ, d), fl(X, 2 * g), ACT.Square), "a_sq")
        if g in (1, 2):
            t = op("vector", [s], lambda e: e.tensor_tensor(fl(SQ, 2), fl(SQ, 2), fl(SQ, 0), ALU.add), "v_sq")
            sq_free[0] = sq_free[1] = nrm["acc"] = [t]
        elif g == 3:
            nrm["last"] = [s]

    def total_squares(b, c0):
        t = total(b, c0, [(SQ[:, 2, :], nrm["acc"]), (SQ[:, 3, :], []), (SQ[:, 0, :], nrm["last"]), (SQ[:, 1, :], [])])
        for i in range(4):
            sq_free[i] = [t]
        return t

    def gain_pair(g, gain):
        for k in (2 * g, 2 * g + 1):
            h = op("scalar", [x_tok[k]] + x_free, lambda e, k=k, s=gain(k): e.activation(
                Hh[:, k, :], X[:, k, :], ACT.Identity, scale=s), "a_xhi")
            t = op("vector", [h] + x_free, lambda e, k=k, s=gain(k): e.scalar_tensor_tensor(
                Hl[:, k, :], X[:, k, :], s, f32(Hh[:, k, :]), ALU.mult, ALU.subtract), "v_xlo")
            nready[k] = [h, t]

    nready = {}

    tt_free = {}

    def apply(src, ks, gain, shift, r, rtok, dst, k0=0, waits=lambda k: []):
        dh, dl = dst
        done = None
        steps = []
        for k in ks:
            s = k % 2
            t = op("vector", [rtok] + waits(k) + tt_free.get(s, []), lambda e, k=k, s=s, g=gain(k): e.scalar_tensor_tensor(
                TT[:, s, :], src(k), g, RB[:, r, :], ALU.mult, ALU.mult), "v_nrm")
            rb_free[r] = [t]
            if shift is None:
                h = op("scalar", [t] + x_free, lambda e, k=k, s=s: e.activation(
                    dh[:, k0 + k, :], TT[:, s, :], ACT.Copy), "a_xhi")
            else:
                h = op("scalar", [t] + x_free, lambda e, k=k, s=s: e.activation(
                    dh[:, k0 + k, :], TT[:, s, :], ACT.Identity, bias=shift(k)), "a_xhi")
            steps.append((k, s, h))
            if len(steps) > 1:
                done = low(dh, dl, k0, shift, steps.pop(0))
        return low(dh, dl, k0, shift, steps.pop(0))

    def low(dh, dl, k0, shift, step):
        k, s, h = step
        if shift is None:
            t = op("vector", [h] + x_free, lambda e: e.tensor_tensor(
                dl[:, k0 + k, :], TT[:, s, :], f32(dh[:, k0 + k, :]), ALU.subtract), "v_xlo")
        else:
            t = op("vector", [h] + x_free, lambda e: e.scalar_tensor_tensor(
                dl[:, k0 + k, :], TT[:, s, :], shift(k), f32(dh[:, k0 + k, :]), ALU.add, ALU.subtract), "v_xlo")
        tt_free[s] = [t]
        xready[k0 + k] = [h, t]
        return t

    x_free = []

    def split(dh, dl, src, waits, free=()):
        h = op("scalar", list(waits) + list(free), lambda e: e.activation(dh, src, ACT.Copy), "a_xhi")
        return h, op("vector", [h], lambda e: e.tensor_tensor(dl, src, f32(dh), ALU.subtract), "v_xlo")

    cact = op("scalar", [small], lambda e: e.activation(CA[:, :], col("c", 0, 8), ACT.Silu), "a_c")
    small_t = op("vector", [small], lambda e: e.tensor_tensor(
        GC[:, :], col("norm_final_g", 0, 8), col("attn_norm", 0, 8), ALU.mult), "v_gs")
    ensure(1)
    x_tok.update({k: xin for k in range(8)})
    for g in range(4):
        square_pair(g)
    sb0 = gbank()
    t = total_squares(sb0, 0)
    t, rx = inverse_rms(sb0, 0, t, D, RB[:, 0, :])
    bank_free[sb0] = [t]
    ANG, KR, RR = PTf[:, 0:256], PTf[:, 256:512], PTf[:, 512:768]
    t = op("vector", [pin], lambda e: e.tensor_copy(ANG, posi), "v_rope")
    t = op("vector", [t, small], lambda e: e.tensor_scalar(ANG, ANG, col("invf"), None, ALU.mult), "v_rope")
    tt_free[0] = [t]
    for dst, shift in ((SIN, 0.0), (COS, 0.25)):
        if shift:
            t = op("vector", [t], lambda e: e.tensor_scalar(KR, ANG, 1.0 / TWO_PI, 0.25, ALU.mult, ALU.add), "v_rope")
            t = op("vector", [t], lambda e: e.tensor_scalar(KR, KR, MAGIC, None, ALU.add), "v_rope")
        else:
            t = op("vector", [t], lambda e: e.tensor_scalar(KR, ANG, 1.0 / TWO_PI, MAGIC, ALU.mult, ALU.add), "v_rope")
        t = op("vector", [t], lambda e: e.tensor_scalar(KR, KR, MAGIC, None, ALU.subtract), "v_rope")
        t = op("vector", [t], lambda e: e.scalar_tensor_tensor(RR, KR, -C1, ANG, ALU.mult, ALU.add), "v_rope")
        t = op("vector", [t], lambda e: e.scalar_tensor_tensor(RR, KR, -C2, RR, ALU.mult, ALU.add), "v_rope")
        t = op("vector", [t], lambda e: e.scalar_tensor_tensor(RR, KR, -C3, RR, ALU.mult, ALU.add), "v_rope")
        if shift:
            t = op("vector", [t], lambda e: e.tensor_scalar(RR, RR, math.pi / 2, None, ALU.add), "v_rope")
        t = op("vector", [t], lambda e: e.tensor_scalar(RR, RR, 3.1415925, -3.1415925, ALU.min, ALU.max), "v_rope")
        t = op("scalar", [t], lambda e, dst=dst: e.activation(dst[:, :], RR, ACT.Sin), "a_sin")
    trig = op("vector", [t], lambda e: e.tensor_scalar(SIN[:, :], SIN[:, :], col("sgn"), None, ALU.mult), "v_rope")

    def lam():
        for i in range(2):
            t = op("vector", [lam_in], lambda e, i=i: e.tensor_tensor_reduce(
                PTf[:, 1024 + i * 64:1088 + i * 64], PTf[:, 768 + i * 128:832 + i * 128], PTf[:, 832 + i * 128:896 + i * 128],
                1.0, 0.0, ALU.mult, ALU.add, LM[:, i:i + 1]), "v_lam")
        t = op("scalar", [t], lambda e: e.activation(LM[:, 2:4], LM[:, 0:2], ACT.Exp), "a_lam")
        t = op("vector", [t], lambda e: e.scalar_tensor_tensor(
            LM[:, 4:5], LM[:, 2:3], LAM_INIT, LM[:, 3:4], ALU.add, ALU.subtract), "v_lam")
        w = op("vector", [small], lambda e: e.tensor_scalar(SW[:, :], col("subln"), 1.0 - LAM_INIT, None, ALU.mult), "v_lam")
        return t, w

    lam_tok, sw_tok = lam()
    H = (Hh, Hl)

    def conditioned(k):
        apply(lambda k: X[:, k, :], [k], lambda k: GS[:, k:k + 1], lambda k: ADA[:, k:k + 1], 0, rx, H,
              waits=lambda k: [gs_tok[k]])

    def next_tile(k):
        if k == 0:
            take_next()
            conditioned(0)
        if k < 7:
            take_next()
            conditioned(k + 1)

    rot["banks"] = [0, 1, 2]
    C5 = lambda k: PBf[:, k * T:(k + 1) * T]
    cq_tok = {}

    def ev_c0(pr, b, tok):
        t = op("scalar", [tok], lambda e: e.activation(PBf[:, 0:512], PS[:, b, 0:512], ACT.Copy), "a_ev")
        cq_tok[0] = cq_tok[1] = t
        bank_free[b] = [t]

    def ev_c1(pr, b, tok):
        t = op("scalar", [tok], lambda e: e.activation(PBf[:, 512:768], PS[:, b, 0:256], ACT.Copy), "a_ev")
        cq_tok[2] = t
        z, az, ls = PTf[0:16, 0:256], PTf[0:16, 256:512], PTf[0:16, 512:768]
        fc, rf, on = PTf[0:16, 768:1024], PTf[0:16, 1024:1280], PTf[0:16, 1280:1536]
        cc = lambda name, i=0, n=1: col(name, i, n, 0, 16)
        t = op("vector", [t, trig], lambda e: e.tensor_scalar(z, PS[0:16, b, 256:512], cc("b_forget"), None, ALU.add), "v_f")
        ev_kr(b)
        o1 = op("vector", [], lambda e: e.memset(on, 1.0), "v_f")
        t = op("vector", [t], lambda e: e.scalar_tensor_tensor(az, z, -1.0, z, ALU.mult, ALU.max), "v_f")
        t = op("scalar", [t], lambda e: e.activation(az, az, ACT.Exp, scale=-1.0), "a_f")
        t = op("scalar", [t], lambda e: e.activation(az, az, ACT.Ln, bias=1.0), "a_f")
        t = op("vector", [t], lambda e: e.scalar_tensor_tensor(ls, z, 0.0, az, ALU.min, ALU.subtract), "v_f")
        t = op("vector", [t, o1], lambda e: e.tensor_tensor_scan(fc, on, ls, 0.0, ALU.mult, ALU.add), "v_f")
        for h in range(8):
            q = op("vector", [t], lambda e, h=h: e.tensor_scalar(
                QF[64:80, h, :], fc, cc("m1", h), cc("m2", h), ALU.mult, ALU.add), "v_fq")
        t = op("vector", [t], lambda e: e.tensor_scalar(rf, fc, cc("m3"), cc("m4"), ALU.mult, ALU.add), "v_f")
        k_ = op("scalar", [t], lambda e: e.activation(
            KF[64:80, :, :], rf.unsqueeze(1).to_broadcast([16, 8, T]), ACT.Copy), "a_f")
        aug[:] = [q, k_]

    aug = []

    def ev_c2(pr, b, tok):
        t = op("scalar", [tok], lambda e: e.activation(PBf[:, 768:1280], PS[:, b, 0:512], ACT.Copy), "a_ev")
        cq_tok[3] = cq_tok[4] = t
        bank_free[b] = [t]

    km_tok = []

    def ev_kr(b):
        a, c = TT[64:96, 0, :], TT[64:96, 1, :]
        t1 = op("vector", tt_free.get(0, []) + tt_free.get(1, []), lambda e: e.tensor_tensor(
            a, PS[64:96, b, 256:512], COS[64:96, :], ALU.mult), "v_kr")
        t2 = op("vector", [], lambda e: e.tensor_tensor(c, PS[96:128, b, 256:512], SIN[96:128, :], ALU.mult), "v_kr")
        bank_free[b] = [t2]
        t = op("vector", [t2], lambda e: e.tensor_tensor(a, a, c, ALU.add), "v_kr")
        t = op("scalar", [t], lambda e: e.activation(
            KM[64:96, :, :], a.unsqueeze(1).to_broadcast([32, 8, T]), ACT.Copy), "a_kr")
        tt_free[0] = tt_free[1] = [t]
        km_tok.append(t)

    def heads_out(dst, h0, toks):
        def ev(b, tok):
            bank = PS[:, b, :].rearrange("p (j t) -> p j t", j=2)
            op("scalar", [tok], lambda e: e.activation(dst[0:64, h0:h0 + 4:2, :], bank[0:64], ACT.Copy), None)
            t = op("scalar", [], lambda e: e.activation(dst[0:64, h0 + 1:h0 + 4:2, :], bank[64:128], ACT.Copy), "a_ev")
            toks.append(t)
            bank_free[b] = [t]
        return ev

    kf_tok, qf_tok, vf_tok, qm_tok, vm_tok = [], [], [], [], []
    VF, VM = V[:, :, 512:1024], V[:, :, 0:512]

    def chunk_N(key, x, evac):
        n = mm_begin(key)
        b = gbank()
        mm_N(n, 8, 256, 0, 256, PS[:, b, 0:256], 0, list(bank_free[b]), x[0], x[1], lambda k: k)
        middle()
        tok = mm_N(n, 8, 256, 0, 256, PS[:, b, 256:512], 1, [], x[0], x[1], lambda k: k, signal="t_mm")
        mm_end(n, tok)
        evac(b, tok)
        after()
        refill(n)

    def v_out(dst, toks):
        def ev(b, tok):
            t = op("scalar", [tok], lambda e: e.activation(
                dst, PS[:, b, :].rearrange("p (h n) -> p h n", h=2), ACT.Copy), "a_ev")
            bank_free[b] = [t]
            toks.append(t)
        return ev

    together([("in", 0), ("in", 1)], H, [ev_c0, ev_c1], next_tile)
    q_norm = small_norm(C5, 3, 384, lambda k: [cq_tok[k]], 1)
    chunk_T(("in", 2), H, ev_c2)
    xr = dict(xready)
    xready.clear()
    rq = q_norm()
    apply(C5, range(3), lambda k: col("q_norm_g", k), None, 1, rq, (Oh, Ol), 0)
    cn = dict(xready)
    xready.clear()
    xready.update(xr)
    kv_norm = small_norm(lambda k: C5(3 + k), 2, 256, lambda k: [cq_tok[3 + k]], 0)
    chunk_T(("in", 3), H, lambda pr, b, tok: heads_out(KF, 0, kf_tok)(b, tok))
    xready.clear()
    rk = kv_norm()
    apply(lambda k: C5(3 + k), range(2), lambda k: col("kv_norm_g", k), None, 0, rk, (Oh, Ol), 3)
    cn.update(xready)
    xready.clear()
    xready.update(xr)
    chunk_T(("in", 4), H, lambda pr, b, tok: heads_out(KF, 4, kf_tok)(b, tok))
    for j in range(2):
        chunk_T(("in", 5 + j), H, lambda pr, b, tok, j=j: heads_out(QF, 4 * j, qf_tok)(b, tok))
    for j in range(2):
        chunk_N(("in", 7 + j), H, v_out(VF[:, :, 256 * j:256 * j + 256], vf_tok))

    def ev_uq(j):
        def ev(pr, b, tok):
            h0 = 4 * j + 2 * pr
            bank = PS[:, b, :].rearrange("p (j t) -> p j t", j=2)
            c = op("scalar", [tok], lambda e: e.activation(QM[0:64, h0:h0 + 2, :], bank[0:64], ACT.Copy), "a_ev")
            s1 = TT[64:96, :, :]
            s2 = SQ[64:96, 0:2, :]
            bc = lambda ap: ap.unsqueeze(1).to_broadcast([32, 2, T])
            op("vector", [c, trig] + tt_free.get(0, []) + tt_free.get(1, []) + sq_free.get(0, []) + sq_free.get(1, []),
               lambda e: e.tensor_tensor(s1, bank[64:96], bc(COS[64:96, :]), ALU.mult), None)
            t = op("vector", [], lambda e: e.tensor_tensor(s2, bank[96:128], bc(SIN[96:128, :]), ALU.mult), "v_qr")
            bank_free[b] = [t]
            t = op("vector", [t], lambda e: e.tensor_tensor(QM[64:96, h0:h0 + 2, :], s1, s2, ALU.add), "v_qr")
            tt_free[0] = tt_free[1] = sq_free[0] = sq_free[1] = [t]
            qm_tok.append([c, t])
        return ev

    pb_free, pt_free = {}, {}
    s_free, t_free = ({b: [gs_tok[b]] for b in banks} for banks in ((4, 5), (6, 7)))
    a_tok, b_tok = {}, {}

    def scores(heads):
        st_, vt_ = {}, {}
        for slot, q, k, waits, bias, scale in heads:
            b = 4 + slot % 2
            op("tensor", list(waits) + s_free.get(b, []), lambda e, b=b, q=q, k=k: e.matmul(
                PS[:, b, 0:128], q[:, 0:128], k[:, 0:128], start=True, stop=True), None)
            st_[slot] = op("tensor", [], lambda e, b=b, q=q, k=k: e.matmul(
                PS[:, b, 128:384], q[:, 128:256], k[:, 0:256], start=True, stop=True), "t_s")
        for slot, q, k, waits, bias, scale in heads:
            b = 4 + slot % 2
            op("vector", [st_[slot], mt] + list(waits) + pb_free.get(slot, []),
               lambda e, b=b, slot=slot, bias=bias, scale=scale: e.tensor_tensor_reduce(
                PB[:, slot, 0:128], PS[:, b, 0:128], bias[:, 128:256], -scale, BIG, ALU.add, ALU.min,
                NM[:, 2 * slot:2 * slot + 1]), None)
            vt_[slot] = op("vector", [], lambda e, b=b, slot=slot, bias=bias, scale=scale: e.tensor_tensor_reduce(
                PB[:, slot, 128:384], PS[:, b, 128:384], bias, -scale, BIG, ALU.add, ALU.min,
                NM[:, 2 * slot + 1:2 * slot + 2]), "v_s")
            s_free[b] = [vt_[slot]]
        for slot, *_ in heads:
            op("scalar", [vt_[slot]], lambda e, slot=slot: e.activation(
                PB[:, slot, 0:128], PB[:, slot, 0:128], ACT.Exp, scale=-1.0, bias=NM[:, 2 * slot:2 * slot + 1],
                accum_out=RS[:, 2 * slot:2 * slot + 1]), None)
            a_tok[slot] = op("scalar", [], lambda e, slot=slot: e.activation(
                PB[:, slot, 128:384], PB[:, slot, 128:384], ACT.Exp, scale=-1.0,
                bias=NM[:, 2 * slot + 1:2 * slot + 2], accum_out=RS[:, 2 * slot + 1:2 * slot + 2]), "a_exp")

    def inverse(slots):
        lo, hi = 2 * slots[0], 2 * slots[-1] + 2
        return op("vector", [a_tok[s] for s in slots], lambda e: e.reciprocal(RS[:, lo:hi], RS[:, lo:hi]), "v_rs")

    def scale_rows(slots):
        r = inverse(slots)
        for slot in slots:
            op("vector", [r], lambda e, slot=slot: e.tensor_scalar(
                PB[:, slot, 0:128], PB[:, slot, 0:128], RS[:, 2 * slot:2 * slot + 1], None, ALU.mult), None)
            a_tok[slot] = op("vector", [], lambda e, slot=slot: e.tensor_scalar(
                PB[:, slot, 128:384], PB[:, slot, 128:384], RS[:, 2 * slot + 1:2 * slot + 2], None, ALU.mult), "v_p")

    def turn(slot):
        b = 6 + slot % 2
        for j in range(3):
            t = op("tensor", [a_tok[slot], mk] + t_free.get(b, []), lambda e, j=j: e.transpose(
                PS[:, b, j * 128:j * 128 + 128], PB[:, slot, j * 128:j * 128 + 128], ID[:, :]),
                "t_t" if j == 2 else None)
        pb_free[slot] = [t]
        t = op("scalar", [t] + pt_free.get(slot, []), lambda e: e.activation(
            PT[:, slot, :], PS[:, b, 0:384], ACT.Copy), "a_t")
        t_free[b] = [t]
        b_tok[slot] = t

    def values(slot, v, dst, waits):
        op("tensor", [b_tok[slot]] + list(waits), lambda e: e.matmul(
            dst[:, 0:256], v(0), PT[:, slot, 0:256], start=True, stop=False), None)
        t = op("tensor", [], lambda e: e.matmul(
            dst[:, 128:256], v(1), PT[:, slot, 256:384], start=False, stop=True), "t_o")
        pt_free[slot] = [t]
        return t

    OB = 3
    otok = {}

    def pair_values(slots, v, tile, oh_free=()):
        for i, s in enumerate(slots):
            t = values(s, v[i][0], PS[64 * i:64 * i + 64, OB, 0:256], list(v[i][1]) + bank_free[OB])
        h, lo = split(Oh[:, tile, :], Ol[:, tile, :], PS[:, OB, 0:256], [t], oh_free)
        bank_free[OB] = [lo]
        otok[tile] = [h, lo]

    def head_pair(i, qs, ks, vs, tile, bias, scale, waits, oh_free=lambda: [], ready=lambda: True):
        slots = [2 * (i % 2), 2 * (i % 2) + 1]
        new_head(
            ready,
            lambda: scores([(s, q, k, waits(), bias(j), scale) for j, (s, q, k) in enumerate(zip(slots, qs, ks))]),
            lambda: scale_rows(slots),
            lambda: [turn(s) for s in slots],
            lambda: pair_values(slots, vs(), tile, oh_free()),
        )

    def fox_pair(i):
        h = 2 * i
        head_pair(
            i, [QF[0:80, h + j, :] for j in range(2)], [KF[0:80, h + j, :] for j in range(2)],
            lambda: [((lambda kb, j=j: VF[:, kb, (h + j) * 64:(h + j + 1) * 64]), [vf_tok[h // 4]]) for j in range(2)],
            4 + i, lambda j: TRI[:, :], SCALE64, lambda: [kf_tok[h // 4], qf_tok[h // 4]] + aug,
            oh_free=lambda: [mm_tok[chunk_no[("ukv", 0)]]], ready=lambda: chunk_no[("ukv", 0)] in mm_tok)

    def mla_pair(i):
        h = 2 * i
        head_pair(
            i, [QM[0:96, h + j, :] for j in range(2)], [KM[0:96, h + j, :] for j in range(2)],
            lambda: [((lambda kb, j=j: VM[:, kb, (h + j) * 64:(h + j + 1) * 64]), vm_tok) for j in range(2)],
            i, lambda j: TRI[:, :], MLA_SCALE, lambda: qm_tok[h // 2] + km_tok,
            oh_free=lambda: [mm_tok[chunk_no[("ukv", 0)]]], ready=lambda: chunk_no[("ukv", 0)] in mm_tok)

    xready.clear()
    xready.update(cn)
    for i in range(4):
        fox_pair(i)
    for j in range(2):
        chunk_T(("uq", j), (Oh, Ol), ev_uq(j), kts=3, ncols=512, pairs=2)

    def ukv():
        n = mm_begin(("ukv", 0))
        for pr in range(2):
            b = gbank()
            mm_T(n, 2, 1024, 2 * pr, PS[:, b, 0:T], list(bank_free[b]), Oh, Ol, lambda k: 3 + k)
            tok = mm_T(n, 2, 1024, 2 * pr + 1, PS[:, b, T:2 * T], [], Oh, Ol, lambda k: 3 + k, signal="t_mm")
            heads_out(KM, 4 * pr, km_tok)(b, tok)
        middle()
        for half in range(2):
            b = gbank()
            tok = mm_N(n, 2, 1024, 512, 512, PS[:, b, :], half, list(bank_free[b]), Oh, Ol, lambda k: 3 + k, signal="t_mm")
            t = op("scalar", [tok], lambda e, b=b, half=half: e.activation(VM[:, half, :], PS[:, b, :], ACT.Copy), "a_ev")
            bank_free[b] = [t]
            vm_tok.append(t)
        mm_end(n, tok)
        after()
        refill(n)

    ukv()
    xready.clear()
    xready.update(xr)
    for i in range(4):
        mla_pair(i)

    ga_tok = []

    def ev_gate(g):
        def ev(pr, b, tok):
            t = op("scalar", [tok], lambda e: e.activation(
                GA[:, 2 * g:2 * g + 2, :].rearrange("p j t -> p (j t)"), PS[:, b, :], ACT.Copy), "a_ev")
            bank_free[b] = [t]
            ga_tok.append(t)
        return ev

    for g in range(8):
        chunk_T(("in", 9 + g), H, ev_gate(g))
    h_used = mm_tok[chunk_no[("in", 16)]]
    flush()
    for tile in range(8):
        xready[tile] = otok[tile]

    yready = {}

    def step_o(i):
        n = mm_begin(("o", i))
        gm, gf = (GA[:, a + 2 * i:a + 2 * i + 2, :].rearrange("p j t -> p (j t)") for a in (0, 8))
        sg = op("scalar", ga_tok, lambda e: e.activation(gm, gm, ACT.Sigmoid), "a_sg")
        sg = op("scalar", [], lambda e: e.activation(gf, gf, ACT.Sigmoid), "a_sg")
        bs, toks = [], []
        for part in (1, 0):
            b = gbank()
            bs.append(b)
            slot = n % HL
            for nt in range(2):
                for k in range(4):
                    kk = 4 * part + k
                    at = kk * 256 + nt * 128
                    wh, wl = whi[slot][:, at:at + 128], wlo[slot][:, at:at + 128]
                    dst = PS[:, b, nt * T:nt * T + T]

                    def go(e, wh=wh, wl=wl, kk=kk, dst=dst, k=k):
                        e.matmul(dst, wh, Oh[:, kk, :], start=k == 0, stop=False)
                        e.matmul(dst, wh, Ol[:, kk, :], start=False, stop=False)
                        return e.matmul(dst, wl, Oh[:, kk, :], start=False, stop=k == 3)

                    tok = op("tensor", bank_free[b] + weight_wait(n, at + 128) + xwait(kk), go,
                             "t_mm" if nt == 1 and k == 3 else None)
            toks.append(tok)
        mm_end(n, tok)
        t = op("vector", [toks[0], sg], lambda e: e.tensor_tensor(gf, PS[:, bs[0], :], gf, ALU.mult), "v_y")
        bank_free[bs[0]] = [t]
        t = op("vector", [toks[1]], lambda e: e.tensor_tensor(gm, PS[:, bs[1], :], gm, ALU.mult), "v_y")
        bank_free[bs[1]] = [t]
        t = op("vector", [t], lambda e: e.tensor_tensor(gm, gm, gf, ALU.add), "v_y")
        fl = lambda x: x[:, 2 * i:2 * i + 2, :].rearrange("p j t -> p (j t)")
        h, lo = split(fl(Hh), fl(Hl), gm, [t], [h_used])
        yready[2 * i] = yready[2 * i + 1] = [h, lo]
        refill(n)
        return t

    rot["banks"] = [0, 1, 2, 3]
    for i in range(4):
        ga_done = step_o(i)
    o_used = mm_tok[chunk_no[("o", 3)]]
    xready.clear()
    xready.update(yready)

    def ev_res(i, gate, gtok):
        def ev(pr, b, tok):
            for j in range(2):
                k = 2 * i + j
                t = op("vector", [tok, x_tok[k]] + gtok, lambda e, k=k, j=j: e.scalar_tensor_tensor(
                    X[:, k, :], PS[:, b, j * T:j * T + T], gate(k), X[:, k, :], ALU.mult, ALU.add), "v_x")
                x_tok[k] = t
            bank_free[b] = [t]
        return ev

    def ev_add(i):
        def ev(pr, b, tok):
            fl = X[:, 2 * i:2 * i + 2, :].rearrange("p j t -> p (j t)")
            t = op("vector", [tok, x_tok[2 * i], x_tok[2 * i + 1]], lambda e: e.tensor_tensor(
                fl, PS[:, b, :], fl, ALU.add), "v_x")
            x_tok[2 * i] = x_tok[2 * i + 1] = t
            bank_free[b] = [t]
        return ev

    def ev_out(i):
        def ev(pr, b, tok):
            ev_res(i, lambda k: ADA[:, 16 + k:17 + k], [ada_acc[2]])(pr, b, tok)
            square_pair(i)
        return ev

    for i in range(3):
        chunk_T(("out", i), H, ev_out(i))
    n = mm_begin(("out", 3))
    gs_ffn = op("vector", [ada_acc[4], small], lambda e: e.scalar_tensor_tensor(
        GS[:, 8:16], ADA[:, 32:40], 1.0, col("norm_ffn_g", 0, 8), ALU.add, ALU.mult), "v_gs")

    def ffn_norm(pr, b, tok):
        ev_out(3)(pr, b, tok)
        x_free[:] = [mm_tok[n]]
        xready.clear()
        sbank = gbank()
        t = total_squares(sbank, 0)
        t, r = inverse_rms(sbank, 0, t, D, RB[:, 0, :], rb_free[0])
        bank_free[sbank] = [t]
        apply(lambda k: X[:, k, :], range(8), lambda k: GS[:, 8 + k:9 + k], lambda k: ADA[:, 24 + k:25 + k], 0, r, H,
              waits=lambda k: [gs_ffn, ada_acc[3]])
        x_free[:] = []

    chunk_T(("out", 3), H, ffn_norm)

    wk_free = {}
    hid = {}
    hid_free = {s: [o_used] for s in range(8)}
    UC = lambda s: PBf[:, s * 512:(s + 1) * 512]

    def up_one(j):
        s = j % 3
        st1 = {}

        def ev(pr, b, tok):
            for i, tile in enumerate((j, 22 + j)):
                t = op("scalar", [tok] + wk_free.get(s, []), lambda e, i=i, tile=tile: e.activation(
                    UC(s)[:, i * T:i * T + T], PS[:, b, i * T:i * T + T], ACT.Identity,
                    bias=col("conv_b", tile), scale=col("conv_w", 88 + tile)), "a_u")
            for tap, sh in ((1, 1), (0, 2)):
                for i, tile in enumerate((j, 22 + j)):
                    u = UC(s)[:, i * T + sh:i * T + T]
                    t = op("vector", [t] if i == 0 else [], lambda e, i=i, u=u, tile=tile, tap=tap, sh=sh: e.scalar_tensor_tensor(
                        u, PS[:, b, i * T:i * T + T - sh], col("conv_w", tap * 44 + tile), u, ALU.mult, ALU.add), "v_u")
            bank_free[b] = [t]
            st1["t"] = t

        def late():
            g, m = PTf[:, (j % 2) * 512:(j % 2) * 512 + 256], PTf[:, (j % 2) * 512 + 256:(j % 2) * 512 + 512]
            t = op("scalar", [st1["t"]] + wk_free.get(("m", j % 2), []), lambda e: e.activation(g, UC(s)[:, 0:T], ACT.Silu), "a_u2")
            t = op("vector", [t], lambda e: e.tensor_tensor(m, g, UC(s)[:, T:2 * T], ALU.mult), "v_u2")
            wk_free[s] = [t]
            h, lo = split(Oh[:, j % 8, :], Ol[:, j % 8, :], m, [t], hid_free.get(j % 8, []))
            wk_free[("m", j % 2)] = [lo]
            hid[j] = [h, lo]

        return ev, late

    def down(key, i, n_pairs, last_one=False):
        n = mm_begin(key)
        slot = n % HL
        done = {}
        for nt in range(8):
            b = 4 + nt // 2
            dst = PS[:, b, (nt % 2) * T:(nt % 2) * T + T]
            for k in range(2):
                tile = (2 * i + k) % 8
                wh, wl = (w[slot][:, k * 1024 + nt * 128:k * 1024 + nt * 128 + 128] for w in (whi, wlo))
                start = i == 0 and k == 0 and nt % 2 == 0
                stop = i == n_pairs - 1 and k == 1

                def go(e, dst=dst, wh=wh, wl=wl, tile=tile, start=start, stop=stop):
                    e.matmul(dst, wh, Oh[:, tile, :], start=start, stop=False, skip_group_check=True)
                    e.matmul(dst, wh, Ol[:, tile, :], start=False, stop=False, skip_group_check=True)
                    return e.matmul(dst, wl, Oh[:, tile, :], start=False, stop=stop, skip_group_check=True)

                last = nt == 7 and k == 1
                sig = "t_mm" if last or (i == n_pairs - 1 and nt % 2 == 1 and k == 1) else None
                fr = bank_free[b] + s_free.get(b, []) + t_free.get(b, []) if i == 0 else []
                tok = op("tensor", weight_wait(n, k * 1024 + nt * 128 + 128) + hid[2 * i + k] + fr, go, sig)
            if nt % 2 == 1:
                done[nt // 2] = tok
        mm_end(n, tok)
        for k in range(2):
            hid_free[(2 * i + k) % 8] = [tok]
        if last_one:
            return n, done
        refill(n)

    late = []

    def then(ev):
        def go(pr, b, tok):
            ev(pr, b, tok)
            if late:
                late.pop(0)()
        return go

    for i in range(11):
        (e0, l0), (e1, l1) = up_one(2 * i), up_one(2 * i + 1)
        if i == 0:
            together([("up", 0), ("up", 1)], H, [e0, e1])
            l0()
            late.append(l1)
        else:
            chunk_T(("up", 2 * i), H, then(e0))
            late.append(l0)
            chunk_T(("up", 2 * i + 1), H, then(e1))
            late.append(l1)
            down(("down", i - 1), i - 1, 11)
    late.pop(0)()
    xready.clear()
    x_free[:] = [mm_tok[chunk_no[("up", 21)]]]
    n, done = down(("down", 10), 10, 11, True)

    sq2 = PTf[:, 1024:1536]
    sum2 = PBf[:, 512:1024]
    s2 = {"acc": wk_free[1]}
    for i in range(4):
        ev_res(i, lambda k: ADA[:, 40 + k:41 + k], [ada_acc[5]])(0, 4 + i, done[i])
        gain_pair(i, lambda k: GC[:, k:k + 1])
        square_pair(i)
        for j in range(2):
            d = sum2 if i == 0 else sq2
            t = op("scalar", [x_tok[2 * i + j]] + s2["acc"], lambda e, i=i, j=j, d=d: e.activation(
                d[:, j * T:j * T + T], X[:, 2 * i + j, :], ACT.Square, scale=col("norm_final_g", 2 * i + j)), "a_sq")
        if i:
            t = op("vector", [t], lambda e: e.tensor_tensor(sum2, sum2, sq2, ALU.add), "v_sq")
            s2["acc"] = [t]
        else:
            s2["acc"] = [t]
    refill(n)

    def both_norms():
        b = OB
        total_squares(b, 0)
        t2 = total(b, T, [(sum2[:, 0:T], s2["acc"]), (sum2[:, T:2 * T], [])])
        r1, r2 = RB[:, 1, :], RB[:, 0, :]
        _, t = inverse_rms(b, 0, t2, D, r1, rb_free[1])
        t = op("vector", [t] + rb_free[0], lambda e: e.scalar_tensor_tensor(
            r2, PS[:, b, T:2 * T], 1.0 / D, r1, ALU.mult, ALU.mult), "v_r")
        bank_free[b] = [t]
        t = op("vector", [t], lambda e: e.tensor_tensor(r2, r2, r1, ALU.mult), "v_r")
        t = op("scalar", [t, small], lambda e: e.activation(r2, r2, ACT.Sqrt, bias=col("eps")), "a_sqrt")
        t = op("vector", [t], lambda e: e.reciprocal(r2, r2), "v_rec")
        nrm["r"] = op("vector", [t], lambda e: e.tensor_tensor(r2, r2, r1, ALU.mult), "v_r")

    def residual(k):
        t = op("vector", [nrm["r"]], lambda e: e.scalar_tensor_tensor(
            X[:, k, :], X[:, k, :], col("norm_final_g", k), RB[:, 1, :], ALU.mult, ALU.mult), "v_x")
        x_tok[k] = t

    ga_free = [ga_done]
    qk_free, v_free = [], []
    fin = None

    def one_norm():
        b = OB
        t = total_squares(b, 0)
        t, nrm["r"] = inverse_rms(b, 0, t, D, RB[:, 0, :], rb_free[0])
        bank_free[b] = [t]

    def row_factors():
        b = OB
        for half in range(2):
            t = op("tensor", [nrm["r"], mk] + bank_free[b], lambda e, half=half: e.matmul(
                PS[:, b, half:half + 1], RB[:, 0, half * 128:half * 128 + 128], ID[:, 0:1], start=True, stop=True), "t_row")
        nrm["st"] = op("vector", [t], lambda e: e.tensor_copy(ST[:, :], PS[:, b, 0:2]), "v_row")
        bank_free[b] = [nrm["st"]]

    def ev_qk(dst, toks, j):
        def ev(pr, b, tok):
            t = op("vector", [tok, nrm["r"]], lambda e: e.tensor_tensor(
                dst[:, 2 * j:2 * j + 2, :], PS[:, b, :].rearrange("p (j t) -> p j t", j=2),
                RB[:, 0, :].unsqueeze(1).to_broadcast([128, 2, T]), ALU.mult), "v_qk")
            bank_free[b] = rb_free[0] = [t]
            toks.append(t)
        return ev

    def ev_v(j, toks):
        def ev(b, tok):
            for half in range(2):
                t = op("scalar", [tok, nrm["st"]], lambda e, half=half: e.activation(
                    V[:, half, 256 * j:256 * j + 256], PS[:, b, half * 256:half * 256 + 256], ACT.Copy,
                    scale=ST[:, half:half + 1]), "a_ev")
            bank_free[b] = [t]
            toks.append(t)
        return ev

    for layer in range(2):
        al = alibi8 if layer == 0 else alibi16
        nh = 8 * (layer + 1)
        al_tok = op("sync", ga_free, lambda e, al=al, nh=nh: e.dma_start(GA[:, 0:nh, :], al), "d_al", 16)
        x_free[:] = []
        xready.clear()
        xready.update(nready)
        rot["banks"] = [0, 1, 2]
        qt, kt_, vt = [], [], []
        otok.clear()
        heads.update(all=[], scored=0, scaled=0, turned=0, valued=0)
        o_free = [hid_free[s][0] for s in range(8)]

        def diff_head(h):
            s0, s1 = slots = [2 * (h % 2), 2 * (h % 2) + 1]

            def scale():
                r = inverse(slots)
                for c0, c1, j in ((0, 128, 0), (128, 384, 1)):
                    t = op("vector", [r, lam_tok], lambda e, c0=c0, c1=c1, j=j: e.tensor_scalar(
                        PB[:, s1, c0:c1], PB[:, s1, c0:c1], RS[:, 2 * s1 + j:2 * s1 + j + 1], LM[:, 4:5],
                        ALU.mult, ALU.mult), "v_p")
                for c0, c1, j in ((0, 128, 0), (128, 384, 1)):
                    t = op("vector", [t], lambda e, c0=c0, c1=c1, j=j: e.scalar_tensor_tensor(
                        PB[:, s0, c0:c1], PB[:, s0, c0:c1], RS[:, 2 * s0 + j:2 * s0 + j + 1], PB[:, s1, c0:c1],
                        ALU.mult, ALU.subtract), "v_a")
                a_tok[s0] = t
                pb_free[s1] = [t]

            def values_out():
                t = values(s0, lambda kb: V[:, kb, h * 128:h * 128 + 128], PS[:, OB, 0:256],
                           [vt[h // 2]] + bank_free[OB])
                t = op("scalar", [t], lambda e: e.activation(QF[:, h, :], PS[:, OB, 0:256], ACT.Copy), "a_ev")
                bank_free[OB] = [t]
                od_tok[h] = t
                if h % 2 == 1:
                    post.extend(subln(h // 2))

            new_head(
                lambda: len(vt) > h // 2,
                lambda: scores([(s, QM[64 * m:64 * m + 64, h, :], KM[64 * m:64 * m + 64, h, :],
                                 [qt[h // 2], kt_[h // 2], al_tok], GA[:, h, :], SCALE64)
                                for m, s in enumerate(slots)]),
                scale,
                lambda: turn(s0),
                values_out,
            )

        od_tok = {}

        def subln(g):
            b = 7
            tk = {}
            fl = lambda x, a: x[:, a:a + 2, :].rearrange("p j t -> p (j t)")

            def squares():
                tk["sq"] = op("scalar", [od_tok[2 * g], od_tok[2 * g + 1]] + sq_free[0] + sq_free[1], lambda e: e.activation(
                    fl(SQ, 0), fl(QF, 2 * g), ACT.Square), "a_sq")

            def sums():
                t = op("tensor", [tk["sq"]] + t_free.get(b, []) + bank_free[b], lambda e: e.matmul(
                    PS[:, b, :], ONES[:, :], fl(SQ, 0), start=True, stop=True), "t_sq")
                t = op("scalar", [t, small], lambda e: e.activation(
                    fl(SQ, 0), PS[:, b, :], ACT.Sqrt, bias=col("eps"), scale=1.0 / 128), "a_sqrt")
                bank_free[b] = [t]
                tk["r"] = op("vector", [t], lambda e: e.reciprocal(fl(SQ, 0), fl(SQ, 0)), "v_rec")

            def finish():
                t = op("vector", [tk["r"], sw_tok] + tt_free.get(0, []) + tt_free.get(1, []), lambda e: e.scalar_tensor_tensor(
                    fl(TT, 0), fl(QF, 2 * g), SW[:, 0:1], fl(SQ, 0), ALU.mult, ALU.mult), "v_nrm")
                sq_free[0] = sq_free[1] = [t]
                hh, lo = split(fl(Oh, 2 * g), fl(Ol, 2 * g), fl(TT, 0), [t], o_free)
                tt_free[0] = tt_free[1] = [lo]
                otok[2 * g] = otok[2 * g + 1] = [hh, lo]

            return [squares, sums, finish]

        def moba_pair(i):
            h = 2 * i
            head_pair(
                i, [QM[64 * j:64 * j + 64, i, :] for j in range(2)], [KM[64 * j:64 * j + 64, i, :] for j in range(2)],
                lambda: [((lambda kb, j=j: V[:, kb, (h + j) * 64:(h + j + 1) * 64]), [vt[h // 4]]) for j in range(2)],
                i, lambda j: GA[:, h + j, :], SCALE64, lambda: [qt[i // 2], kt_[i // 2], al_tok],
                oh_free=lambda: o_free, ready=lambda: len(vt) > i // 2)

        def at_five(k):
            if k == 5:
                both_norms() if layer == 0 else one_norm()

        together([(f"qkv{layer}", 0), (f"qkv{layer}", 4)], H, [ev_qk(QM, qt, 0), ev_qk(KM, kt_, 0)], at_five)
        row_factors()
        one_head = diff_head if layer == 0 else moba_pair
        one_head(0)
        one_head(1)
        for i, c in enumerate(QKV_ORDER[2:]):
            if layer == 0 and i in (6, 7, 8, 9):
                residual(2 * i - 12)
                residual(2 * i - 11)
            if c < 4:
                chunk_T((f"qkv{layer}", c), H, ev_qk(QM, qt, c))
            elif c < 8:
                chunk_T((f"qkv{layer}", c), H, ev_qk(KM, kt_, c - 4))
                one_head(2 * (c - 4))
                one_head(2 * (c - 4) + 1)
            else:
                chunk_N((f"qkv{layer}", c), H, ev_v(c - 8, vt))
        xready.clear()
        while 0 not in otok:
            advance()
        xready[0] = otok[0]
        h_used = mm_tok[chunk_no[(f"qkv{layer}", 11)]]
        x_free[:] = [h_used]

        def ev_norm(i):
            def ev(pr, b, tok):
                ev_add(i)(pr, b, tok)
                gain_pair(i, lambda k: col("mlp_norm", layer * 8 + k))
                square_pair(i)
            return ev

        together([(f"out{layer}", i) for i in range(3)], (Oh, Ol), [ev_norm(i) for i in range(3)], arriving(otok))
        flush()
        ga_free = [("v_s", P.counts["v_s"])]
        rot["banks"] = [0, 1, 2, 3]
        chunk_T((f"out{layer}", 3), (Oh, Ol), ev_norm(3))
        o_used = mm_tok[chunk_no[(f"out{layer}", 3)]]
        x_free[:] = []
        xready.clear()
        xready.update(nready)
        for s in range(8):
            hid_free[s] = [o_used]
        hid.clear()
        wk_free.clear()

        def mlp_one(i):
            s = i % 2
            st1 = {}
            r, m = PBf[:, s * 512:s * 512 + 512], PTf[:, s * 512:s * 512 + 512]

            def ev(pr, b, tok):
                t = op("vector", [tok, nrm["r"]] + wk_free.get(("r", s), []), lambda e: e.scalar_tensor_tensor(
                    r.rearrange("p (j t) -> p j t", j=2), PS[:, b, :].rearrange("p (j t) -> p j t", j=2), 0.0,
                    RB[:, 0, :].unsqueeze(1).to_broadcast([128, 2, T]), ALU.max, ALU.mult), "v_u")
                bank_free[b] = rb_free[0] = [t]
                st1["t"] = t

            def late():
                a = (2 * i) % 8
                fl = lambda x: x[:, a:a + 2, :].rearrange("p j t -> p (j t)")
                t = op("scalar", [st1["t"]] + wk_free.get(("m", s), []), lambda e: e.activation(m, r, ACT.Square), "a_u")
                wk_free[("r", s)] = [t]
                h, lo = split(fl(Oh), fl(Ol), m, [t], hid_free[a])
                wk_free[("m", s)] = [lo]
                hid[2 * i] = hid[2 * i + 1] = [h, lo]

            return ev, late

        def at_five(k):
            if k == 5:
                b = gbank()
                t = total_squares(b, 0)
                t, nrm["r"] = inverse_rms(b, 0, t, D, RB[:, 0, :], rb_free[0])
                bank_free[b] = [t]

        (e0, l0), (e1, l1) = mlp_one(0), mlp_one(1)
        together([(f"ff1{layer}", 0), (f"ff1{layer}", 1)], H, [e0, e1], at_five)
        l0()
        late.append(l1)
        for i in range(2, 16):
            ev, lt = mlp_one(i)
            chunk_T((f"ff1{layer}", i), H, then(ev))
            late.append(lt)
            if i >= 2:
                down((f"ff2{layer}", i - 2), i - 2, 16)
        late.pop(0)()
        down((f"ff2{layer}", 14), 14, 16)
        x_free[:] = [mm_tok[chunk_no[(f"ff1{layer}", 15)]]]
        n, done = down((f"ff2{layer}", 15), 15, 16, True)
        for i in range(4):
            ev_add(i)(0, 4 + i, done[i])
            if layer == 0:
                gain_pair(i, lambda k: col("attn_norm", 8 + k))
            square_pair(i)
        if layer == 0:
            refill(n)

    b = gbank()
    t = total_squares(b, 0)
    t, r = inverse_rms(b, 0, t, D, RB[:, 0, :], rb_free[0])
    for k in range(8):
        t = op("vector", [r], lambda e, k=k: e.scalar_tensor_tensor(
            X[:, k, :], X[:, k, :], col("final_norm", k), RB[:, 0, :], ALU.mult, ALU.mult), "v_x")
        if k % 2 == 1:
            fin = op("sync" if k % 4 == 1 else "scalar", [t], lambda e, k=k: e.dma_start(
                out[:, k - 1:k + 1, :], X[:, k - 1:k + 1, :]), "d_out", 16)

    with nc.Block() as block:
        @block.sync
        def _(e):
            P.run("sync", e)
            e.wait_ge(P.sems["d_out"], P.counts["d_out"])

        @block.scalar
        def _(e):
            P.run("scalar", e)

        @block.vector
        def _(e):
            P.run("vector", e)

        @block.gpsimd
        def _(e):
            P.run("gpsimd", e)

        @block.tensor
        def _(e):
            P.run("tensor", e)


def _tiles(w, cols):
    k = w.shape[0] // 128
    return w[:, cols].reshape(k, 128, len(cols)).transpose(1, 0, 2).reshape(128, k * len(cols))


def _chunks(a):
    r = np.arange
    cut = np.cumsum([0, 384, 256, 32, 512, 512, 512, 8, 1024, 1024])
    cq, ckv, kr, fq, fk, fv, ff, gm, gf = (r(cut[i], cut[i + 1]) for i in range(9))
    sw = np.concatenate([r(16, 32), r(16)])
    cols_in = np.concatenate([cq, np.tile(ff, 8), kr, kr[sw], ckv, fk, fq, fv, gm, gf])
    uq = np.concatenate([np.concatenate([r(64), 64 + r(32), 64 + sw]) + 96 * h for h in range(8)])
    ukv = np.concatenate([np.concatenate([r(64) + 128 * h for h in range(8)]),
                          np.concatenate([64 + r(64) + 128 * h for h in range(8)])])
    up = np.concatenate([np.concatenate([r(128) + 128 * j, 2816 + r(128) + 128 * j]) for j in range(22)])
    out = []
    for kind, i in weight_order():
        c = r(256 * i, 256 * i + 256)
        if kind == "in":
            t = _tiles(a["w_in"][0], cols_in[c])
        elif kind == "uq":
            t = np.pad(_tiles(a["w_uq"][0], uq[512 * i:512 * i + 512]), ((0, 0), (0, 512)))
        elif kind == "ukv":
            t = _tiles(a["w_ukv"][0], ukv)
        elif kind == "o":
            t = np.concatenate([_tiles(a["w_o_mla"][0], c), _tiles(a["w_o_fox"][0], c)], axis=1)
        elif kind == "out":
            t = _tiles(a["w_out"][0], c)
        elif kind == "up":
            t = _tiles(a["w_up"][0], up[c])
        elif kind == "down":
            t = _tiles(a["w_down"][0][c], r(1024))
        else:
            layer = int(kind[-1])
            w = a[{"qkv": "w_in_2", "out": "w_out_2", "ff1": "w_ff1_2", "ff2": "w_ff2_2"}[kind[:-1]]][layer]
            t = _tiles(w[c], r(1024)) if kind[:-1] == "ff2" else _tiles(w, c)
        out.append(t)
    return np.stack(out)


def _slopes(n):
    return np.array([2.0 ** (-8.0 * (h + 1) / n) for h in range(n)], dtype=np.float32)


def _alibi(n):
    dist = (128 + np.arange(128)[:, None] - np.arange(256)[None, :]).astype(np.float32)
    t = -_slopes(n)[None, :, None] * dist[:, None, :] / np.float32(SCALE64)
    return np.where(dist[:, None, :] >= 0, t, np.float32(NEG)).astype(np.float32)


def _smalls(a):
    def tiles(v):
        return np.asarray(v).reshape(-1, 128).T

    p = np.arange(128)
    one = lambda f: np.array([f(i) for i in range(128)], np.float32)[:, None]
    inv = np.float32(10000.0) ** (-np.arange(0, 32, 2, dtype=np.float32) / np.float32(32))
    m1 = np.stack([one(lambda q: 8.0 if q == h else 0.0)[:, 0] for h in range(8)], 1)
    m2 = np.stack([one(lambda q: 1.0 if q - 8 == h else 0.0)[:, 0] for h in range(8)], 1)
    parts = [
        tiles(a["c"]), tiles(a["b_ada"]), tiles(a["norm_mix_g"]), tiles(a["norm_ffn_g"]), tiles(a["norm_final_g"]),
        tiles(a["q_norm_g"]), tiles(a["kv_norm_g"]), tiles(a["conv_w"]), tiles(a["conv_b"]),
        tiles(a["attn_norm_2"]), tiles(a["mlp_norm_2"]), tiles(a["final_norm_2"]), tiles(a["diff_subln_2"]),
        np.tile(a["b_forget"][0], 16)[:, None], inv[p % 16][:, None].astype(np.float32),
        one(lambda q: -1.0 if q % 32 < 16 else 1.0), one(lambda q: EPS), m1, m2,
        one(lambda q: -8.0 if q >= 8 else 0.0), one(lambda q: 1.0 if q < 8 else 0.0),
    ]
    return np.concatenate(parts, axis=1)


def _layout(a):
    w = a["w_ada"][0]
    first = w[:, 0:2048].reshape(8, 128, 2, 8, 128).transpose(3, 1, 0, 2, 4).reshape(8, 128, 2048)
    rest = w.reshape(4, 2, 128, 6, 1024).transpose(3, 0, 2, 1, 4).reshape(24, 128, 2048)[8:]
    ada = np.concatenate([first, rest])
    tri = np.where(np.arange(128)[None, :] <= np.arange(128)[:, None], np.float32(0), np.float32(NEG))
    masks = np.concatenate([np.eye(128, dtype=np.float32), np.zeros((128, 128), np.float32), tri], axis=1)
    return {
        "wall": _chunks(a),
        "wada": ada,
        "smalls": _smalls(a),
        "pos": np.tile(a["positions"], (128, 1)),
        "xt": a["x"][0].T.reshape(8, 128, 256).transpose(1, 0, 2),
        "masks": masks.astype(np.float32),
        "lam4": np.tile(a["diff_lambda_2"][0].reshape(1, 256), (128, 1)),
        "alibi8": _alibi(8),
        "alibi16": _alibi(16),
    }


def kernel(**inputs):
    import concourse.bacc as _bacc
    from concourse.bass_utils import run_bass_kernel_spmd as _run

    a = {k: np.asarray(v) for k, v in inputs.items()}
    arrays = {k: np.ascontiguousarray(v) for k, v in _layout(a).items()}
    nc = _bacc.Bacc("TRN2", target_bir_lowering=False, num_devices=1)
    aps = [nc.dram_tensor(k, v.shape, mybir.dt.from_np(v.dtype), kind="ExternalInput").ap() for k, v in arrays.items()]
    o = nc.dram_tensor("out", (128, 8, 256), F32, kind="ExternalOutput").ap()
    build(nc, *aps, o)
    r = _run(nc, [arrays], core_ids=[0])
    y = r.results[0]["out"]
    return np.ascontiguousarray(y.transpose(1, 0, 2).reshape(1024, 256).T).reshape(1, 256, 1024)
```

```python
import math
from contextlib import ExitStack

import numpy as np

import concourse.bass as bass
from concourse import mybir
from concourse.alu_op_type import AluOpType as ALU

F32 = mybir.dt.float32
F32R = mybir.dt.float32r
I32 = mybir.dt.int32
ACT = mybir.ActivationFunctionType

T = 256
D = 1024
CH = 2048
EPS = 1e-6
NEG = -1e30
BIG = 3e38
MLA_SCALE = 1.0 / math.sqrt(96.0)
SCALE64 = 0.125
LAM_INIT = 0.8 - 0.6 * math.exp(0.0)
TWO_PI = 2.0 * math.pi
MAGIC = 12582912.0
C1 = 6.28125
C2 = float(np.float32(np.round((TWO_PI - C1) * 2.0**18) / 2.0**18))
C3 = float(np.float32(TWO_PI - C1 - C2))

RAW = 4
HL = 3

COLS = {}


def _columns():
    at = 0
    for name, n in [
        ("c", 8), ("b_ada", 48), ("norm_mix_g", 8), ("norm_ffn_g", 8), ("norm_final_g", 8),
        ("q_norm_g", 3), ("kv_norm_g", 2), ("conv_w", 132), ("conv_b", 44), ("attn_norm", 16),
        ("mlp_norm", 16), ("final_norm", 8), ("subln", 1), ("b_forget", 1), ("invf", 1), ("sgn", 1),
        ("eps", 1), ("m1", 8), ("m2", 8), ("m3", 1), ("m4", 1),
    ]:
        COLS[name] = at
        at += n
    return at


NCOL = _columns()


QKV_ORDER = (0, 4, 1, 5, 8, 2, 6, 9, 3, 7, 10, 11)


def weight_order():
    order = [("in", i) for i in range(7)]
    order += [("uq", 0), ("in", 7), ("uq", 1), ("in", 8), ("ukv", 0)]
    order += [("in", i) for i in range(9, 17)]
    order += [("o", i) for i in range(4)] + [("out", i) for i in range(4)]
    for i in range(11):
        order += [("up", 2 * i), ("up", 2 * i + 1)]
        if i >= 1:
            order.append(("down", i - 1))
    order.append(("down", 10))
    for layer in range(2):
        order += [(f"qkv{layer}", j) for j in QKV_ORDER]
        order += [(f"out{layer}", i) for i in range(4)]
        for i in range(16):
            order.append((f"ff1{layer}", i))
            if i >= 2:
                order.append((f"ff2{layer}", i - 2))
        order += [(f"ff2{layer}", 14), (f"ff2{layer}", 15)]
    return order


USED = {"uq": 1536}


def stream_order():
    order = weight_order()
    items = [("w", n) + order[n] for n in range(2)]
    late = [("ada", cb, kk) for cb in range(2, 6) for kk in range(4)]
    after = [3, 5, 7, 10, 13, 14, 15, 16, 17, 18, 19, 21] + [n for n in range(len(order)) if order[n][0] == "down"][1:5]
    for n in range(2, len(order)):
        items.append(("w", n) + order[n])
        if n in after:
            items.append(late.pop(0))
    return items


class Program:

    def __init__(self, nc, ctx):
        self.nc, self.ctx = nc, ctx
        self.queues = {e: [] for e in ("sync", "scalar", "vector", "gpsimd", "tensor")}
        self.sems, self.counts, self.seen = {}, {}, {}

    def op(self, engine, waits, issue, signal=None, by=1):
        q = self.queues[engine]
        for name, value in waits:
            if self.seen.get((engine, name), 0) < value:
                self.seen[(engine, name)] = value
                q.append((None, self.sems[name], value))
        if signal is None:
            q.append((issue, None, 0))
            return None
        if signal not in self.sems:
            self.sems[signal] = self.ctx.enter_context(self.nc.semaphore(signal))
        self.counts[signal] = self.counts.get(signal, 0) + by
        q.append((issue, self.sems[signal], by))
        return signal, self.counts[signal]

    def run(self, engine, eng):
        for issue, sem, n in self.queues[engine]:
            if issue is None:
                eng.wait_ge(sem, n)
            else:
                ins = issue(eng)
                if sem is not None:
                    ins.then_inc(sem, n)


def build(nc, wall, wada, smalls, pos, xt, masks, lam4, alibi8, alibi16, out):
    ctx = ExitStack()
    with ctx:
        _build(nc, ctx, wall, wada, smalls, pos, xt, masks, lam4, alibi8, alibi16, out)


def _build(nc, ctx, wall, wada, smalls, pos, xt, masks, lam4, alibi8, alibi16, out):
    def sb(name, shape, dt=F32):
        return ctx.enter_context(nc.sbuf_tensor(name, shape, dt))

    P = Program(nc, ctx)
    op = P.op

    raw = [sb(f"raw{i}", [128, CH]) for i in range(RAW)]
    whi = [sb(f"whi{i}", [128, CH], F32R) for i in range(HL)]
    wlo = [sb(f"wlo{i}", [128, CH], F32R) for i in range(HL)]
    X = sb("X", [128, 8, T])
    Hh = sb("Hh", [128, 8, T], F32R)
    Hl = sb("Hl", [128, 8, T], F32R)
    Oh = sb("Oh", [128, 8, T], F32R)
    Ol = sb("Ol", [128, 8, T], F32R)
    QM = sb("QM", [128, 8, T])
    KM = sb("KM", [128, 8, T])
    with ExitStack() as first:
        QF, KF = (first.enter_context(nc.sbuf_tensor(name, [128, 8, T], F32)) for name in ("QF", "KF"))
    whi.append(sb("whi3", [128, CH], F32R))
    wlo.append(sb("wlo3", [128, CH], F32R))
    V = sb("V", [128, 2, 1024])
    GA = sb("GA", [128, 16, T])
    ACC = sb("ACC", [128, 1024])
    SQ = sb("SQ", [128, 4, T])
    COS = sb("COS", [128, T])
    SIN = sb("SIN", [128, T])
    PB = sb("PB", [128, 4, 384])
    PT = sb("PT", [128, 4, 384])
    TT = sb("TT", [128, 2, T])
    RB = sb("RB", [128, 2, T])
    ID = sb("ID", [128, 128])
    TRI = sb("TRI", [128, T])
    ONES = sb("ONES", [128, 128])
    SM = sb("SM", [128, NCOL])
    ADA = sb("ADA", [128, 48])
    GS = sb("GS", [128, 16])
    CA = sb("CA", [128, 8])
    GC = sb("GC", [128, 8])
    ST = sb("ST", [128, 10])
    RS = sb("RS", [128, 8])
    NM = sb("NM", [128, 8])
    LM = sb("LM", [128, 6])
    SW = sb("SW", [128, 1])
    LV = sb("LV", [128, 256])
    PS = ctx.enter_context(nc.psum_tensor("PS", [128, 8, 512], F32))

    def col(name, i=0, n=1, p0=0, p1=128):
        return SM[p0:p1, COLS[name] + i:COLS[name] + i + n]

    PBf = PB[:, :, :].rearrange("p a b -> p (a b)")
    PTf = PT[:, :, :].rearrange("p a b -> p (a b)")
    f32 = lambda ap: ap.bitcast(F32)

    small = op("sync", [], lambda e: e.dma_start(SM[:, :], smalls), "d_small", 16)
    xin = op("sync", [], lambda e: e.dma_start(X[:, :, :], xt), "d_x", 16)
    items = stream_order()
    chunk_no = {it[2:]: it[1] for it in items if it[0] == "w"}
    raw_free = {}
    landed = {}

    def load(i):
        it = items[i]
        slot = i % RAW
        if it[0] == "ada":
            _, cb, kk = it
            dst, src = raw[slot][:, :], wada[cb * 4 + kk]
        else:
            n = USED.get(it[2], CH)
            dst, src = raw[slot][:, 0:n], wall[it[1]][:, 0:n]
        landed[i] = op("sync", raw_free.get(i - RAW, []), lambda e: e.dma_start(dst, src), f"d_raw{slot}", 16)

    flat = lambda x: x[:, :, :].rearrange("p a b -> p (a b)")
    first_ada = [raw[2][:, :], raw[3][:, :]] + [flat(x) for x in (KM, QF, KF, V, GA[:, 0:8], GA[:, 8:16])]
    ada0_in = []
    for i in range(2):
        load(i)
    for j in range(8):
        ada0_in.append(op("sync", [], lambda e, j=j: e.dma_start(first_ada[j], wada[j]), f"d_ada{j}", 16))
    posi = TT[:, 0, :].bitcast(I32)
    pin = op("scalar", [], lambda e: e.dma_start(posi, pos), "d_pos", 16)
    mk = op("scalar", [], lambda e: e.dma_start(ID[:, :], masks[:, 0:128]), "d_id", 16)
    mt = op("scalar", [], lambda e: e.dma_start(TRI[:, :], masks[:, 128:384]), "d_tri", 16)
    lam_in = op("scalar", [], lambda e: e.dma_start(LV[:, :], lam4), "d_lam", 16)
    ones = op("gpsimd", [], lambda e: e.memset(ONES[:, :], 1.0), "g_ones")

    st = {"next": 0, "ada": None}
    hi_tok, lo_tok, mm_tok = {}, {}, {}

    more_from = chunk_no[("out", 0)]
    place3_free = []

    def place(n):
        if n < more_from:
            return n % HL
        return (HL, *((more_from - HL + i) % HL for i in range(HL)))[(n - more_from) % (HL + 1)]

    ada_acc = {}
    ada_free = []

    def take_ada(i, cb, kk):
        src = raw[i % RAW]
        for half in range(2):
            k = 2 * kk + half
            w = src[:, half * 1024:(half + 1) * 1024]
            if k == 0:
                while ada_late:
                    ada_late.pop(0)[1]()
                tok = op("vector", [landed[i], cact] + ada_free, lambda e, w=w: e.tensor_scalar(
                    ACC[:, :], w, CA[:, 0:1], None, ALU.mult), "v_ada")
            else:
                tok = op("vector", [landed[i], st["ada"]], lambda e, w=w, k=k: e.scalar_tensor_tensor(
                    ACC[:, :], w, CA[:, k:k + 1], ACC[:, :], ALU.mult, ALU.add), "v_ada")
            st["ada"] = tok
        raw_free[i] = [st["ada"]]
        if kk == 3:
            acc = st["ada"]
            ada_late.append((max(mm_tok) + 2, lambda: ada_sum(cb, acc)))

    ada_late = []

    def ada_sum(cb, acc):
        b = gbank()
        for j in range(8):
            t = op("tensor", [acc, ones] + bank_free[b], lambda e, j=j, b=b: e.matmul(
                PS[:, b, j:j + 1], ACC[:, j * 128:(j + 1) * 128], ONES[:, 0:1],
                start=True, stop=True), "t_ada" if j == 7 else None)
        ada_free[:] = [t]
        tok = op("vector", [t, small], lambda e, b=b, cb=cb: e.tensor_tensor(
            ADA[:, cb * 8:(cb + 1) * 8], PS[:, b, 0:8], col("b_ada", cb * 8, 8), ALU.add), "v_adab")
        bank_free[b] = [tok]
        ada_acc[cb] = tok

    gs_tok = {}

    ada0_tok, ada0_steps = {}, []

    def steps(n):
        while n and ada0_steps:
            ada0_steps.pop(0)()
            n -= 1

    ada0_rows = ((1, 2), (2, 2), (2, 1), (2, 1))

    def ada0_products(p, half):
        j = 2 * p + half
        src, here = first_ada[j], ada0_in[j]
        row = 4 + p % 2
        for k in range(ada0_rows[p][half]):
            c = CA[:, 4 * half + k:4 * half + k + 1]
            ada0_tok[("pe", j)] = op("tensor", [here, cact] + bank_free[row], lambda e, k=k, c=c: e.matmul(
                PS[0:1, row, :], c, src[:, k * 512:k * 512 + 512], start=half == 0 and k == 0, stop=False), "t_arow")

    def ada0_add(p, half):
        j = 2 * p + half
        src, here = first_ada[j], ada0_in[j]
        a = ACC[:, (p % 2) * 512:(p % 2) * 512 + 512]
        n = ada0_rows[p][half]

        def step(k):
            w = src[:, k * 512:k * 512 + 512]
            c = CA[:, 4 * half + k:4 * half + k + 1]
            if half == 0 and k == n:
                free = [ada0_tok[("sum", p - 2)]] if p >= 2 else []
                t = op("vector", [here, cact] + free, lambda e: e.tensor_scalar(a, w, c, None, ALU.mult), "v_ada")
            else:
                t = op("vector", [here, ada0_tok[("v", p)]], lambda e: e.scalar_tensor_tensor(
                    a, w, c, a, ALU.mult, ALU.add), "v_ada")
            ada0_tok[("v", p)] = ada0_tok[("ve", j)] = t

        ada0_steps.extend(lambda k=k: step(k) for k in range(n, 4))

    def ada0_sum(p):
        a = ACC[:, (p % 2) * 512:(p % 2) * 512 + 512]
        row = 4 + p % 2
        t = op("tensor", [ada0_tok[("v", p)], ones], lambda e: e.matmul(
            PS[0:1, row, :], ONES[:, 0:1], a, start=False, stop=True), "t_arow")
        ada0_tok[("sum", p)] = t
        r = op("scalar", [t], lambda e: e.activation(
            PBf[0:1, (p % 2) * 512:(p % 2) * 512 + 512], PS[0:1, row, :], ACT.Copy), "a_arow")
        bank_free[row] = [r]
        ada0_tok[("row", p)] = r

    def ada0_total(p):
        b = 6 + p % 2
        for q in range(4):
            m = op("tensor", [ada0_tok[("row", p)], mk] + bank_free[b], lambda e, q=q: e.transpose(
                PS[:, b, q:q + 1], PBf[0:1, (p % 2) * 512 + q * 128:(p % 2) * 512 + q * 128 + 128], ID[0:1, 0:1]),
                "t_ada" if q == 3 else None)
        two = lambda x, at: x[:, at + 2 * p:at + 2 * p + 2]
        op("vector", [m, small], lambda e: e.tensor_tensor(
            two(ADA, 0), PS[:, b, 0:2], two(SM, COLS["b_ada"]), ALU.add), None)
        u = op("vector", [], lambda e: e.tensor_tensor(
            two(ADA, 8), PS[:, b, 2:4], two(SM, COLS["b_ada"] + 8), ALU.add), "v_adab")
        bank_free[b] = [u]
        gs_tok[2 * p] = gs_tok[2 * p + 1] = op("vector", [u], lambda e: e.scalar_tensor_tensor(
            two(GS, 0), two(ADA, 8), 1.0, two(SM, COLS["norm_mix_g"]), ALU.add, ALU.mult), "v_gs")

    def take_weight(i, n, kind):
        slot = place(n)
        w = USED.get(kind, CH)
        src = raw[i % RAW]
        if n == more_from:
            free = place3_free
        else:
            free = [mm_tok[n - HL - (n > more_from)]] if n >= HL else []
        hi_tok[n], lo_tok[n] = [], []
        for half in range(2):
            c = slice(half * CH // 2, min(w, (half + 1) * CH // 2))
            hi_tok[n].append(op("scalar", [landed[i]] + free, lambda e, c=c: e.activation(
                whi[slot][:, c], src[:, c], ACT.Copy), "a_whi"))
        for half in range(2):
            c = slice(half * CH // 2, min(w, (half + 1) * CH // 2))
            lo_tok[n].append(op("vector", [hi_tok[n][half]] + free, lambda e, c=c: e.tensor_tensor(
                wlo[slot][:, c], src[:, c], f32(whi[slot][:, c]), ALU.subtract), "v_wlo"))
        raw_free[i] = [lo_tok[n][1]]

    def weight_wait(n, last_col):
        half = (last_col - 1) // (CH // 2)
        return [hi_tok[n][half], lo_tok[n][half]]

    def take_next():
        i = st["next"]
        it = items[i]
        if it[0] == "ada":
            take_ada(i, it[1], it[2])
        else:
            take_weight(i, it[1], it[2])
        st["next"] = i + 1
        if i >= 2 and i + RAW < len(items):
            load(i + RAW)

    def ensure(n):
        while st["next"] < len(items) and max(hi_tok, default=-1) < n:
            take_next()

    bank_free = {b: [] for b in range(8)}
    rot = {"banks": [0, 1, 2, 3], "at": 0}

    def gbank():
        b = rot["banks"][rot["at"] % len(rot["banks"])]
        rot["at"] += 1
        return b

    def mm_begin(key):
        n = chunk_no[key]
        ensure(n)
        return n

    def mm_end(n, tok):
        mm_tok[n] = tok

    chores = []

    def refill(n):
        if ada_late and ada_late[0][0] <= n:
            ada_late.pop(0)[1]()
        ensure(n + HL + (n + HL + 1 >= more_from))
        if chores:
            chores.pop(0)()

    def mm_T(n, kts, ncols, nt, dst, waits, xh, xl, xk, first=True, last=True, share=False, signal=None):
        slot = place(n)
        w0 = list(waits)
        tok = None
        for k in range(kts):
            wh = whi[slot][:, k * ncols + nt * 128:k * ncols + nt * 128 + 128]
            wl = wlo[slot][:, k * ncols + nt * 128:k * ncols + nt * 128 + 128]
            a, b = xh[:, xk(k), :], xl[:, xk(k), :]
            ww = (w0 if k == 0 else []) + weight_wait(n, k * ncols + nt * 128 + 128) + xwait(xk(k))

            def go(e, wh=wh, wl=wl, a=a, b=b, k=k):
                e.matmul(dst, wh, a, start=first and k == 0, stop=False, skip_group_check=share)
                e.matmul(dst, wh, b, start=False, stop=False, skip_group_check=share)
                return e.matmul(dst, wl, a, start=False, stop=last and k == kts - 1, skip_group_check=share)

            tok = op("tensor", ww, go, signal if k == kts - 1 else None)
        return tok

    def mm_N(n, kts, ncols, c0, nc_, dst, half, waits, xh, xl, xk, signal=None):
        slot = place(n)
        tok = None
        for k in range(kts):
            wh = whi[slot][:, k * ncols + c0:k * ncols + c0 + nc_]
            wl = wlo[slot][:, k * ncols + c0:k * ncols + c0 + nc_]
            a, b = (x[:, xk(k), half * 128:half * 128 + 128] for x in (xh, xl))
            ww = (list(waits) if k == 0 else []) + weight_wait(n, k * ncols + c0 + nc_) + xwait(xk(k))

            def go(e, wh=wh, wl=wl, a=a, b=b, k=k):
                e.matmul(dst, a, wh, start=k == 0, stop=False)
                e.matmul(dst, b, wh, start=False, stop=False)
                return e.matmul(dst, a, wl, start=False, stop=k == kts - 1)

            tok = op("tensor", ww, go, signal if k == kts - 1 else None)
        return tok

    xready = {}

    def xwait(k):
        return xready.get(k, [])

    heads = {"all": [], "scored": 0, "scaled": 0, "turned": 0, "valued": 0}
    post = []

    def new_head(ready, *stages):
        heads["all"].append((ready, stages))

    def middle():
        n, hs = dict(heads), heads["all"]
        if n["valued"] < n["turned"] and hs[n["valued"]][0]():
            hs[n["valued"]][1][3]()
            heads["valued"] += 1
        if post:
            post.pop(0)()
        if n["turned"] < n["scaled"] and n["turned"] - heads["valued"] < 2:
            hs[n["turned"]][1][2]()
            heads["turned"] += 1
        if n["scored"] < len(hs) and n["scored"] - heads["turned"] < 2:
            hs[n["scored"]][1][0]()
            heads["scored"] += 1

    def after():
        if post:
            post.pop(0)()
        if heads["scaled"] < heads["scored"]:
            heads["all"][heads["scaled"]][1][1]()
            heads["scaled"] += 1

    def advance():
        middle()
        after()

    def flush():
        while heads["valued"] < len(heads["all"]) or post:
            advance()

    def arriving(tiles):
        def hook(k):
            if k == 8:
                return
            if k:
                advance()
            while k not in tiles:
                advance()
            xready[k] = tiles[k]
        return hook

    def chunk_T(key, x, evac, kts=8, ncols=256, pairs=1, xk=lambda k: k, mid=True, fill=True):
        xh, xl = x
        n = mm_begin(key)
        for pr in range(pairs):
            b = gbank()
            fr = list(bank_free[b])
            mm_T(n, kts, ncols, 2 * pr, PS[:, b, 0:T], fr, xh, xl, xk)
            if pr == 0 and mid:
                middle()
            tok = mm_T(n, kts, ncols, 2 * pr + 1, PS[:, b, T:2 * T], [], xh, xl, xk, signal="t_mm")
            if pr == pairs - 1:
                mm_end(n, tok)
            evac(pr, b, tok)
        after()
        if fill:
            refill(n)

    def together(keys, x, evacs, hook=None):
        xh, xl = x
        ns = [mm_begin(key) for key in keys]
        bs = [gbank() for _ in keys]
        order = [(0, 0), (0, 1), (1, 0), (1, 1)] + [(k, 2) for k in range(2) if len(keys) > 2]
        order += [(k, c) for k in range(2, 6) for c in range(len(keys))]
        order += [(k, c) for c in range(len(keys)) for k in (6, 7)]
        for k, c in order:
            if hook and c == 0:
                hook(k)
            n, b = ns[c], bs[c]
            slot = place(n)
            for nt in range(2):
                at = k * 256 + nt * 128
                wh, wl = whi[slot][:, at:at + 128], wlo[slot][:, at:at + 128]
                dst = PS[:, b, nt * T:nt * T + T]

                def upper(e, wh=wh, wl=wl, dst=dst, k=k, nt=nt):
                    e.matmul(dst, wh, xh[:, k, :], start=k == 0 and nt == 0, stop=False, skip_group_check=True)
                    return e.matmul(dst, wl, xh[:, k, :], start=False, stop=False, skip_group_check=True)

                def lower(e, wh=wh, dst=dst, k=k):
                    return e.matmul(dst, wh, xl[:, k, :], start=False, stop=k == 7, skip_group_check=True)

                op("tensor", bank_free[b] + weight_wait(n, at + 128) + xwait(k)[0:1], upper)
                tok = op("tensor", xwait(k)[1:], lower, "t_mm" if k == 7 and nt == 1 else None)
            if k == 7:
                mm_end(n, tok)
        if hook:
            hook(8)
        three = len(ns) > 2
        for c, (b, evac) in enumerate(zip(bs, evacs)):
            evac(0, b, mm_tok[chunk_no[keys[c]]])
            if three and c == 0:
                refill(ns[0])
                refill(ns[1])
        after()
        if not three:
            for n in ns:
                refill(n)

    sq_free = {i: [] for i in range(4)}
    rb_free = {0: [], 1: []}

    def total(b, c0, parts):
        for i, (tile, waits) in enumerate(parts):
            for half in range(2):
                t = op("tensor", [ones] + list(waits) + bank_free[b], lambda e, i=i, tile=tile, half=half: e.matmul(
                    PS[:, b, c0 + half:c0 + half + 1], tile[:, half * 128:half * 128 + 128], ONES[:, 0:1],
                    start=i == 0 and half == 0, stop=i == len(parts) - 1, skip_group_check=True), "t_sq")
        return t

    def root(b, c0, n, tok, dim, dst, free=()):
        t = op("scalar", [tok, small] + list(free), lambda e: e.activation(
            dst, PS[:, b, c0:c0 + n], ACT.Sqrt, bias=col("eps"), scale=1.0 / dim), "a_sqrt")
        return op("vector", [t], lambda e: e.reciprocal(dst, dst), "v_rec")

    def spread(b, c0, src, n, tok):
        for h in range(n):
            t = op("tensor", [tok, mk], lambda e, h=h: e.matmul(
                PS[:, b, c0 + 128 * h:c0 + 128 * h + 128], src[:, h:h + 1].to_broadcast([128, 128]), ID[:, :],
                start=True, stop=True), "t_row" if h == n - 1 else None)
        return t

    def inverse_rms(b, tok, dim, cols, r):
        u = root(b, 0, 2, tok, dim, cols)

        def finish(copy=True):
            t = spread(b, 256, cols, 2, u)
            if not copy:
                return t
            t = op("scalar", [t] + rb_free[r], lambda e: e.activation(RB[:, r, :], PS[:, b, 256:512], ACT.Copy), "a_rb")
            bank_free[b] = [t]
            return t

        return finish

    def small_norm(srcs, squares, dim, waits, r):
        parts = []
        for k, (src, sq) in enumerate(zip(srcs, squares)):
            s = op("scalar", list(waits(k)), lambda e, src=src, sq=sq: e.activation(sq, src, ACT.Square), "a_sq")
            parts.append((sq, [s]))

        def finish():
            b = gbank()
            t = total(b, 0, parts)
            for k in range(4):
                sq_free[k] = [t]
            return inverse_rms(b, t, dim, ST[:, 2 * r:2 * r + 2], r)

        return finish

    x_tok = {}
    nrm = {}

    def square_pair(g):
        d = 2 if g == 0 else 0
        fl = lambda x, a: x[:, a:a + 2, :].rearrange("p j t -> p (j t)")
        s = op("scalar", [x_tok[2 * g], x_tok[2 * g + 1]] + sq_free[d] + sq_free[d + 1], lambda e: e.activation(
            fl(SQ, d), fl(X, 2 * g), ACT.Square), "a_sq")
        if g in (1, 2):
            t = op("vector", [s], lambda e: e.tensor_tensor(fl(SQ, 2), fl(SQ, 2), fl(SQ, 0), ALU.add), "v_sq")
            sq_free[0] = sq_free[1] = nrm["acc"] = [t]
        elif g == 3:
            nrm["last"] = [s]

    def total_squares(b, c0):
        t = total(b, c0, [(SQ[:, 2, :], nrm["acc"]), (SQ[:, 3, :], []), (SQ[:, 0, :], nrm["last"]), (SQ[:, 1, :], [])])
        for i in range(4):
            sq_free[i] = [t]
        return t

    def gain_pair(g, gain):
        for k in (2 * g, 2 * g + 1):
            h = op("scalar", [x_tok[k]] + x_free, lambda e, k=k, s=gain(k): e.activation(
                Hh[:, k, :], X[:, k, :], ACT.Identity, scale=s), "a_xhi")
            t = op("vector", [h] + x_free, lambda e, k=k, s=gain(k): e.scalar_tensor_tensor(
                Hl[:, k, :], X[:, k, :], s, f32(Hh[:, k, :]), ALU.mult, ALU.subtract), "v_xlo")
            nready[k] = [h, t]

    nready = {}

    tt_free = {}

    def apply(src, ks, gain, shift, r, rtok, dst, k0=0, waits=lambda k: [], ready=None, by=None):
        dh, dl = dst
        steps = []
        ready = xready if ready is None else ready
        for k in ks:
            s = k % 2
            t = op("vector", [rtok] + waits(k) + tt_free.get(s, []), lambda e, k=k, s=s, g=gain(k): e.scalar_tensor_tensor(
                TT[:, s, :], src(k), g, RB[:, r, :] if by is None else by, ALU.mult, ALU.mult), "v_nrm")
            rb_free[r] = [t]
            if shift is None:
                h = op("scalar", [t] + x_free, lambda e, k=k, s=s: e.activation(
                    dh[:, k0 + k, :], TT[:, s, :], ACT.Copy), "a_xhi")
            else:
                h = op("scalar", [t] + x_free, lambda e, k=k, s=s: e.activation(
                    dh[:, k0 + k, :], TT[:, s, :], ACT.Identity, bias=shift(k)), "a_xhi")
            steps.append((k, s, h))
            if len(steps) > 1:
                low(dh, dl, k0, shift, steps.pop(0), ready)
        low(dh, dl, k0, shift, steps.pop(0), ready)

    def low(dh, dl, k0, shift, step, ready):
        k, s, h = step
        if shift is None:
            t = op("vector", [h] + x_free, lambda e: e.tensor_tensor(
                dl[:, k0 + k, :], TT[:, s, :], f32(dh[:, k0 + k, :]), ALU.subtract), "v_xlo")
        else:
            t = op("vector", [h] + x_free, lambda e: e.scalar_tensor_tensor(
                dl[:, k0 + k, :], TT[:, s, :], shift(k), f32(dh[:, k0 + k, :]), ALU.add, ALU.subtract), "v_xlo")
        tt_free[s] = [t]
        ready[k0 + k] = [h, t]

    x_free = []

    def split(dh, dl, src, waits, free=()):
        h = op("scalar", list(waits) + list(free), lambda e: e.activation(dh, src, ACT.Copy), "a_xhi")
        return h, op("vector", [h], lambda e: e.tensor_tensor(dl, src, f32(dh), ALU.subtract), "v_xlo")

    cact = op("scalar", [small], lambda e: e.activation(CA[:, :], col("c", 0, 8), ACT.Silu), "a_c")
    ANG = PTf[:, 0:256]
    t = op("vector", [pin], lambda e: e.tensor_copy(ANG, posi), "v_rope")
    ang = op("vector", [t, small], lambda e: e.tensor_scalar(ANG, ANG, col("invf"), None, ALU.mult), "v_rope")
    tt_free[0] = [ang]

    def rotary(dst, cosine):
        KR, RR = (PTf[:, a + 512 * cosine:a + 512 * cosine + 256] for a in (256, 512))
        steps = []
        if cosine:
            steps.append(lambda e: e.tensor_scalar(KR, ANG, 1.0 / TWO_PI, 0.25, ALU.mult, ALU.add))
            steps.append(lambda e: e.tensor_scalar(KR, KR, MAGIC, None, ALU.add))
        else:
            steps.append(lambda e: e.tensor_scalar(KR, ANG, 1.0 / TWO_PI, MAGIC, ALU.mult, ALU.add))
        steps.append(lambda e: e.tensor_scalar(KR, KR, MAGIC, None, ALU.subtract))
        steps.append(lambda e: e.scalar_tensor_tensor(RR, KR, -C1, ANG, ALU.mult, ALU.add))
        steps.append(lambda e: e.scalar_tensor_tensor(RR, KR, -C2, RR, ALU.mult, ALU.add))
        steps.append(lambda e: e.scalar_tensor_tensor(RR, KR, -C3, RR, ALU.mult, ALU.add))
        if cosine:
            steps.append(lambda e: e.tensor_scalar(RR, RR, math.pi / 2, None, ALU.add))
        steps.append(lambda e: e.tensor_scalar(RR, RR, 3.1415925, -3.1415925, ALU.min, ALU.max))
        return steps, lambda e: e.activation(dst[:, :], RR, ACT.Sin)

    both = [rotary(COS, True), rotary(SIN, False)]
    t = [ang, ang]
    while both[0][0]:
        for i in range(2):
            if both[i][0]:
                t[i] = op("vector", [t[i]], both[i][0].pop(0), "v_rope")
    trig = []

    def tables():
        trig.extend(op("scalar", [t], both[i][1], "a_sin") for i, t in enumerate(angles))

    def signs():
        trig[1] = op("vector", [trig[1]], lambda e: e.tensor_scalar(SIN[:, :], SIN[:, :], col("sgn"), None, ALU.mult), "v_rope")

    angles = t
    op("vector", [small], lambda e: e.tensor_tensor(
        GC[:, :], col("norm_final_g", 0, 8), col("attn_norm", 0, 8), ALU.mult), "v_gs")
    def warm(n):
        for _ in range(n):
            op("tensor", [ones], lambda e: e.matmul(PS[:, 0, 0:128], ONES[:, :], ONES[:, :], start=True, stop=True), None)

    warm(32)
    x_tok.update({k: xin for k in range(8)})
    for g in range(4):
        square_pair(g)
    ensure(0)
    rot["at"] = 1
    sb0 = gbank()
    t = total_squares(sb0, 0)
    rx = inverse_rms(sb0, t, D, ST[:, 0:2], 0)
    ada0_products(0, 0)
    ada0_add(0, 0)
    steps(4)
    ensure(1)
    rx = rx()

    def lam():
        for i in range(2):
            t = op("vector", [lam_in], lambda e, i=i: e.tensor_tensor_reduce(
                PTf[:, 1024 + i * 64:1088 + i * 64], LV[:, i * 128:64 + i * 128], LV[:, 64 + i * 128:128 + i * 128],
                1.0, 0.0, ALU.mult, ALU.add, LM[:, i:i + 1]), "v_lam")
        t = op("scalar", [t], lambda e: e.activation(LM[:, 2:4], LM[:, 0:2], ACT.Exp), "a_lam")
        t = op("vector", [t], lambda e: e.scalar_tensor_tensor(
            LM[:, 4:5], LM[:, 2:3], LAM_INIT, LM[:, 3:4], ALU.add, ALU.subtract), "v_lam")
        w = op("vector", [small], lambda e: e.tensor_scalar(SW[:, :], col("subln"), 1.0 - LAM_INIT, None, ALU.mult), "v_lam")
        return t, w

    H = (Hh, Hl)

    def next_tile(k):
        if k % 2 == 1 or k == 8:
            return
        p = k // 2

        def tiles(p):
            for i in (2 * p, 2 * p + 1):
                sl = i % 2
                t = op("scalar", [gs_tok[i], xn[i]] + tt_free.get(sl, []), lambda e, i=i, sl=sl: e.activation(
                    TT[:, sl, :], QM[:, i, :], ACT.Identity, scale=GS[:, i:i + 1], bias=ADA[:, i:i + 1]), "a_x")
                steps(1)
                h, lo = split(Hh[:, i, :], Hl[:, i, :], TT[:, sl, :], [t])
                tt_free[sl] = [lo]
                xready[i] = [h, lo]

        def follow(p):
            if p < 3:
                ada0_products(p + 1, 0)
                ada0_add(p + 1, 0)
                steps(4)
            ada0_total(p)
            if p < 3:
                ada0_add(p + 1, 1)
            tiles(p)

        if p == 0:
            ada0_products(0, 1)
            ada0_add(0, 1)
            steps(4)
            ada0_sum(0)
            for i in range(8):
                xn[i] = op("vector", [rx, xin], lambda e, i=i: e.tensor_tensor(
                    QM[:, i, :], X[:, i, :], RB[:, 0, :], ALU.mult), "v_nrm")
            rb_free[0] = [xn[7]]
            for i in range(2):
                raw_free[i + 2 - RAW] = [ada0_tok[("pe", i)], ada0_tok[("ve", i)]]
                load(i + 2)
            for i in range(2):
                load(i + RAW)
            follow(0)
            tables()
        if p < 3:
            ada0_products(p + 1, 1)
            steps(4)
            if p == 2:
                ensure(2)
            ada0_sum(p + 1)
            follow(p + 1)
        if p == 1:
            signs()

    xn = {}

    C5 = lambda k: PBf[:, k * T:(k + 1) * T]
    cq_tok = {}

    def ev_c0(pr, b, tok):
        t = op("scalar", [tok], lambda e: e.activation(PBf[:, 0:512], PS[:, b, 0:512], ACT.Copy), "a_ev")
        cq_tok[0] = cq_tok[1] = t
        bank_free[b] = [t]

    FK = V[:, 0, 0:256]

    def ev_c1(pr, b, tok):
        op("scalar", [tok], lambda e: e.activation(PBf[:, 512:768], PS[:, b, 0:256], ACT.Copy), None)
        t = op("scalar", [], lambda e: e.activation(FK, PS[:, b, 256:512], ACT.Copy), "a_ev")
        cq_tok[2] = t
        bank_free[b] = [t]

    def forget():
        z, az, ls = PTf[0:16, 0:256], PTf[0:16, 256:512], PTf[0:16, 512:768]
        fc, rf, on = PTf[0:16, 768:1024], PTf[0:16, 1024:1280], PTf[0:16, 1280:1536]
        cc = lambda name, i=0, n=1: col(name, i, n, 0, 16)
        tk = {}

        def one():
            o1 = op("vector", [], lambda e: e.memset(on, 1.0), "v_f")
            t = op("vector", [cq_tok[2], *trig], lambda e: e.tensor_scalar(z, FK[0:16, :], cc("b_forget"), None, ALU.add), "v_f")
            tk["t"] = op("vector", [t], lambda e: e.scalar_tensor_tensor(az, z, -1.0, z, ALU.mult, ALU.max), "v_f")
            tk["o1"] = o1

        def log():
            t = op("scalar", [tk["t"]], lambda e: e.activation(az, az, ACT.Exp, scale=-1.0), "a_f")
            t = op("scalar", [t], lambda e: e.activation(az, az, ACT.Ln, bias=1.0), "a_f")
            tk["t"] = t

        def two():
            t = op("vector", [tk["t"]], lambda e: e.scalar_tensor_tensor(ls, z, 0.0, az, ALU.min, ALU.subtract), "v_f")
            t = op("vector", [t, tk["o1"]], lambda e: e.tensor_tensor_scan(fc, on, ls, 0.0, ALU.mult, ALU.add), "v_f")
            tk["t"] = t
            tk["rf"] = op("vector", [t], lambda e: e.tensor_scalar(rf, fc, cc("m3"), cc("m4"), ALU.mult, ALU.add), "v_f")

        def queries(h0):
            for h in range(h0, h0 + 4):
                q = op("scalar", [tk["t"]], lambda e, h=h: e.activation(
                    QF[64:80, h, :], fc, ACT.Identity, scale=cc("m1", h), bias=cc("m2", h)), "a_f")
            aug.append(q)

        def keys():
            aug.append(op("scalar", [tk["rf"]], lambda e: e.activation(
                KF[64:80, :, :], rf.unsqueeze(1).to_broadcast([16, 8, T]), ACT.Copy), "a_f"))

        return [one, log, two, lambda: queries(0), keys, lambda: queries(4)]

    aug = []

    def ev_c2(pr, b, tok):
        t = op("scalar", [tok], lambda e: e.activation(PBf[:, 768:1280], PS[:, b, 0:512], ACT.Copy), "a_ev")
        cq_tok[3] = cq_tok[4] = t
        bank_free[b] = [t]

    km_tok = []

    def rope_key():
        a, c = V[64:96, 0, 256:512], V[64:96, 1, 256:512]
        tk = {}

        def turn_key():
            op("vector", [cq_tok[2], *trig], lambda e: e.tensor_tensor(a, FK[64:96, :], COS[64:96, :], ALU.mult), "v_kr")
            t2 = op("vector", [], lambda e: e.tensor_tensor(c, FK[96:128, :], SIN[96:128, :], ALU.mult), "v_kr")
            tk["t"] = op("vector", [t2], lambda e: e.tensor_tensor(a, a, c, ALU.add), "v_kr")

        def copies():
            km_tok.append(op("scalar", [tk["t"]], lambda e: e.activation(
                KM[64:96, :, :], a.unsqueeze(1).to_broadcast([32, 8, T]), ACT.Copy), "a_kr"))

        return turn_key, copies

    def heads_out(dst, h0, toks):
        def ev(b, tok):
            bank = PS[:, b, :].rearrange("p (j t) -> p j t", j=2)
            op("scalar", [tok], lambda e: e.activation(dst[0:64, h0:h0 + 4:2, :], bank[0:64], ACT.Copy), None)
            t = op("scalar", [], lambda e: e.activation(dst[0:64, h0 + 1:h0 + 4:2, :], bank[64:128], ACT.Copy), "a_ev")
            toks.append(t)
            bank_free[b] = [t]
        return ev

    kf_tok, qf_tok, vf_tok, qm_tok, vm_tok = [], [], [], [], []
    VF, VM = V[:, :, 512:1024], V[:, :, 0:512]

    def chunk_N(key, x, evac):
        n = mm_begin(key)
        b = gbank()
        mm_N(n, 8, 256, 0, 256, PS[:, b, 0:256], 0, list(bank_free[b]), x[0], x[1], lambda k: k)
        middle()
        tok = mm_N(n, 8, 256, 0, 256, PS[:, b, 256:512], 1, [], x[0], x[1], lambda k: k, signal="t_mm")
        mm_end(n, tok)
        evac(b, tok)
        after()
        refill(n)

    def v_out(dst, toks):
        def ev(b, tok):
            t = op("scalar", [tok], lambda e: e.activation(
                dst, PS[:, b, :].rearrange("p (h n) -> p h n", h=2), ACT.Copy), "a_ev")
            bank_free[b] = [t]
            toks.append(t)
        return ev

    together([("in", 0), ("in", 1)], H, [ev_c0, ev_c1], next_tile)
    chores += forget()
    turn_key, key_copies = rope_key()
    log = chores[1]
    chores[1] = lambda: (log(), turn_key())
    chores.append(key_copies)
    xr, cn = dict(xready), {}
    q_norm = small_norm([C5(k) for k in range(3)], [SQ[:, k, :] for k in range(3)], 384, lambda k: [cq_tok[k]], 1)
    chunk_T(("in", 2), H, ev_c2)
    kv_norm = small_norm([C5(3), C5(4)], [SQ[:, 3, :], V[:, 1, 0:256]], 256, lambda k: [cq_tok[3 + k]], 0)
    chunk_T(("in", 3), H, lambda pr, b, tok: heads_out(KF, 0, kf_tok)(b, tok))
    rq, rk = q_norm(), kv_norm()
    chunk_T(("in", 4), H, lambda pr, b, tok: heads_out(KF, 4, kf_tok)(b, tok))
    rq, rk = rq(), rk()
    apply(C5, range(3), lambda k: col("q_norm_g", k), None, 1, rq, (Oh, Ol), 0, ready=cn)
    for j in range(2):
        chunk_T(("in", 5 + j), H, lambda pr, b, tok, j=j: heads_out(QF, 4 * j, qf_tok)(b, tok))
        if j == 0:
            apply(lambda k: C5(3 + k), range(2), lambda k: col("kv_norm_g", k), None, 0, rk, (Oh, Ol), 3, ready=cn)

    def ev_uq(pr, b, tok):
        heads_out(QM, 4 * pr, qm_tok)(b, tok)

    def ev_uq_rope(pr, b, tok):
        dst, table = ((TT[:, :, :], COS), (SQ[:, 0:2, :], SIN))[pr]
        t = op("vector", [tok, *trig] + tt_free.get(0, []) + tt_free.get(1, []) + sq_free[0] + sq_free[1],
               lambda e: e.tensor_tensor(dst, PS[:, b, :].rearrange("p (j t) -> p j t", j=2),
                                         table[:, :].unsqueeze(1).to_broadcast([128, 2, T]), ALU.mult), "v_qr")
        bank_free[b] = [t]
        if pr == 0:
            return
        r = op("vector", [t], lambda e: e.tensor_tensor(TT[:, :, :], TT[:, :, :], SQ[:, 0:2, :], ALU.add), "v_qr")
        sq_free[0] = sq_free[1] = [r]

        def copies():
            for j in range(4):
                t = op("scalar", [r], lambda e, j=j: e.activation(
                    QM[64:96, j:8:4, :], TT[32 * j:32 * j + 32, :, :], ACT.Copy), "a_qr")
            tt_free[0] = tt_free[1] = [t]
            qm_tok.append(t)
        chores.append(copies)

    pb_free, pt_free = {}, {}
    s_free, t_free = ({b: list(bank_free[b]) for b in banks} for banks in ((4, 5), (6, 7)))
    a_tok, b_tok = {}, {}

    def scores(heads):
        st_, vt_ = {}, {}
        for slot, q, k, waits, bias, scale in heads:
            b = 4 + slot % 2
            op("tensor", list(waits) + s_free.get(b, []), lambda e, b=b, q=q, k=k: e.matmul(
                PS[:, b, 0:128], q[:, 0:128], k[:, 0:128], start=True, stop=True), None)
            st_[slot] = op("tensor", [], lambda e, b=b, q=q, k=k: e.matmul(
                PS[:, b, 128:384], q[:, 128:256], k[:, 0:256], start=True, stop=True), "t_s")
        for slot, q, k, waits, bias, scale in heads:
            b = 4 + slot % 2
            op("vector", [st_[slot], mt] + list(waits) + pb_free.get(slot, []),
               lambda e, b=b, slot=slot, bias=bias, scale=scale: e.tensor_tensor_reduce(
                PB[:, slot, 0:128], PS[:, b, 0:128], bias[:, 128:256], -scale, BIG, ALU.add, ALU.min,
                NM[:, 2 * slot:2 * slot + 1]), None)
            vt_[slot] = op("vector", [], lambda e, b=b, slot=slot, bias=bias, scale=scale: e.tensor_tensor_reduce(
                PB[:, slot, 128:384], PS[:, b, 128:384], bias, -scale, BIG, ALU.add, ALU.min,
                NM[:, 2 * slot + 1:2 * slot + 2]), "v_s")
            s_free[b] = [vt_[slot]]
        for slot, *_ in heads:
            op("scalar", [vt_[slot]], lambda e, slot=slot: e.activation(
                PB[:, slot, 0:128], PB[:, slot, 0:128], ACT.Exp, scale=-1.0, bias=NM[:, 2 * slot:2 * slot + 1],
                accum_out=RS[:, 2 * slot:2 * slot + 1]), None)
            a_tok[slot] = op("scalar", [], lambda e, slot=slot: e.activation(
                PB[:, slot, 128:384], PB[:, slot, 128:384], ACT.Exp, scale=-1.0,
                bias=NM[:, 2 * slot + 1:2 * slot + 2], accum_out=RS[:, 2 * slot + 1:2 * slot + 2]), "a_exp")

    def inverse(slots):
        lo, hi = 2 * slots[0], 2 * slots[-1] + 2
        return op("vector", [a_tok[s] for s in slots], lambda e: e.reciprocal(RS[:, lo:hi], RS[:, lo:hi]), "v_rs")

    def scale_rows(slots):
        r = inverse(slots)
        for slot in slots:
            op("vector", [r], lambda e, slot=slot: e.tensor_scalar(
                PB[:, slot, 0:128], PB[:, slot, 0:128], RS[:, 2 * slot:2 * slot + 1], None, ALU.mult), None)
            a_tok[slot] = op("vector", [], lambda e, slot=slot: e.tensor_scalar(
                PB[:, slot, 128:384], PB[:, slot, 128:384], RS[:, 2 * slot + 1:2 * slot + 2], None, ALU.mult), "v_p")

    def turn(slot):
        b = 6 + slot % 2
        for j in range(3):
            t = op("tensor", [a_tok[slot], mk] + t_free.get(b, []), lambda e, j=j: e.transpose(
                PS[:, b, j * 128:j * 128 + 128], PB[:, slot, j * 128:j * 128 + 128], ID[:, :]),
                "t_t" if j == 2 else None)
        pb_free[slot] = [t]
        t = op("scalar", [t] + pt_free.get(slot, []), lambda e: e.activation(
            PT[:, slot, :], PS[:, b, 0:384], ACT.Copy), "a_t")
        t_free[b] = [t]
        b_tok[slot] = t

    def values(slot, v, dst, waits):
        op("tensor", [b_tok[slot]] + list(waits), lambda e: e.matmul(
            dst[:, 0:256], v(0), PT[:, slot, 0:256], start=True, stop=False), None)
        t = op("tensor", [], lambda e: e.matmul(
            dst[:, 128:256], v(1), PT[:, slot, 256:384], start=False, stop=True), "t_o")
        pt_free[slot] = [t]
        return t

    OB = 3
    otok = {}

    def pair_values(slots, v, tile, oh_free=()):
        for i, s in enumerate(slots):
            t = values(s, v[i][0], PS[64 * i:64 * i + 64, OB, 0:256], list(v[i][1]) + bank_free[OB])
        h, lo = split(Oh[:, tile, :], Ol[:, tile, :], PS[:, OB, 0:256], [t], oh_free)
        bank_free[OB] = [lo]
        otok[tile] = [h, lo]

    def head_pair(i, qs, ks, vs, tile, bias, scale, waits, oh_free=lambda: [], ready=lambda: True):
        slots = [2 * (i % 2), 2 * (i % 2) + 1]
        new_head(
            ready,
            lambda: scores([(s, q, k, waits(), bias(j), scale) for j, (s, q, k) in enumerate(zip(slots, qs, ks))]),
            lambda: scale_rows(slots),
            lambda: [turn(s) for s in slots],
            lambda: pair_values(slots, vs(), tile, oh_free()),
        )

    def fox_pair(i):
        h = 2 * i
        head_pair(
            i, [QF[0:80, h + j, :] for j in range(2)], [KF[0:80, h + j, :] for j in range(2)],
            lambda: [((lambda kb, j=j: VF[:, kb, (h + j) * 64:(h + j + 1) * 64]), [vf_tok[h // 4]]) for j in range(2)],
            4 + i, lambda j: TRI[:, :], SCALE64, lambda: [kf_tok[h // 4], qf_tok[h // 4]] + aug[0:2 + h // 4],
            oh_free=lambda: [mm_tok[chunk_no[("ukv", 0)]]], ready=lambda: chunk_no[("ukv", 0)] in mm_tok)

    def mla_pair(i):
        h = 2 * i
        head_pair(
            i, [QM[0:96, h + j, :] for j in range(2)], [KM[0:96, h + j, :] for j in range(2)],
            lambda: [((lambda kb, j=j: VM[:, kb, (h + j) * 64:(h + j + 1) * 64]), vm_tok) for j in range(2)],
            i, lambda j: TRI[:, :], MLA_SCALE, lambda: qm_tok + km_tok,
            oh_free=lambda: [mm_tok[chunk_no[("ukv", 0)]]], ready=lambda: chunk_no[("ukv", 0)] in mm_tok)

    def from_norms(tiles):
        xready.clear()
        xready.update(tiles)

    for j in range(2):
        from_norms(cn)
        chunk_T(("uq", j), (Oh, Ol), (ev_uq, ev_uq_rope)[j], kts=3, ncols=512, pairs=2, mid=False)
        from_norms(xr)
        fox_pair(j)
        chunk_N(("in", 7 + j), H, v_out(VF[:, :, 256 * j:256 * j + 256], vf_tok))
    from_norms(cn)

    def ukv():
        n = mm_begin(("ukv", 0))
        for pr in range(2):
            b = gbank()
            mm_T(n, 2, 1024, 2 * pr, PS[:, b, 0:T], list(bank_free[b]), Oh, Ol, lambda k: 3 + k)
            tok = mm_T(n, 2, 1024, 2 * pr + 1, PS[:, b, T:2 * T], [], Oh, Ol, lambda k: 3 + k, signal="t_mm")
            heads_out(KM, 4 * pr, km_tok)(b, tok)
        for half in range(2):
            b = gbank()
            tok = mm_N(n, 2, 1024, 512, 512, PS[:, b, :], half, list(bank_free[b]), Oh, Ol, lambda k: 3 + k, signal="t_mm")
            t = op("scalar", [tok, km_tok[0]], lambda e, b=b, half=half: e.activation(VM[:, half, :], PS[:, b, :], ACT.Copy), "a_ev")
            bank_free[b] = [t]
            vm_tok.append(t)
        mm_end(n, tok)
        after()
        refill(n)

    ukv()
    rot["banks"] = [0, 1, 2]
    from_norms(xr)
    for i in range(2, 4):
        fox_pair(i)
    for i in range(4):
        mla_pair(i)

    ga_tok = []

    def ev_gate(g):
        def ev(pr, b, tok):
            t = op("scalar", [tok], lambda e: e.activation(
                GA[:, 2 * g:2 * g + 2, :].rearrange("p j t -> p (j t)"), PS[:, b, :], ACT.Copy), "a_ev")
            bank_free[b] = [t]
            ga_tok.append(t)
        return ev

    for g in range(8):
        chunk_T(("in", 9 + g), H, ev_gate(g))
    h_used = mm_tok[chunk_no[("in", 16)]]
    while 7 not in otok:
        advance()
    for tile in range(4, 8):
        xready[tile] = otok[tile]

    yready = {}

    def step_o(i):
        n = mm_begin(("o", i))
        gm, gf = (GA[:, a + 2 * i:a + 2 * i + 2, :].rearrange("p j t -> p (j t)") for a in (0, 8))
        sg = op("scalar", ga_tok, lambda e: e.activation(gm, gm, ACT.Sigmoid), "a_sg")
        sg = op("scalar", [], lambda e: e.activation(gf, gf, ACT.Sigmoid), "a_sg")
        bs, toks = [], []
        for part in (1, 0):
            if i == 0 and part == 0:
                flush()
                place3_free.append(("t_s", P.counts["t_s"]))
                for tile in range(4):
                    xready[tile] = otok[tile]
                rot["banks"] = [0, 1, 2, 3]
            b = gbank()
            bs.append(b)
            slot = place(n)
            for nt in range(2):
                if i == 0 and part == 1:
                    advance()
                for k in range(4):
                    kk = 4 * part + k
                    at = kk * 256 + nt * 128
                    wh, wl = whi[slot][:, at:at + 128], wlo[slot][:, at:at + 128]
                    dst = PS[:, b, nt * T:nt * T + T]

                    def go(e, wh=wh, wl=wl, kk=kk, dst=dst, k=k):
                        e.matmul(dst, wh, Oh[:, kk, :], start=k == 0, stop=False)
                        e.matmul(dst, wh, Ol[:, kk, :], start=False, stop=False)
                        return e.matmul(dst, wl, Oh[:, kk, :], start=False, stop=k == 3)

                    tok = op("tensor", bank_free[b] + weight_wait(n, at + 128) + xwait(kk), go,
                             "t_mm" if nt == 1 and k == 3 else None)
            toks.append(tok)
        mm_end(n, tok)
        t = op("vector", [toks[0], sg], lambda e: e.tensor_tensor(gf, PS[:, bs[0], :], gf, ALU.mult), "v_y")
        bank_free[bs[0]] = [t]
        t = op("vector", [toks[1]], lambda e: e.tensor_tensor(gm, PS[:, bs[1], :], gm, ALU.mult), "v_y")
        bank_free[bs[1]] = [t]
        t = op("vector", [t], lambda e: e.tensor_tensor(gm, gm, gf, ALU.add), "v_y")
        fl = lambda x: x[:, 2 * i:2 * i + 2, :].rearrange("p j t -> p (j t)")
        h, lo = split(fl(Hh), fl(Hl), gm, [t], [h_used])
        yready[2 * i] = yready[2 * i + 1] = [h, lo]
        refill(n)
        return t

    for i in range(4):
        ga_done = step_o(i)
    o_used = mm_tok[chunk_no[("o", 3)]]
    lam_tok, sw_tok = lam()
    xready.clear()
    xready.update(yready)

    def ev_res(i, gate, gtok):
        def ev(pr, b, tok):
            for j in range(2):
                k = 2 * i + j
                t = op("vector", [tok, x_tok[k]] + gtok, lambda e, k=k, j=j: e.scalar_tensor_tensor(
                    X[:, k, :], PS[:, b, j * T:j * T + T], gate(k), X[:, k, :], ALU.mult, ALU.add), "v_x")
                x_tok[k] = t
            bank_free[b] = [t]
        return ev

    def ev_add(i):
        def ev(pr, b, tok):
            fl = X[:, 2 * i:2 * i + 2, :].rearrange("p j t -> p (j t)")
            t = op("vector", [tok, x_tok[2 * i], x_tok[2 * i + 1]], lambda e: e.tensor_tensor(
                fl, PS[:, b, :], fl, ALU.add), "v_x")
            x_tok[2 * i] = x_tok[2 * i + 1] = t
            bank_free[b] = [t]
        return ev

    def ev_out(i):
        def ev(pr, b, tok):
            ev_res(i, lambda k: ADA[:, 16 + k:17 + k], [ada_acc[2]])(pr, b, tok)
            square_pair(i)
        return ev

    together([("out", i) for i in range(2)], H, [ev_out(i) for i in range(2)])
    chunk_T(("out", 2), H, ev_out(2), fill=False)
    n = mm_begin(("out", 3))
    gs_ffn = op("vector", [ada_acc[4], small], lambda e: e.scalar_tensor_tensor(
        GS[:, 8:16], ADA[:, 32:40], 1.0, col("norm_ffn_g", 0, 8), ALU.add, ALU.mult), "v_gs")

    def ffn_norm(pr, b, tok):
        ev_out(3)(pr, b, tok)
        x_free[:] = [mm_tok[n]]
        xready.clear()
        sbank = gbank()
        t = total_squares(sbank, 0)
        r = inverse_rms(sbank, t, D, ST[:, 0:2], 0)(False)
        apply(lambda k: X[:, k, :], range(8), lambda k: GS[:, 8 + k:9 + k], lambda k: ADA[:, 24 + k:25 + k], 0, r, H,
              waits=lambda k: [gs_ffn, ada_acc[3]], by=PS[:, sbank, 256:512])
        bank_free[sbank] = list(rb_free[0])
        x_free[:] = []

    chunk_T(("out", 3), H, ffn_norm)

    wk_free = {}
    hid = {}
    hid_free = {s: [o_used] for s in range(8)}
    UC = lambda s: PBf[:, s * 512:(s + 1) * 512]

    def up_one(j):
        s = j % 3
        st1 = {}

        def ev(pr, b, tok):
            for i, tile in enumerate((j, 22 + j)):
                t = op("scalar", [tok] + wk_free.get(s, []), lambda e, i=i, tile=tile: e.activation(
                    UC(s)[:, i * T:i * T + T], PS[:, b, i * T:i * T + T], ACT.Identity,
                    bias=col("conv_b", tile), scale=col("conv_w", 88 + tile)), "a_u")
            for tap, sh in ((1, 1), (0, 2)):
                for i, tile in enumerate((j, 22 + j)):
                    u = UC(s)[:, i * T + sh:i * T + T]
                    t = op("vector", [t] if i == 0 else [], lambda e, i=i, u=u, tile=tile, tap=tap, sh=sh: e.scalar_tensor_tensor(
                        u, PS[:, b, i * T:i * T + T - sh], col("conv_w", tap * 44 + tile), u, ALU.mult, ALU.add), "v_u")
            bank_free[b] = [t]
            st1["t"] = t

        def late():
            g, m = PTf[:, (j % 2) * 512:(j % 2) * 512 + 256], PTf[:, (j % 2) * 512 + 256:(j % 2) * 512 + 512]
            t = op("scalar", [st1["t"]] + wk_free.get(("m", j % 2), []), lambda e: e.activation(g, UC(s)[:, 0:T], ACT.Silu), "a_u2")
            t = op("vector", [t], lambda e: e.tensor_tensor(m, g, UC(s)[:, T:2 * T], ALU.mult), "v_u2")
            wk_free[s] = [t]
            h, lo = split(Oh[:, j % 8, :], Ol[:, j % 8, :], m, [t], hid_free.get(j % 8, []))
            wk_free[("m", j % 2)] = [lo]
            hid[j] = [h, lo]

        return ev, late

    def down(key, i, n_pairs, last_one=False):
        n = mm_begin(key)
        slot = place(n)
        done = {}
        for nt in range(8):
            b = 4 + nt // 2
            dst = PS[:, b, (nt % 2) * T:(nt % 2) * T + T]
            for k in range(2):
                tile = (2 * i + k) % 8
                wh, wl = (w[slot][:, k * 1024 + nt * 128:k * 1024 + nt * 128 + 128] for w in (whi, wlo))
                start = i == 0 and k == 0 and nt % 2 == 0
                stop = i == n_pairs - 1 and k == 1

                def go(e, dst=dst, wh=wh, wl=wl, tile=tile, start=start, stop=stop):
                    e.matmul(dst, wh, Oh[:, tile, :], start=start, stop=False, skip_group_check=True)
                    e.matmul(dst, wh, Ol[:, tile, :], start=False, stop=False, skip_group_check=True)
                    return e.matmul(dst, wl, Oh[:, tile, :], start=False, stop=stop, skip_group_check=True)

                last = nt == 7 and k == 1
                sig = "t_mm" if last or (i == n_pairs - 1 and nt % 2 == 1 and k == 1) else None
                fr = bank_free[b] + s_free.get(b, []) + t_free.get(b, []) if i == 0 else []
                tok = op("tensor", weight_wait(n, k * 1024 + nt * 128 + 128) + hid[2 * i + k] + fr, go, sig)
            if nt % 2 == 1:
                done[nt // 2] = tok
        mm_end(n, tok)
        for k in range(2):
            hid_free[(2 * i + k) % 8] = [tok]
        if last_one:
            return n, done
        refill(n)

    late = []

    def then(ev, last=None):
        def go(pr, b, tok):
            ev(pr, b, tok)
            while late:
                late.pop(0)()
            if last:
                last()
        return go

    for i in range(11):
        (e0, l0), (e1, l1) = up_one(2 * i), up_one(2 * i + 1)
        if i == 0:
            late.append(l0)
            together([("up", 0), ("up", 1)], H, [e0, then(e1)])
            late.append(l1)
        else:
            chunk_T(("up", 2 * i), H, then(e0))
            late.append(l0)
            chunk_T(("up", 2 * i + 1), H, then(e1, l1 if i == 10 else None))
            if i < 10:
                late.append(l1)
            down(("down", i - 1), i - 1, 11)
    xready.clear()
    x_free[:] = [mm_tok[chunk_no[("up", 21)]]]
    n, done = down(("down", 10), 10, 11, True)

    sq2 = PTf[:, 1024:1536]
    sum2 = PBf[:, 512:1024]
    s2 = {"acc": wk_free[1]}
    for i in range(4):
        ev_res(i, lambda k: ADA[:, 40 + k:41 + k], [ada_acc[5]])(0, 4 + i, done[i])
        gain_pair(i, lambda k: GC[:, k:k + 1])
        square_pair(i)
        for j in range(2):
            d = sum2 if i == 0 else sq2
            t = op("scalar", [x_tok[2 * i + j]] + s2["acc"], lambda e, i=i, j=j, d=d: e.activation(
                d[:, j * T:j * T + T], X[:, 2 * i + j, :], ACT.Square, scale=col("norm_final_g", 2 * i + j)), "a_sq")
        if i:
            t = op("vector", [t], lambda e: e.tensor_tensor(sum2, sum2, sq2, ALU.add), "v_sq")
            s2["acc"] = [t]
        else:
            s2["acc"] = [t]

    def both_norms():
        b = OB
        total_squares(b, 0)
        t = total(b, 2, [(sum2[:, 0:T], s2["acc"]), (sum2[:, T:2 * T], [])])
        r1, r2 = ST[:, 4:6], ST[:, 0:2]
        u = root(b, 0, 2, t, D, r1)
        t = op("vector", [u], lambda e: e.scalar_tensor_tensor(r2, PS[:, b, 2:4], 1.0 / D, r1, ALU.mult, ALU.mult), "v_r")
        t = op("vector", [t], lambda e: e.tensor_tensor(r2, r2, r1, ALU.mult), "v_r")
        t = op("scalar", [t, small], lambda e: e.activation(r2, r2, ACT.Sqrt, bias=col("eps")), "a_sqrt")
        t = op("vector", [t], lambda e: e.reciprocal(r2, r2), "v_rec")
        t = op("vector", [t], lambda e: e.tensor_tensor(r2, r2, r1, ALU.mult), "v_r")

        def finish():
            spread(b, 256, r1, 2, t)
            u = spread(b, 0, r2, 2, t)
            nrm["r"] = op("scalar", [u] + rb_free[0] + rb_free[1], lambda e: e.activation(
                RB[:, :, :], PS[:, b, :].rearrange("p (j t) -> p j t", j=2), ACT.Copy), "a_rb")
            bank_free[b] = [nrm["r"]]
        nrm["finish"] = finish

    def residual(k):
        t = op("vector", [nrm["r"]], lambda e: e.scalar_tensor_tensor(
            X[:, k, :], X[:, k, :], col("norm_final_g", k), RB[:, 1, :], ALU.mult, ALU.mult), "v_x")
        x_tok[k] = t

    ga_free = [ga_done]
    gained = {}

    def one_norm():
        b = OB
        t = total_squares(b, 0)
        done = inverse_rms(b, t, D, ST[:, 0:2], 0)

        def finish():
            nrm["r"] = done()
        nrm["finish"] = finish

    def ev_qk(dst, toks, j):
        def ev(pr, b, tok):
            t = op("vector", [tok, nrm["r"]], lambda e: e.tensor_tensor(
                dst[:, 2 * j:2 * j + 2, :], PS[:, b, :].rearrange("p (j t) -> p j t", j=2),
                RB[:, 0, :].unsqueeze(1).to_broadcast([128, 2, T]), ALU.mult), "v_qk")
            bank_free[b] = rb_free[0] = [t]
            toks.append(t)
        return ev

    def ev_v(j, toks):
        def ev(b, tok):
            for half in range(2):
                t = op("scalar", [tok, nrm["r"]], lambda e, half=half: e.activation(
                    V[:, half, 256 * j:256 * j + 256], PS[:, b, half * 256:half * 256 + 256], ACT.Copy,
                    scale=ST[:, half:half + 1]), "a_ev")
            bank_free[b] = [t]
            toks.append(t)
        return ev

    for layer in range(2):
        al = alibi8 if layer == 0 else alibi16
        nh = 8 * (layer + 1)
        al_tok = op("sync", ga_free, lambda e, al=al, nh=nh: e.dma_start(GA[:, 0:nh, :], al), "d_al", 16)
        x_free[:] = []
        xready.clear()
        xready.update(nready)
        rot["banks"] = [0, 1, 2]
        qt, kt_, vt = [], [], []
        otok.clear()
        heads.update(all=[], scored=0, scaled=0, turned=0, valued=0)
        o_free = [hid_free[s][0] for s in range(8)]

        def diff_head(h):
            s0, s1 = slots = [2 * (h % 2), 2 * (h % 2) + 1]

            def scale():
                r = inverse(slots)
                for c0, c1, j in ((0, 128, 0), (128, 384, 1)):
                    t = op("vector", [r, lam_tok], lambda e, c0=c0, c1=c1, j=j: e.tensor_scalar(
                        PB[:, s1, c0:c1], PB[:, s1, c0:c1], RS[:, 2 * s1 + j:2 * s1 + j + 1], LM[:, 4:5],
                        ALU.mult, ALU.mult), "v_p")
                for c0, c1, j in ((0, 128, 0), (128, 384, 1)):
                    t = op("vector", [t], lambda e, c0=c0, c1=c1, j=j: e.scalar_tensor_tensor(
                        PB[:, s0, c0:c1], PB[:, s0, c0:c1], RS[:, 2 * s0 + j:2 * s0 + j + 1], PB[:, s1, c0:c1],
                        ALU.mult, ALU.subtract), "v_a")
                a_tok[s0] = t
                pb_free[s1] = [t]

            def values_out():
                t = values(s0, lambda kb: V[:, kb, h * 128:h * 128 + 128], PS[:, OB, 0:256],
                           [vt[h // 2]] + bank_free[OB])
                t = op("scalar", [t], lambda e: e.activation(GA[:, 8 + h, :], PS[:, OB, 0:256], ACT.Copy), "a_ev")
                bank_free[OB] = [t]
                od_tok[h] = t
                if h % 2 == 1:
                    post.extend(subln(h // 2))

            new_head(
                lambda: len(vt) > h // 2,
                lambda: scores([(s, QM[64 * m:64 * m + 64, h, :], KM[64 * m:64 * m + 64, h, :],
                                 [qt[h // 2], kt_[h // 2], al_tok], GA[:, h, :], SCALE64)
                                for m, s in enumerate(slots)]),
                scale,
                lambda: turn(s0),
                values_out,
            )

        od_tok = {}

        def subln(g):
            b = 7
            tk = {}
            fl = lambda x, a: x[:, a:a + 2, :].rearrange("p j t -> p (j t)")

            def squares():
                tk["sq"] = op("scalar", [od_tok[2 * g], od_tok[2 * g + 1]] + sq_free[0] + sq_free[1], lambda e: e.activation(
                    fl(SQ, 0), fl(GA, 8 + 2 * g), ACT.Square), "a_sq")

            def sums():
                for h in range(4):
                    t = op("tensor", [tk["sq"]] + t_free.get(b, []) + bank_free[b], lambda e, h=h: e.matmul(
                        PS[:, b, h:h + 1], fl(SQ, 0)[:, h * 128:h * 128 + 128], ONES[:, 0:1], start=True, stop=True),
                        "t_sq")
                sq_free[0] = sq_free[1] = [t]
                tk["r"] = root(b, 0, 4, t, 128, ST[:, 6:10])

            def rows():
                tk["m"] = spread(b, 0, ST[:, 6:10], 4, tk["r"])

            def finish():
                t = op("vector", [tk["m"], sw_tok] + tt_free.get(0, []) + tt_free.get(1, []), lambda e: e.scalar_tensor_tensor(
                    fl(TT, 0), fl(GA, 8 + 2 * g), SW[:, 0:1], PS[:, b, :], ALU.mult, ALU.mult), "v_nrm")
                bank_free[b] = [t]
                hh, lo = split(fl(Oh, 2 * g), fl(Ol, 2 * g), fl(TT, 0), [t], o_free)
                tt_free[0] = tt_free[1] = [lo]
                otok[2 * g] = otok[2 * g + 1] = [hh, lo]

            return [squares, sums, rows, finish]

        def moba_pair(i):
            h = 2 * i
            head_pair(
                i, [QM[64 * j:64 * j + 64, i, :] for j in range(2)], [KM[64 * j:64 * j + 64, i, :] for j in range(2)],
                lambda: [((lambda kb, j=j: V[:, kb, (h + j) * 64:(h + j + 1) * 64]), [vt[h // 4]]) for j in range(2)],
                i, lambda j: GA[:, h + j, :], SCALE64, lambda: [qt[i // 2], kt_[i // 2], al_tok],
                oh_free=lambda: o_free, ready=lambda: len(vt) > i // 2)

        def on_the_way(k):
            if k == 6:
                both_norms() if layer == 0 else one_norm()
                refill(chunk_no[(f"qkv{layer}", 0)] - 1)
            elif k == 8:
                nrm["finish"]()

        together([(f"qkv{layer}", 0), (f"qkv{layer}", 4)], H, [ev_qk(QM, qt, 0), ev_qk(KM, kt_, 0)], on_the_way)
        one_head = diff_head if layer == 0 else moba_pair
        for i, c in enumerate(QKV_ORDER[2:]):
            if i == 1:
                one_head(0)
                one_head(1)
            if layer == 0 and i in (6, 7, 8, 9):
                residual(2 * i - 12)
                residual(2 * i - 11)
            if c < 4:
                chunk_T((f"qkv{layer}", c), H, ev_qk(QM, qt, c))
            elif c < 8:
                chunk_T((f"qkv{layer}", c), H, ev_qk(KM, kt_, c - 4))
                one_head(2 * (c - 4))
                one_head(2 * (c - 4) + 1)
            else:
                chunk_N((f"qkv{layer}", c), H, ev_v(c - 8, vt))
        xready.clear()
        while 0 not in otok:
            advance()
        xready[0] = otok[0]
        h_used = mm_tok[chunk_no[(f"qkv{layer}", 11)]]
        x_free[:] = [h_used]

        def ev_norm(i):
            def ev(pr, b, tok):
                ev_add(i)(pr, b, tok)
                gain_pair(i, lambda k: col("mlp_norm", layer * 8 + k))
                square_pair(i)
            return ev

        together([(f"out{layer}", i) for i in range(3)], (Oh, Ol), [ev_norm(i) for i in range(3)], arriving(otok))
        flush()
        ga_free = [("v_s", P.counts["v_s"]), ("v_nrm", P.counts["v_nrm"])]
        rot.update(banks=[0, 1, 2, 3], at=3)
        chunk_T((f"out{layer}", 3), (Oh, Ol), ev_norm(3), fill=False)
        o_used = mm_tok[chunk_no[(f"out{layer}", 3)]]
        x_free[:] = []
        xready.clear()
        xready.update(nready)
        for s in range(8):
            hid_free[s] = [o_used]
        hid.clear()
        wk_free.clear()

        def mlp_one(i):
            s = i % 2
            st1 = {}
            r, m = PBf[:, s * 512:s * 512 + 512], PTf[:, s * 512:s * 512 + 512]

            def ev(pr, b, tok):
                t = op("vector", [tok, nrm["r"]] + wk_free.get(("r", s), []), lambda e: e.scalar_tensor_tensor(
                    r.rearrange("p (j t) -> p j t", j=2), PS[:, b, :].rearrange("p (j t) -> p j t", j=2), 0.0,
                    RB[:, 0, :].unsqueeze(1).to_broadcast([128, 2, T]), ALU.max, ALU.mult), "v_u")
                bank_free[b] = rb_free[0] = [t]
                st1["t"] = t

            def late():
                a = (2 * i) % 8
                fl = lambda x: x[:, a:a + 2, :].rearrange("p j t -> p (j t)")
                t = op("scalar", [st1["t"]] + wk_free.get(("m", s), []), lambda e: e.activation(m, r, ACT.Square), "a_u")
                wk_free[("r", s)] = [t]
                h, lo = split(fl(Oh), fl(Ol), m, [t], hid_free[a])
                wk_free[("m", s)] = [lo]
                hid[2 * i] = hid[2 * i + 1] = [h, lo]

            return ev, late

        def on_the_way(k):
            if k == 5:
                b = gbank()
                t = total_squares(b, 0)
                done = inverse_rms(b, t, D, ST[:, 2:4], 0)

                def finish():
                    nrm["r"] = done()
                nrm["finish"] = finish
                refill(chunk_no[(f"out{layer}", 3)])
            elif k == 8:
                nrm["finish"]()

        (e0, l0), (e1, l1) = mlp_one(0), mlp_one(1)
        late.append(l0)
        together([(f"ff1{layer}", 0), (f"ff1{layer}", 1)], H, [e0, then(e1)], on_the_way)
        late.append(l1)
        for i in range(2, 16):
            ev, lt = mlp_one(i)
            chunk_T((f"ff1{layer}", i), H, then(ev, lt if i == 15 else None))
            if i < 15:
                late.append(lt)
            if i >= 2:
                down((f"ff2{layer}", i - 2), i - 2, 16)
        down((f"ff2{layer}", 14), 14, 16)
        x_free[:] = [mm_tok[chunk_no[(f"ff1{layer}", 15)]]]
        n, done = down((f"ff2{layer}", 15), 15, 16, True)
        def gains(i):
            if layer == 0:
                gain_pair(i, lambda k: col("attn_norm", 8 + k))
                return
            for k in (2 * i, 2 * i + 1):
                gained[k] = op("scalar", [x_tok[k]], lambda e, k=k: e.activation(
                    QM[:, k, :], X[:, k, :], ACT.Copy, scale=col("final_norm", k)), "a_x")

        for i in range(4):
            ev_add(i)(0, 4 + i, done[i])
            if i == 3:
                square_pair(2)
            if layer == 0:
                gains(i)
            if i != 2:
                square_pair(i)
            if layer == 1 and i != 2:
                for g in range(max(i - 1, 0) if i == 3 else i, i + 1):
                    gains(g)

    b = gbank()
    t = total_squares(b, 0)
    r = inverse_rms(b, t, D, ST[:, 0:2], 0)(False)
    for k in range(0, 8, 2):
        t = op("vector", [r, gained[k + 1]], lambda e, k=k: e.tensor_tensor(
            X[:, k:k + 2, :], QM[:, k:k + 2, :], PS[:, b, 256:512].unsqueeze(1).to_broadcast([128, 2, T]), ALU.mult), "v_x")
        op("sync" if k % 4 == 0 else "scalar", [t], lambda e, k=k: e.dma_start(
            out[:, k:k + 2, :], X[:, k:k + 2, :]), "d_out", 16)

    with nc.Block() as block:
        @block.sync
        def _(e):
            P.run("sync", e)
            e.wait_ge(P.sems["d_out"], P.counts["d_out"])

        @block.scalar
        def _(e):
            P.run("scalar", e)

        @block.vector
        def _(e):
            P.run("vector", e)

        @block.gpsimd
        def _(e):
            P.run("gpsimd", e)

        @block.tensor
        def _(e):
            P.run("tensor", e)


def _tiles(w, cols):
    k = w.shape[0] // 128
    return w[:, cols].reshape(k, 128, len(cols)).transpose(1, 0, 2).reshape(128, k * len(cols))


def _chunks(a):
    r = np.arange
    cut = np.cumsum([0, 384, 256, 32, 512, 512, 512, 8, 1024, 1024])
    cq, ckv, kr, fq, fk, fv, ff, gm, gf = (r(cut[i], cut[i + 1]) for i in range(9))
    sw = np.concatenate([r(16, 32), r(16)])
    cols_in = np.concatenate([cq, np.tile(ff, 8), kr, kr[sw], ckv, fk, fq, fv, gm, gf])
    uq = np.concatenate([p + 96 * h for p in (r(64), 64 + r(32), 64 + sw) for h in range(8)])
    ukv = np.concatenate([np.concatenate([r(64) + 128 * h for h in range(8)]),
                          np.concatenate([64 + r(64) + 128 * h for h in range(8)])])
    up = np.concatenate([np.concatenate([r(128) + 128 * j, 2816 + r(128) + 128 * j]) for j in range(22)])
    out = []
    for kind, i in weight_order():
        c = r(256 * i, 256 * i + 256)
        if kind == "in":
            t = _tiles(a["w_in"][0], cols_in[c])
        elif kind == "uq":
            t = np.pad(_tiles(a["w_uq"][0], uq[512 * i:512 * i + 512]), ((0, 0), (0, 512)))
        elif kind == "ukv":
            t = _tiles(a["w_ukv"][0], ukv)
        elif kind == "o":
            t = np.concatenate([_tiles(a["w_o_mla"][0], c), _tiles(a["w_o_fox"][0], c)], axis=1)
        elif kind == "out":
            t = _tiles(a["w_out"][0], c)
        elif kind == "up":
            t = _tiles(a["w_up"][0], up[c])
        elif kind == "down":
            t = _tiles(a["w_down"][0][c], r(1024))
        else:
            layer = int(kind[-1])
            w = a[{"qkv": "w_in_2", "out": "w_out_2", "ff1": "w_ff1_2", "ff2": "w_ff2_2"}[kind[:-1]]][layer]
            t = _tiles(w[c], r(1024)) if kind[:-1] == "ff2" else _tiles(w, c)
        out.append(t)
    return np.stack(out)


def _slopes(n):
    return np.array([2.0 ** (-8.0 * (h + 1) / n) for h in range(n)], dtype=np.float32)


def _alibi(n):
    dist = (128 + np.arange(128)[:, None] - np.arange(256)[None, :]).astype(np.float32)
    t = -_slopes(n)[None, :, None] * dist[:, None, :] / np.float32(SCALE64)
    return np.where(dist[:, None, :] >= 0, t, np.float32(NEG)).astype(np.float32)


def _smalls(a):
    def tiles(v):
        return np.asarray(v).reshape(-1, 128).T

    p = np.arange(128)
    one = lambda f: np.array([f(i) for i in range(128)], np.float32)[:, None]
    inv = np.float32(10000.0) ** (-np.arange(0, 32, 2, dtype=np.float32) / np.float32(32))
    m1 = np.stack([one(lambda q: 8.0 if q == h else 0.0)[:, 0] for h in range(8)], 1)
    m2 = np.stack([one(lambda q: 1.0 if q - 8 == h else 0.0)[:, 0] for h in range(8)], 1)
    parts = [
        tiles(a["c"]), tiles(a["b_ada"]), tiles(a["norm_mix_g"]), tiles(a["norm_ffn_g"]), tiles(a["norm_final_g"]),
        tiles(a["q_norm_g"]), tiles(a["kv_norm_g"]), tiles(a["conv_w"]), tiles(a["conv_b"]),
        tiles(a["attn_norm_2"]), tiles(a["mlp_norm_2"]), tiles(a["final_norm_2"]), tiles(a["diff_subln_2"]),
        np.tile(a["b_forget"][0], 16)[:, None], inv[p % 16][:, None].astype(np.float32),
        one(lambda q: -1.0 if q % 32 < 16 else 1.0), one(lambda q: EPS), m1, m2,
        one(lambda q: -8.0 if q >= 8 else 0.0), one(lambda q: 1.0 if q < 8 else 0.0),
    ]
    return np.concatenate(parts, axis=1)


def _layout(a):
    w = a["w_ada"][0]
    first = w[:, 0:2048].reshape(2, 4, 128, 2, 4, 256).transpose(4, 0, 2, 1, 3, 5).reshape(8, 128, 2048)
    rest = w.reshape(4, 2, 128, 6, 1024).transpose(3, 0, 2, 1, 4).reshape(24, 128, 2048)[8:]
    ada = np.concatenate([first, rest])
    tri = np.where(np.arange(128)[None, :] <= np.arange(128)[:, None], np.float32(0), np.float32(NEG))
    masks = np.concatenate([np.eye(128, dtype=np.float32), np.zeros((128, 128), np.float32), tri], axis=1)
    return {
        "wall": _chunks(a),
        "wada": ada,
        "smalls": _smalls(a),
        "pos": np.tile(a["positions"], (128, 1)),
        "xt": a["x"][0].T.reshape(8, 128, 256).transpose(1, 0, 2),
        "masks": masks.astype(np.float32),
        "lam4": np.tile(a["diff_lambda_2"][0].reshape(1, 256), (128, 1)),
        "alibi8": _alibi(8),
        "alibi16": _alibi(16),
    }


def kernel(**inputs):
    import concourse.bacc as _bacc
    from concourse.bass_utils import run_bass_kernel_spmd as _run

    a = {k: np.asarray(v) for k, v in inputs.items()}
    arrays = {k: np.ascontiguousarray(v) for k, v in _layout(a).items()}
    nc = _bacc.Bacc("TRN2", target_bir_lowering=False, num_devices=1)
    aps = [nc.dram_tensor(k, v.shape, mybir.dt.from_np(v.dtype), kind="ExternalInput").ap() for k, v in arrays.items()]
    o = nc.dram_tensor("out", (128, 8, 256), F32, kind="ExternalOutput").ap()
    build(nc, *aps, o)
    r = _run(nc, [arrays], core_ids=[0])
    y = r.results[0]["out"]
    return np.ascontiguousarray(y.transpose(1, 0, 2).reshape(1024, 256).T).reshape(1, 256, 1024)
```
